# Optimizing a Trainium2 kernel written in Bass

```python
import jax, jax.numpy as jnp
from jax import lax
import numpy as np

D_MODEL = 1024
BATCH = 1
SEQ = 1024
DEPTH = 1
DEC_BATCH = 8
DEC_SEQ = 16
PAST_LEN = 512

CHUNK = 64
PLE_DIM = 256
EPS = 1e-6
N_BRANCH = 3
SC_WIDTH = D_MODEL
SC_KERNEL = 3
SSM_INNER = 2 * D_MODEL
SSM_HEAD_DIM = 64
SSM_HEADS = SSM_INNER // SSM_HEAD_DIM
SSM_GROUPS = 4
SSM_STATE = 128
SSM_CONV = 4
SSM_CONV_DIM = SSM_INNER + 2 * SSM_GROUPS * SSM_STATE
CF_WIDTH = D_MODEL
CF_KERNEL = 31
FF_DIM = 2816
FF_KERNEL = 3
OFF_SC = N_BRANCH * D_MODEL
OFF_Z = OFF_SC + 3 * SC_WIDTH
OFF_XBC = OFF_Z + SSM_INNER
OFF_DT = OFF_XBC + SSM_CONV_DIM
OFF_CF = OFF_DT + SSM_HEADS
N_IN = OFF_CF + 2 * CF_WIDTH

kernel_name = "hybrid_streaming_encoder_step"

def rmsnorm(x, g):
    xf = x.astype(jnp.float32)
    xf = xf * lax.rsqrt(jnp.mean(xf * xf, axis=-1, keepdims=True) + EPS)
    return xf.astype(x.dtype) * g

def layernorm(x, g, b):
    xf = x.astype(jnp.float32)
    mu = jnp.mean(xf, axis=-1, keepdims=True)
    xc = xf - mu
    var = jnp.mean(xc * xc, axis=-1, keepdims=True)
    return (xc * lax.rsqrt(var + EPS)).astype(x.dtype) * g + b

def causal_dwconv(x, prev, w, b=None):
    k = w.shape[0]
    xp = jnp.concatenate([prev.astype(x.dtype), x], axis=1)
    y = lax.conv_general_dilated(xp, w[:, None, :].astype(x.dtype), window_strides=(1,),
                                 padding='VALID', dimension_numbers=('NWC', 'WIO', 'NWC'),
                                 feature_group_count=x.shape[-1])
    if b is not None:
        y = y + b
    return y, xp[:, xp.shape[1] - (k - 1):]

def ssd_scan(x, dt, a, bmat, cmat, h0):
    bsz, t, nh, hp = x.shape
    tp = -(-t // CHUNK) * CHUNK
    pad = tp - t

    def pad_t(z):
        return jnp.pad(z, [(0, 0), (0, pad)] + [(0, 0)] * (z.ndim - 2))

    x, dt, bmat, cmat = pad_t(x), pad_t(dt), pad_t(bmat), pad_t(cmat)
    nc = tp // CHUNK
    r = nh // SSM_GROUPS
    f32 = jnp.float32
    xc = x.reshape(bsz, nc, CHUNK, SSM_GROUPS, r, hp).astype(f32)
    dtc = dt.reshape(bsz, nc, CHUNK, SSM_GROUPS, r).astype(f32)
    bc = bmat.reshape(bsz, nc, CHUNK, SSM_GROUPS, SSM_STATE).astype(f32)
    cc = cmat.reshape(bsz, nc, CHUNK, SSM_GROUPS, SSM_STATE).astype(f32)
    acs = jnp.cumsum(dtc * a.reshape(SSM_GROUPS, r), axis=2)
    diff = acs[:, :, :, None] - acs[:, :, None, :]
    causal = jnp.tril(jnp.ones((CHUNK, CHUNK), dtype=bool))[None, None, :, :, None, None]
    lmat = jnp.exp(jnp.where(causal, diff, -jnp.inf))
    xdt = xc * dtc[..., None]
    cb = jnp.einsum('bclgn,bcsgn->bclsg', cc, bc)
    y_diag = jnp.einsum('bclsgr,bcsgrp->bclgrp', cb[..., None] * lmat, xdt)
    a_last = acs[:, :, -1]
    decay_to_end = jnp.exp(a_last[:, :, None] - acs)
    chunk_states = jnp.einsum('bcsgn,bcsgr,bcsgrp->bcgrpn', bc, decay_to_end, xdt)

    def step(h_prev, inp):
        s_c, al = inp
        h_new = jnp.exp(al)[..., None, None] * h_prev + s_c
        return h_new, h_prev

    h0g = h0.reshape(bsz, SSM_GROUPS, r, hp, SSM_STATE).astype(f32)
    h_final, h_in = lax.scan(step, h0g, (jnp.moveaxis(chunk_states, 1, 0), jnp.moveaxis(a_last, 1, 0)))
    h_in = jnp.moveaxis(h_in, 0, 1)
    y_off = jnp.einsum('bclgn,bcgrpn,bclgr->bclgrp', cc, h_in, jnp.exp(acs))
    y = (y_diag + y_off).reshape(bsz, tp, nh, hp)[:, :t]
    return y, h_final.reshape(bsz, nh, hp, SSM_STATE)

def hybrid_layer(h, p_i, st_sc, st_mconv, st_ssm, st_cf, st_ff, L):
    bsz, t, _ = h.shape
    w_in = L['w_in']
    n = rmsnorm(h, L['g_mix'])

    def proj(lo, hi):
        return n @ w_in[:, lo:hi]

    g_a, g_b, g_c = jnp.split(jax.nn.sigmoid(proj(0, OFF_SC)), N_BRANCH, axis=-1)

    s_b, s_c, s_h = jnp.split(proj(OFF_SC, OFF_Z), 3, axis=-1)
    u, new_sc = causal_dwconv(s_c * s_h, st_sc, L['sc_conv_w'])
    y_a = (s_b * u) @ L['w_sc_out']

    z = proj(OFF_Z, OFF_XBC)
    xbc, new_mconv = causal_dwconv(proj(OFF_XBC, OFF_DT), st_mconv, L['ssm_conv_w'], L['ssm_conv_b'])
    xbc = jax.nn.silu(xbc)
    gn = SSM_GROUPS * SSM_STATE
    xs = xbc[..., :SSM_INNER].reshape(bsz, t, SSM_HEADS, SSM_HEAD_DIM)
    bm = xbc[..., SSM_INNER:SSM_INNER + gn].reshape(bsz, t, SSM_GROUPS, SSM_STATE)
    cm = xbc[..., SSM_INNER + gn:].reshape(bsz, t, SSM_GROUPS, SSM_STATE)
    dt = jax.nn.softplus(proj(OFF_DT, OFF_CF).astype(jnp.float32) + L['ssm_dt_bias'].astype(jnp.float32))
    a = -jnp.exp(L['ssm_a_log'].astype(jnp.float32))
    ys, new_ssm = ssd_scan(xs, dt, a, bm, cm, st_ssm)
    ys = ys + L['ssm_d'].astype(jnp.float32)[:, None] * xs.astype(jnp.float32)
    ys = ys.reshape(bsz, t, SSM_INNER) * jax.nn.silu(z.astype(jnp.float32))
    yg = ys.reshape(bsz, t, SSM_GROUPS, SSM_INNER // SSM_GROUPS)
    yg = yg * lax.rsqrt(jnp.mean(yg * yg, axis=-1, keepdims=True) + EPS)
    ys = yg.reshape(bsz, t, SSM_INNER).astype(h.dtype) * L['ssm_norm_g']
    y_b = ys @ L['w_ssm_out']

    c_a, c_g = jnp.split(proj(OFF_CF, N_IN), 2, axis=-1)
    v, new_cf = causal_dwconv(c_a * jax.nn.sigmoid(c_g), st_cf, L['cf_conv_w'], L['cf_conv_b'])
    y_c = jax.nn.silu(layernorm(v, L['cf_ln_g'], L['cf_ln_b'])) @ L['w_cf_out']

    h = h + (g_a * y_a + g_b * y_b + g_c * y_c) @ L['w_o']

    up, new_ff = causal_dwconv(rmsnorm(h, L['g_ffn']) @ L['w_up'], st_ff, L['ff_conv_w'], L['ff_conv_b'])
    u_a, u_b = jnp.split(up, 2, axis=-1)
    h = h + (jax.nn.silu(u_a) * u_b) @ L['w_down']

    h = h + (p_i @ L['w_ple_proj']) * jax.nn.sigmoid(rmsnorm(h, L['g_ple']) @ L['w_ple_gate'])
    return h, (new_sc, new_mconv, new_ssm, new_cf, new_ff)

def run_trunk(x, p, st_sc, st_mconv, st_ssm, st_cf, st_ff, W, g_final):
    h = x
    outs = [[], [], [], [], []]
    for i in range(DEPTH):
        L = {k: v[i] for k, v in W.items()}
        h, new = hybrid_layer(h, p[i], st_sc[i], st_mconv[i], st_ssm[i], st_cf[i], st_ff[i], L)
        for lst, s in zip(outs, new):
            lst.append(s)
    y = rmsnorm(h, g_final)
    return y, [jnp.stack(lst) for lst in outs]

def setup_inputs(seed: int = 0) -> dict:
    key = jax.random.key(seed)
    ks = iter(jax.random.split(key, 48))
    f32 = jnp.float32

    def nrm(shape, scale):
        return jax.random.normal(next(ks), shape, f32) * scale

    def gain(shape):
        return 1.0 + nrm(shape, 0.05)

    dt0 = jnp.exp(jax.random.uniform(next(ks), (DEPTH, SSM_HEADS), f32, np.log(1e-3), np.log(1e-1)))
    dt_bias = dt0 + jnp.log(-jnp.expm1(-dt0))
    a_log = jnp.log(jax.random.uniform(next(ks), (DEPTH, SSM_HEADS), f32, 1.0, 16.0))
    return {
        'x_prompt': nrm((BATCH, SEQ, D_MODEL), 1.0),
        'x_sample': nrm((DEC_BATCH, DEC_SEQ, D_MODEL), 1.0),
        'p_prompt': nrm((DEPTH, BATCH, SEQ, PLE_DIM), 1.0),
        'p_sample': nrm((DEPTH, DEC_BATCH, DEC_SEQ, PLE_DIM), 1.0),
        'state_short_conv': nrm((DEPTH, DEC_BATCH, SC_KERNEL - 1, SC_WIDTH), 0.5),
        'state_ssm_conv': nrm((DEPTH, DEC_BATCH, SSM_CONV - 1, SSM_CONV_DIM), 1.0),
        'state_ssm': nrm((DEPTH, DEC_BATCH, SSM_HEADS, SSM_HEAD_DIM, SSM_STATE), 0.1),
        'state_cf_conv': nrm((DEPTH, DEC_BATCH, CF_KERNEL - 1, CF_WIDTH), 0.5),
        'state_ffn_conv': nrm((DEPTH, DEC_BATCH, FF_KERNEL - 1, 2 * FF_DIM), 1.0),
        'g_mix': gain((DEPTH, D_MODEL)),
        'w_in': nrm((DEPTH, D_MODEL, N_IN), D_MODEL ** -0.5),
        'sc_conv_w': nrm((DEPTH, SC_KERNEL, SC_WIDTH), SC_KERNEL ** -0.5),
        'w_sc_out': nrm((DEPTH, SC_WIDTH, D_MODEL), SC_WIDTH ** -0.5),
        'ssm_conv_w': nrm((DEPTH, SSM_CONV, SSM_CONV_DIM), SSM_CONV ** -0.5),
        'ssm_conv_b': nrm((DEPTH, SSM_CONV_DIM), 0.02),
        'ssm_dt_bias': dt_bias,
        'ssm_a_log': a_log,
        'ssm_d': gain((DEPTH, SSM_HEADS)),
        'ssm_norm_g': gain((DEPTH, SSM_INNER)),
        'w_ssm_out': nrm((DEPTH, SSM_INNER, D_MODEL), SSM_INNER ** -0.5),
        'cf_conv_w': nrm((DEPTH, CF_KERNEL, CF_WIDTH), CF_KERNEL ** -0.5),
        'cf_conv_b': nrm((DEPTH, CF_WIDTH), 0.02),
        'cf_ln_g': gain((DEPTH, CF_WIDTH)),
        'cf_ln_b': nrm((DEPTH, CF_WIDTH), 0.02),
        'w_cf_out': nrm((DEPTH, CF_WIDTH, D_MODEL), CF_WIDTH ** -0.5),
        'w_o': nrm((DEPTH, D_MODEL, D_MODEL), D_MODEL ** -0.5),
        'g_ffn': gain((DEPTH, D_MODEL)),
        'w_up': nrm((DEPTH, D_MODEL, 2 * FF_DIM), D_MODEL ** -0.5),
        'ff_conv_w': nrm((DEPTH, FF_KERNEL, 2 * FF_DIM), FF_KERNEL ** -0.5),
        'ff_conv_b': nrm((DEPTH, 2 * FF_DIM), 0.02),
        'w_down': nrm((DEPTH, FF_DIM, D_MODEL), FF_DIM ** -0.5),
        'g_ple': gain((DEPTH, D_MODEL)),
        'w_ple_gate': nrm((DEPTH, D_MODEL, D_MODEL), D_MODEL ** -0.5),
        'w_ple_proj': nrm((DEPTH, PLE_DIM, D_MODEL), PLE_DIM ** -0.5),
        'g_final': gain((D_MODEL,)),
    }

def reference(x_prompt, x_sample, p_prompt, p_sample, state_short_conv, state_ssm_conv, state_ssm,
              state_cf_conv, state_ffn_conv, g_mix, w_in, sc_conv_w, w_sc_out, ssm_conv_w, ssm_conv_b,
              ssm_dt_bias, ssm_a_log, ssm_d, ssm_norm_g, w_ssm_out, cf_conv_w, cf_conv_b, cf_ln_g,
              cf_ln_b, w_cf_out, w_o, g_ffn, w_up, ff_conv_w, ff_conv_b, w_down, g_ple, w_ple_gate,
              w_ple_proj, g_final):
    W = {
        'g_mix': g_mix, 'w_in': w_in, 'sc_conv_w': sc_conv_w, 'w_sc_out': w_sc_out,
        'ssm_conv_w': ssm_conv_w, 'ssm_conv_b': ssm_conv_b, 'ssm_dt_bias': ssm_dt_bias,
        'ssm_a_log': ssm_a_log, 'ssm_d': ssm_d, 'ssm_norm_g': ssm_norm_g, 'w_ssm_out': w_ssm_out,
        'cf_conv_w': cf_conv_w, 'cf_conv_b': cf_conv_b, 'cf_ln_g': cf_ln_g, 'cf_ln_b': cf_ln_b,
        'w_cf_out': w_cf_out, 'w_o': w_o, 'g_ffn': g_ffn, 'w_up': w_up, 'ff_conv_w': ff_conv_w,
        'ff_conv_b': ff_conv_b, 'w_down': w_down, 'g_ple': g_ple, 'w_ple_gate': w_ple_gate,
        'w_ple_proj': w_ple_proj,
    }
    bp, dtp = x_prompt.shape[0], x_prompt.dtype
    z_sc = jnp.zeros((DEPTH, bp, SC_KERNEL - 1, SC_WIDTH), dtp)
    z_mconv = jnp.zeros((DEPTH, bp, SSM_CONV - 1, SSM_CONV_DIM), dtp)
    z_ssm = jnp.zeros((DEPTH, bp, SSM_HEADS, SSM_HEAD_DIM, SSM_STATE), jnp.float32)
    z_cf = jnp.zeros((DEPTH, bp, CF_KERNEL - 1, CF_WIDTH), dtp)
    z_ff = jnp.zeros((DEPTH, bp, FF_KERNEL - 1, 2 * FF_DIM), dtp)
    y_prompt, sp = run_trunk(x_prompt, p_prompt, z_sc, z_mconv, z_ssm, z_cf, z_ff, W, g_final)
    y_sample, ss = run_trunk(x_sample, p_sample, state_short_conv, state_ssm_conv, state_ssm,
                             state_cf_conv, state_ffn_conv, W, g_final)
    return (y_prompt, y_sample, sp[0], sp[1], sp[2], sp[3], sp[4], ss[0], ss[1], ss[2], ss[3], ss[4])


_drawn_inputs = setup_inputs


def setup_inputs(seed=0):
    import zlib

    import numpy as np

    out = dict(_drawn_inputs(seed))
    spreads = {}
    factors = {'ssm_d': 32.662,
     'cf_conv_b': 5.379,
     'cf_ln_g': 3.685,
     'cf_ln_b': 8.0,
     'ff_conv_b': 4.917,
     'g_ple': 26.758,
     'ssm_norm_g': 3.669}
    for name, (base, spread) in spreads.items():
        noise = np.random.default_rng([zlib.crc32(name.encode()), seed]).standard_normal(out[name].shape)
        drawn = base * np.exp(spread * noise) if base else spread * noise
        out[name] = __import__('jax').numpy.asarray(drawn.astype(out[name].dtype))
    for name, factor in factors.items():
        out[name] = (out[name] * factor).astype(out[name].dtype)
    return out
```

```python
from contextlib import ExitStack, contextmanager

import concourse.bass as bass
from concourse import mybir

F32 = mybir.dt.float32
F32R = mybir.dt.float32r
ALU = mybir.AluOpType
ACT = mybir.ActivationFunctionType
ds = bass.ds

P = 128
D = 1024
TP = 1024
NS, TS = 8, 16
T = TP + NS * TS
NB, BW = 3, T // 3
KD = D // P
HEADS, HD, GROUPS, NST = 32, 64, 4, 128
HG = HEADS // GROUPS
INNER = HEADS * HD
XBC = INNER + 2 * GROUPS * NST
FF = 2816
FK = FF // P
PLE = 256
EPS = 1e-6
OFF_SC = 3 * D
OFF_Z = OFF_SC + 3 * D
OFF_XBC = OFF_Z + INNER
OFF_DT = OFF_XBC + XBC
OFF_CF = OFF_DT + HEADS
PAD = 3
SEG = PAD + TS
PADW = PAD + TP + NS * SEG + 2
CK = 31
CPAD = CK - 1
CSEG = CPAD + TS
CFW = CPAD + TP + NS * CSEG
FF_PARTS = (8, 8, 6)

TB_STATE, TB_TAPS, TB_LNG, TB_LNB, TB_GFFN, TB_GPLE, TB_NORM, TB_PROMPT = 0, 16, 19, 20, 21, 22, 23, 25
TC_STATE, TC_TAPS, TC_BIAS, TC_PROMPT = 0, 24, 28, 29
TF_STATE, TF_TAPS, TF_BIAS, TF_PROMPT = 0, 16, 19, 20

STEPS = {
    "pool_steps": (("stage_zero", 2), ("eps_done", 1), ("ident_done", 1), ("ones_done", 1), ("v_pads", 1), ("vs_zero", 1), ("pads1", 2), ("ssd_consts", 7), ("pads2", 2)),
    "dve_steps": (("cf_state", 1), ("tables", 1), ("cf_new", 2), ("dt_one_plus", 1), ("dt_done", 2), ("conv_new", 2), ("ssd_region", 1), ("rstd_done", 4), ("ff_new", 1)),
    "pe_steps": (("dt_tok_ps", 1), ("hout_ps", 1), ("ea_ps", 1)),
    "act_steps": (("dt_exp", 1), ("dt_log", 1), ("hout_done", 1), ("ea_done", 1)),
    "once_in": (("small_in", 80), ("vs_store", 16), ("out_ssm_p", 16), ("vs_in", 16), ("gf_in", 16)),
    "states_out": (("cf_new_out", 576), ("conv_new_out", 256), ("ff_new_out", 128)),
    "op_in": (("ya_in", 128), ("yc_in", 128), ("yb1_in", 128), ("yb2_in", 128)),
    "op_rg": (("yb1_rg", 32), ("yb2_rg", 32)),
    "op_norm": (("yc_norm", 8), ("yb1_norm", 8), ("yb2_norm", 8)),
    "op_hi": (("ya_hi", 8), ("yc_hi", 8), ("yb1_hi", 8), ("yb2_hi", 8), ("wo_hi", 8)),
    "op_done": (("ya_op", 8), ("yc_op", 8), ("yb1_op", 8), ("yb2_op", 8), ("wo_op", 8)),
}


def gemm_phases():
    out = []
    out.append(("cf", 8, "N", [("w_in", 0, 8, OFF_CF, P), ("w_in", 0, 8, OFF_CF + D, P)]))
    out.append(("xbc", 4, "N", [("w_in", 0, 8, OFF_XBC + t * P, 6 * P) for t in range(6)]))
    out.append(("dt", 1, "N", [("w_in", 0, 8, OFF_DT, 0)]))
    sc = []
    for h in range(2):
        for part in (1, 2, 0):
            sc.append(("w_in", 0, 8, OFF_SC + part * D + h * P, 2 * P))
    out.append(("sc", 4, "N", sc))
    out.append(("z", 4, "N", [("w_in", 0, 8, OFF_Z + t * P, 4 * P) for t in range(4)]))
    out.append(("gate", 4, "N", [("w_in", 0, 8, t * P, 6 * P) for t in range(6)]))
    out.append(("ya", 4, "M", [("w_sc_out", 0, 8, t * P, 2 * P) for t in range(2)]))
    out.append(("yc", 2, "N", [("w_cf_out", 0, 8, t * P, 4 * P) for t in range(4)]))
    out.append(("yb1", 2, "M", [("w_ssm_out", 0, 8, t * P, 4 * P) for t in range(4)]))
    out.append(("yb2", 4, "N", [("w_ssm_out", 8, 8, t * P, 2 * P) for t in range(2)]))
    out.append(("wo", 4, "M", [("w_o", 0, 8, t * P, 2 * P) for t in range(2)]))
    first = 0
    for p, n in enumerate(FF_PARTS):
        out.append((f"up{p}", n, "N", [("w_up", 0, 8, (first + a * FK) * P, P) for a in range(2)]))
        out.append((f"dn{p}", 4, "M", [("w_down", first, n, t * P, 2 * P) for t in range(2)]))
        first += n
    out.append(("ple", 8, "N", [("w_ple_gate", 0, 8, 0, P), ("w_ple_proj", 0, 2, 0, P)]))
    return out


def shared(name):
    for sem, steps in STEPS.items():
        count = 0
        for step, adds in steps:
            if step == name:
                return sem, count
            count += adds
    raise KeyError(name)


def past(name):
    return shared(name)[1]


class Done:

    def __init__(self, eng, sem):
        self.eng, self.sem, self.n, self.i, self.per = eng, sem, 0, None, 0

    def mark(self, ins):
        ins.then_inc(self.sem, 1)
        self.n += 1

    def wait(self, but=0):
        v = self.n - but
        self.eng.wait_ge(self.sem, v if self.i is None else self.i * self.per + v)

    def do(self, ins):
        self.mark(ins)
        self.wait()

    @contextmanager
    def loop(self, n, per):
        first = self.n
        with self.eng.Fori(0, n) as i:
            self.i, self.per = i, per
            yield i
            assert self.n - first == per, f"{self.n - first} instructions in an iteration"
        self.i, self.n = None, first + n * per


def cols(t, base, n):
    return t[:, ds(base, n)]


def seqs(t, base, pad, shift=0, n=TS):
    seg = pad + TS
    return cols(t, base + pad + TP, NS * seg).rearrange("p (s n) -> p s n", s=NS)[:, :, pad - shift:pad - shift + n]


def tile3(ap):
    return ap.rearrange("p (b n) -> p b n", b=NB)


def tail(ap):
    return ap.rearrange("p (s n) -> p s n", n=TS)


def build(nc, A, O):
    with ExitStack() as ctx:
        sems = {}

        def S(name):
            if name not in sems:
                sems[name] = ctx.enter_context(nc.semaphore(name))
            return sems[name]

        def step(name):
            return S(shared(name)[0])

        base = (nc.sbuf_base + 63) // 64 * 64
        top = [base]

        def at(name, shape, dt, offset):
            return nc.alloc_sbuf_tensor_at(name, shape, dt, offset=offset)

        def take(name, cols_, dt=F32):
            off = top[0]
            top[0] += -(-cols_ * 4 // 32) * 32
            assert top[0] <= nc.sbuf_usable_end, (name, top[0])
            return at(name, [P, cols_], dt, off), off

        n_hi, _ = take("n_hi", KD * T, F32R)
        n_lo, _ = take("n_lo", KD * T, F32R)
        m_hi, m_at = take("m_hi", KD * T, F32R)
        m_lo, m_lo_at = take("m_lo", KD * T, F32R)
        w_raw = [take(f"w_raw{s}", KD * P)[0] for s in range(2)]
        w_hi = [take(f"w_hi{s}", KD * P, F32R)[0] for s in range(2)]
        w_lo = [take(f"w_lo{s}", KD * P, F32R)[0] for s in range(2)]
        t_cf, _ = take("t_cf", KD * 32)
        t_sc, _ = take("t_sc", KD * 32)
        t_xbc, _ = take("t_xbc", XBC // P * 32)
        t_ff, _ = take("t_ff", 2 * FK * 32)
        wide, wide_at = take("wide", 4 * PADW)
        row0, row0_at = take("row0", T)
        row1, _ = take("row1", T)
        ident, _ = take("ident", P)
        ones, _ = take("ones", P)
        d_col, _ = take("d_col", INNER // P)
        eps, _ = take("eps", 1)
        dtb, _ = take("dtb", 1)
        a_neg, _ = take("a_neg", 1)
        rows = [row0, row1]

        def wcol(k):
            return k * PADW

        v_in = at("v_in", [P, KD * CFW], F32, m_at)
        s_cf = at("s_cf", [P, KD * NS * 32], F32, m_at + KD * CFW * 4)
        s_cfp = at("s_cfp", [P, KD * 32], F32, m_at + KD * CFW * 4 + 8192)
        v_acc = at("v_acc", [P, T], F32, m_at + KD * CFW * 4 + 9216)
        v_sum = at("v_sum", [P, T], F32, m_at + KD * CFW * 4 + 9216 + 4608)
        dt_t = at("dt_t", [P, T], F32, m_at + KD * CFW * 4 + 9216 + 2 * 4608)
        da_t = at("da_t", [P, T], F32, m_at + KD * CFW * 4 + 9216 + 3 * 4608)
        assert KD * CFW * 4 + 9216 + 4 * 4608 <= KD * T * 8
        x_tok = [at(f"x_tok{b}", [P, D], F32, m_at + 4096 * b) for b in range(2)]
        xn_tok = [at(f"xn_tok{b}", [P, D], F32, m_at + 4096 * (2 + b)) for b in range(2)]
        xt_out = [at(f"xt_out{b}", [P, D], F32, m_at + 4096 * (4 + b)) for b in range(2)]
        g_row = at("g_row", [P, D], F32, m_at + 4096 * 6)
        x_junk = at("x_junk", [P, D], F32, m_at + 4096 * 7)
        x_ms = at("x_ms", [P, 32], F32, m_at + 4096 * 8)
        xbc_blk = [at(f"xbc_blk{b}", [P, 24 * P], F32, m_at + 12288 * b) for b in range(2)]
        xdt = at("xdt", [P, INNER], F32, m_at + 24576)
        xdd = at("xdd", [P, INNER], F32, m_at + 32768)
        b_tok = at("b_tok", [P, GROUPS * NST], F32, m_at + 40960)
        h_t = at("h_t", [P, INNER], F32, m_at + 43008)
        y_out = [at(f"y_out{b}", [P, 4 * P], F32, m_at + 51200 + 2048 * b) for b in range(2)]
        lm = [at(f"lm{b}", [P, HG * P], F32, m_at + 55296 + 4096 * b) for b in range(2)]
        ec = [at(f"ec{b}", [P, HG * P], F32, m_at + 63488 + 4096 * b) for b in range(2)]
        off = [wide_at]

        def small(name, n):
            t = at(name, [P, n], F32, off[0])
            off[0] += -(-n * 4 // 32) * 32
            assert off[0] <= wide_at + 16 * PADW
            return t

        tri = [small(f"tri{m}", P) for m in range(2)]
        after = [small(f"after{m}", P) for m in range(2)]
        bar = [small(f"bar{m}", P) for m in range(2)]
        sel = small("sel", NS)
        dt_tok = small("dt_tok", 9 * HEADS)
        da_tok = small("da_tok", 9 * HEADS)
        da_cur = small("da_cur", HEADS)
        acs_col = small("acs_col", HEADS)
        dec_col = small("dec_col", HEADS)
        ea_last = small("ea_last", HEADS)
        ea_seq = small("ea_seq", 16 * NS)
        b_msk = small("b_msk", NS * NST)
        s_in = [at(f"s_in{b}", [P, NS * NST], F32, row0_at + 4096 * b) for b in range(2)]
        s_t = at("s_t", [P, NS * NST], F32, m_at + 43008)
        s_out = [at(f"s_out{b}", [P, NS * NST], F32, m_at + 12288 + 4096 * b) for b in range(2)]
        h_out = at("h_out", [P, INNER], F32, wide_at + 10560)
        assert off[0] <= wide_at + 10560, off[0] - wide_at
        p_hi = at("p_hi", [P, 2 * T], F32R, m_at)
        p_lo = at("p_lo", [P, 2 * T], F32R, m_at + 9216)
        p_tok = at("p_tok", [P, 9 * PLE], F32, m_lo_at)
        h_fin = at("h_fin", [P, KD * T], F32, m_lo_at)
        y_tok = [at(f"y_tok{b}", [P, D], F32, m_at + 18432 + 4096 * b) for b in range(2)]
        gf_row = at("gf_row", [P, D], F32, m_at + 18432 + 8192)
        y_junk = at("y_junk", [P, D], F32, wide_at)

        PS = ctx.enter_context(nc.psum_tensor("PS", [P, 8, 512], F32))

        def pset(s, n=P):
            return PS[0:n, 3 * s:3 * s + 3, 0:BW]

        def flat(b0, nb):
            return PS[:, b0:b0 + nb, :].rearrange("p b n -> p (b n)")

        def pieces(s, buf, at_, pad):
            two = PS[:, 3 * s:3 * s + 2, 0:BW]
            return [(two, cols(buf, at_ + pad, 2 * BW).rearrange("p (b n) -> p b n", b=2)),
                    (PS[:, 3 * s + 2, 0:TP - 2 * BW], cols(buf, at_ + pad + 2 * BW, TP - 2 * BW)),
                    (PS[:, 3 * s + 2, TP - 2 * BW:BW].rearrange("p (s n) -> p s n", n=TS), seqs(buf, at_, pad))]

        def scratch(name, rows_, n=T):
            return nc.dram_tensor(name, (rows_, n), F32, kind="Internal").ap()

        xt_d = scratch("xt_d", D)
        xbc_d = scratch("xbc_d", XBC)
        yin_d = scratch("yin_d", D)
        v_d = scratch("v_d", D)
        vs_d = scratch("vs_d", P)
        y_d = scratch("y_d", INNER)
        ys_d = scratch("ys_d", INNER)
        rg_d = scratch("rg_d", GROUPS * P)
        gate_d = scratch("gate_d", 3 * D)
        acc_d = scratch("acc_d", D)
        h_d = scratch("h_d", D)

        def chunk(t, j):
            return t[ds(j * P, P), :]

        W = {n: A[n][0].rearrange("(k p) n -> p k n", p=P) for n in
             ("w_in", "w_sc_out", "w_cf_out", "w_ssm_out", "w_o", "w_up", "w_down", "w_ple_gate", "w_ple_proj")}
        phases, q = {}, 0
        for name, n, operand, body in gemm_phases():
            phases[name] = (n, operand, body, q)
            q += n * len(body)
        n_tiles = q

        def first(name):
            return phases[name][3]

        def body_len(name):
            return len(phases[name][2])

        w_loaded = [S("w_loaded0"), S("w_loaded1")]
        w_hi_done = S("w_hi_done")
        w_lo_done = S("w_lo_done")
        tile_done = S("tile_done")
        ps_free = [S("ps_free0"), S("ps_free1")]

        def wait_tile(eng, q):
            eng.wait_ge(tile_done, q + 2)

        def freed(name, t):
            qb = first(name) + t
            return qb % 2, qb // 2 + 2, body_len(name) // 2

        def wait_freed(eng, name, t, i):
            s, b, per = freed(name, t)
            eng.wait_ge(ps_free[s], i * per + b)

        def free(name, t):
            return ps_free[(first(name) + t) % 2]

        def last_free(name, s):
            end = first(name) + phases[name][0] * body_len(name)
            return (end + 1 - s) // 2 + 1

        def slot(name, t):
            return (first(name) + t) % 2

        block = ctx.enter_context(nc.Block())
        CHUNK_TOKENS = [(c, A["x_prompt"][0][c * P:(c + 1) * P, :]) for c in range(8)] + \
            [(8, A["x_sample"].rearrange("s t d -> (s t) d"))]
        P_TOKENS = [A["p_prompt"][0, 0][c * P:(c + 1) * P, :] for c in range(8)] + \
            [A["p_sample"][0].rearrange("s t d -> (s t) d")]

        stage_cf, stage_sc, stage_xbc, stage_ff = 0, 256, 512, 512 + 768
        def one(x):
            return x.rearrange("(a n) -> a n", a=1)
        norm_rows = A["ssm_norm_g"][0].rearrange("(a n) -> a n", a=2)
        TABLES = [
            (stage_xbc, 24, A["ssm_conv_w"][0], TC_TAPS), (stage_xbc, 24, one(A["ssm_conv_b"][0]), TC_BIAS),
            (stage_xbc, 24, A["state_ssm_conv"][0].rearrange("s r c -> (s r) c"), TC_STATE),
            (stage_cf, 8, A["cf_conv_w"][0], 0), (stage_cf, 8, one(A["cf_conv_b"][0]), CK),
            (stage_sc, 8, A["state_short_conv"][0].rearrange("s r c -> (s r) c"), TB_STATE),
            (stage_sc, 8, A["sc_conv_w"][0], TB_TAPS), (stage_sc, 8, one(A["cf_ln_g"][0]), TB_LNG),
            (stage_sc, 8, one(A["cf_ln_b"][0]), TB_LNB), (stage_sc, 8, one(A["g_ffn"][0]), TB_GFFN),
            (stage_sc, 8, one(A["g_ple"][0]), TB_GPLE), (stage_sc, 8, norm_rows, TB_NORM),
            (stage_ff, 44, A["state_ffn_conv"][0].rearrange("s r c -> (s r) c"), TF_STATE),
            (stage_ff, 44, A["ff_conv_w"][0], TF_TAPS), (stage_ff, 44, one(A["ff_conv_b"][0]), TF_BIAS),
        ]

        cf_new = at("cf_new", [P, 2304], F32, row0_at)
        conv_new = at("conv_new", [P, 1024], F32, row0_at)
        ff_new = wide[:, 2 * PADW:2 * PADW + 2 * FK * 32]
        cf_stage = at("cf_stage", [P, KD * NS * 32], F32, row0_at)

        @block.sync
        def _(sp):
            def load_w(name, t, i):
                n, _, body, qb = phases[name]
                weight, k0, nk, col, step = body[t]
                s = slot(name, t)
                sp.wait_ge(w_lo_done, i * len(body) + qb + t + 1)
                src = W[weight][:, k0:k0 + nk, ds(i * step + col, P)]
                sp.dma_start(w_raw[s][:, 0:nk * P].rearrange("p (k n) -> p k n", k=nk), src).then_inc(w_loaded[s], 16)

            for t in range(2):
                load_w("cf", t, 0)
            sp.wait_ge(step("stage_zero"), past("stage_zero") + 2)
            for b in range(NS):
                src = A["state_cf_conv"][0, b].rearrange("r (j q c) -> r j q c", q=4, c=32)
                for qd in range(4):
                    dst = cf_stage[32 * qd:32 * qd + CPAD, :].rearrange("r (j s c) -> r j s c", j=KD, s=NS)[:, :, b, :]
                    sp.dma_start(dst, src[:, :, qd, :]).then_inc(S("cf_state_in"), 16)
            for stage, n_, src, r0 in TABLES:
                r = src.shape[0]
                src_q = src.rearrange("r (j q c) -> r j q c", q=4, c=32)
                for qd in range(4):
                    dst = wide[32 * qd + r0:32 * qd + r0 + r, stage:stage + n_ * 32].rearrange("r (j c) -> r j c", c=32)
                    sp.dma_start(dst, src_q[:, :, qd, :]).then_inc(S("tables_in"), 16)

            def save_rows(sem_, stage, n_, r0, dst):
                r = dst.shape[0]
                for qd in range(4):
                    sp.dma_start(dst.rearrange("r (j q c) -> r j q c", q=4, c=32)[:, :, qd, :],
                                 stage[32 * qd + r0:32 * qd + r0 + r, 0:n_ * 32].rearrange("r (j c) -> r j c", c=32))\
                        .then_inc(step(sem_), 16)

            def after_loads(name):
                if name == "xbc":
                    sp.wait_ge(step("cf_new"), past("cf_new") + 2)
                    for b in range(NS):
                        dst = O["cf_s"][0, b].rearrange("r (j q c) -> r j q c", q=4, c=32)
                        for qd in range(4):
                            src = cf_new[32 * qd:32 * qd + CPAD, 0:2048].rearrange("r (j s c) -> r j s c", j=KD, s=NS)
                            sp.dma_start(dst[:, :, qd, :], src[:, :, b, :]).then_inc(step("cf_new_out"), 16)
                    save_rows("cf_new_out", cf_new[:, 2048:2304], KD, 0, O["cf_p"][0, 0])
                if name == "sc":
                    sp.wait_ge(step("conv_new"), past("conv_new") + 2)
                    save_rows("conv_new_out", conv_new[:, 0:768], 24, TC_STATE, O["xbc_s"][0].rearrange("s r c -> (s r) c"))
                    save_rows("conv_new_out", conv_new[:, 0:768], 24, TC_PROMPT, O["xbc_p"][0, 0])
                    save_rows("conv_new_out", conv_new[:, 768:1024], KD, TB_STATE, O["sc_s"][0].rearrange("s r c -> (s r) c"))
                    save_rows("conv_new_out", conv_new[:, 768:1024], KD, TB_PROMPT, O["sc_p"][0, 0])
                if name == "dn2":
                    sp.wait_ge(step("ff_new"), past("ff_new") + 1)
                    save_rows("ff_new_out", ff_new, 2 * FK, TF_STATE, O["ff_s"][0].rearrange("s r c -> (s r) c"))
                    save_rows("ff_new_out", ff_new, 2 * FK, TF_PROMPT, O["ff_p"][0, 0])

            for name, (n, operand, body, qb) in phases.items():
                if n == 1:
                    load_w(name, 0, 0)
                    continue
                with sp.Fori(1 if name == "cf" else 0, n) as i:
                    for t in range(len(body)):
                        load_w(name, t, i)
                after_loads(name)
            sp.wait_ge(step("cf_new_out"), past("cf_new_out") + 16 * 36)
            sp.wait_ge(step("conv_new_out"), past("conv_new_out") + 16 * 16)
            sp.wait_ge(step("ff_new_out"), past("ff_new_out") + 16 * 8)

        @block.tensor
        def _(pe):
            pe.sem_inc(tile_done, 1)
            pe.sem_inc(S("y_ps"), 2)

            def operand_count(name):
                if name in ("ya", "yc", "yb1", "yb2", "wo"):
                    return step(f"{name}_op"), past(f"{name}_op") + 1
                if name in ("up0", "ple"):
                    return S("norm_op"), 0 if name == "up0" else KD
                if name.startswith("dn"):
                    return S("ff_op"), sum(FF_PARTS[:int(name[2])]) + 1
                return None, 0

            def tile(name, t, i):
                split, before = operand_count(name)
                n, operand, body, qb = phases[name]
                nk = body[t][2]
                s = slot(name, t)
                x_hi, x_lo = (p_hi, p_lo) if body[t][0] == "w_ple_proj" else (n_hi, n_lo) if operand == "N" else (m_hi, m_lo)
                pe.wait_ge(w_lo_done, i * len(body) + qb + t + 3)
                fs, fb, per = freed(name, t)
                pe.wait_ge(ps_free[fs], i * per + fb - 1)
                for k in range(nk):
                    if split is not None and t == 0:
                        pe.wait_ge(split, before + k + 1)
                    w_h, w_l = (x[:, k * P:(k + 1) * P] for x in (w_hi[s], w_lo[s]))
                    for w, x, z in ((w_h, x_hi, 0), (w_h, x_lo, 1), (w_l, x_hi, 2)):
                        for b in range(NB):
                            at_ = k * T + b * BW
                            last = pe.matmul(PS[:, 3 * s + b, 0:BW], w, x[:, at_:at_ + BW],
                                             start=(k == 0 and z == 0), stop=(k == nk - 1 and z == 2))
                last.then_inc(tile_done, 1)

            def product(name):
                n, operand, body, qb = phases[name]
                if n == 1:
                    tile(name, 0, 0)
                    return
                with pe.Fori(0, n) as i:
                    for t in range(len(body)):
                        tile(name, t, i)

            pe.wait_ge(step("ident_done"), past("ident_done") + 1)
            for c in range(9):
                b = c % 2
                if c >= 2:
                    pe.wait_ge(S("xt_evac"), c - 1)
                    pe.wait_ge(S("n_ready"), c - 1)
                pe.wait_ge(S(f"x_in{b}"), 16 * (c // 2 + 1))
                for k in range(KD):
                    last = pe.transpose(PS[:, 4 * b + k // 4, (k % 4) * P:(k % 4 + 1) * P],
                                        x_tok[b][:, k * P:(k + 1) * P], ident[:, :])
                last.then_inc(S("xt_done"), 1)
                pe.wait_ge(S("xn_done"), c + 1)
                for k in range(KD):
                    last = pe.transpose(PS[:, 4 * b + 2 + k // 4, (k % 4) * P:(k % 4 + 1) * P],
                                        xn_tok[b][:, k * P:(k + 1) * P], ident[:, :])
                last.then_inc(S("xnt_done"), 1)
            pe.wait_ge(S("n_ready"), 9)
            pe.wait_ge(S("xt_evac"), 9)
            product("cf")
            product("xbc")
            product("dt")
            product("sc")

            for s in range(2):
                pe.wait_ge(ps_free[s], last_free("sc", s))
            pe.wait_ge(step("ssd_consts"), past("ssd_consts") + 7)
            pe.wait_ge(step("dt_done"), past("dt_done") + 2)
            for m, src in enumerate((dt_t, da_t)):
                for c in range(9):
                    last = pe.transpose(PS[:, m, c * HEADS:(c + 1) * HEADS], src[0:HEADS, c * P:(c + 1) * P],
                                        ident[0:HEADS, 0:HEADS])
            last.then_inc(step("dt_tok_ps"), 1)

            def block_head(sample, c, b):
                blk = xbc_blk[b]
                pe.wait_ge(S(f"blk_in{b}"), 8 * (c - b) + 16)
                pe.wait_ge(S("blk_done"), c + 1)
                pe.wait_ge(S("da_cur_done"), c + 1)
                for m, w in enumerate((tri[sample], after[sample])):
                    last = pe.matmul(PS[:, 4, m * HEADS:(m + 1) * HEADS], w[:, :], da_cur[:, :], start=True, stop=True)
                last.then_inc(S("acs_ps"), 1)
                for g in range(GROUPS):
                    last = pe.transpose(PS[:, 5, g * P:(g + 1) * P], blk[:, (16 + g) * P:(17 + g) * P], ident[:, :])
                for g in range(GROUPS):
                    last = pe.matmul(PS[:, 6, g * P:(g + 1) * P], blk[:, (16 + g) * P:(17 + g) * P],
                                     blk[:, (20 + g) * P:(21 + g) * P], start=True, stop=True)
                last.then_inc(S("b_ps"), 1)
                for j in range(16):
                    last = pe.transpose(PS[:, j // 4, (j % 4) * P:(j % 4 + 1) * P], blk[:, j * P:(j + 1) * P], ident[:, :])
                last.then_inc(S("x_ps"), 1)

            def cum_rows(sample, g, b0):
                for r in range(HG):
                    h = g * HG + r
                    last = pe.matmul(PS[:, b0 + r // 4, (r % 4) * P:(r % 4 + 1) * P],
                                     da_cur[:, h:h + 1].to_broadcast([P, P]), tri[sample][:, :], start=True, stop=True)
                last.then_inc(S("cum_ps"), 1)

            def prompt_block(c, b):
                block_head(0, c, b)
                pe.wait_ge(S("xdt_done"), c + 1)
                for g in range(2):
                    cum_rows(0, g, 2 * g)
                for g in range(GROUPS):
                    pe.wait_ge(S("ec_done"), c * 4 + g + 1)
                    pe.wait_ge(S("lm_done"), c * 4 + g + 1)
                    if g == 0:
                        pe.wait_ge(S("acs_done"), c + 1)
                        pe.wait_ge(S("dec_done"), c + 1)
                        pe.wait_ge(S("btok_done"), c + 1)
                    if g >= 2:
                        pe.wait_ge(S("y_done"), c * 4 + g)
                    for r in range(HG):
                        h = g * HG + r
                        o = PS[64 * (r % 2):64 * (r % 2) + 64, 4 + g % 2, (r // 2) * P:(r // 2 + 1) * P]
                        pe.matmul(o, xdt[:, h * HD:(h + 1) * HD], lm[g % 2][:, r * P:(r + 1) * P], start=True, stop=False)
                        last = pe.matmul(o, h_t[:, h * HD:(h + 1) * HD], ec[g % 2][:, r * P:(r + 1) * P],
                                         start=False, stop=True)
                    last.then_inc(S("y_ps"), 1)
                    if g + 2 < GROUPS:
                        cum_rows(0, g + 2, 2 * (g % 2))
                    pe.wait_ge(S("xdd_done"), c + 1)
                    pe.wait_ge(S("h_done"), c * 4 + g + 1)
                    pe.matmul(PS[:, 7, :], b_tok[:, g * P:(g + 1) * P], xdd[:, g * 512:(g + 1) * 512],
                              start=True, stop=True).then_inc(S("h_ps"), 1)

            with pe.Fori(0, 4) as i:
                for b in range(2):
                    prompt_block(2 * i + b, b)
            pe.wait_ge(S("h_done"), 33)
            pe.wait_ge(S("y_done"), 33)
            for j in range(16):
                last = pe.transpose(PS[:, j // 4, (j % 4) * P:(j % 4 + 1) * P], h_t[:, j * P:(j + 1) * P], ident[:, :])
            last.then_inc(step("hout_ps"), 1)
            pe.wait_ge(step("hout_done"), past("hout_done") + 1)

            block_head(1, 8, 0)
            pe.wait_ge(S("xdt_done"), 9)
            pe.wait_ge(step("hout_done"), past("hout_done") + 1)
            for h in range(HEADS):
                r = h % 2
                last = pe.matmul(PS[64 * r:64 * r + 64, 7, h // 2 * NS:(h // 2 + 1) * NS],
                                 da_cur[:, h:h + 1].to_broadcast([P, HD]), sel[:, :], start=True, stop=True)
            last.then_inc(step("ea_ps"), 1)
            for g in range(GROUPS):
                if g:
                    pe.wait_ge(S("lm_done"), 32 + g)
                    pe.wait_ge(S("ec_done"), 32 + g)
                cum_rows(1, g, 0)
                pe.wait_ge(S("lm_done"), 33 + g)
                pe.wait_ge(S("ec_done"), 33 + g)
                if g == 0:
                    pe.wait_ge(step("ea_done"), past("ea_done") + 1)
                else:
                    pe.wait_ge(S("y_done"), 33 + g)
                for r in range(HG):
                    h = g * HG + r
                    o = PS[64 * (r % 2):64 * (r % 2) + 64, 7, (r // 2) * P:(r // 2 + 1) * P]
                    last = pe.matmul(o, xdt[:, h * HD:(h + 1) * HD], lm[0][:, r * P:(r + 1) * P],
                                     start=(r < 2), stop=True, skip_group_check=True)
                for pr in range(4):
                    j = 4 * g + pr
                    pe.wait_ge(S(f"s_in_sem{j % 2}"), 16 * (j // 2 + 1))
                    if j:
                        pe.wait_ge(S("st_done"), j)
                    for b in range(NS):
                        last = pe.transpose(PS[:, 2 + b // 4, (b % 4) * P:(b % 4 + 1) * P],
                                            s_in[j % 2][:, b * P:(b + 1) * P], ident[:, :])
                    last.then_inc(S("st_ps"), 1)
                    if pr == 0:
                        pe.wait_ge(S("bmsk_done"), g + 1)
                    if j == 0:
                        pe.wait_ge(S("xdd_done"), 9)
                        pe.wait_ge(S("btok_done"), 9)
                    if j:
                        pe.wait_ge(S("sout_done"), j)
                    for z in range(2):
                        last = pe.matmul(PS[:, 4 + z, :], xdd[:, j * P:(j + 1) * P], b_msk[:, z * 512:(z + 1) * 512],
                                         start=True, stop=True)
                    last.then_inc(S("sb_ps"), 1)
                    pe.wait_ge(S("st_done"), j + 1)
                    for r in range(2):
                        for b in range(NS):
                            o = PS[64 * r:64 * r + 64, 7, pr * P + b * TS:pr * P + (b + 1) * TS]
                            e = (2 * pr + r) * P + b * TS
                            last = pe.matmul(o, s_t[:, b * P + r * HD:b * P + (r + 1) * HD], ec[0][:, e:e + TS],
                                             start=False, stop=True, skip_group_check=True)
                    last.then_inc(S("ys_ps"), 1)
            pe.wait_ge(S("y_done"), 37)
            pe.wait_ge(S("sout_done"), 16)

            product("z")

            n_stat = [0]

            def stat(src):
                for b in range(NB):
                    k = 3 * n_stat[0] + b
                    if k >= 2:
                        pe.wait_ge(S("stat_out"), k - 1)
                    pe.matmul(PS[:, 6 + k % 2, 0:BW], ones[:, :], src[:, b * BW:(b + 1) * BW],
                              start=True, stop=True).then_inc(S("stat_ps"), 1)
                n_stat[0] += 1

            pe.wait_ge(S("grp_sum"), 17)
            for g in range(GROUPS):
                stat(wide[:, wcol(g):wcol(g) + T])
            pe.wait_ge(step("vs_in"), past("vs_in") + 16)
            stat(row0)
            product("gate")
            pe.wait_ge(S("var_sum"), 9)
            stat(wide[:, wcol(1):wcol(1) + T])
            for name in ("ya", "yc", "yb1", "yb2", "wo"):
                product(name)
            pe.wait_ge(S("sq_sum"), 9)
            stat(wide[:, 0:T])
            for p, n in enumerate(FF_PARTS):
                product(f"up{p}")
                product(f"dn{p}")
            pe.wait_ge(S("sq_sum"), 18)
            stat(wide[:, 0:T])
            pe.wait_ge(S("p_in"), 16 * 9)
            pe.wait_ge(S("stat_out"), 3 * n_stat[0])
            for c in range(9):
                if c >= 2:
                    pe.wait_ge(S("p_op"), c - 1)
                for k in range(2):
                    last = pe.transpose(PS[:, 6 + c % 2, k * P:(k + 1) * P],
                                        p_tok[:, c * PLE + k * P:c * PLE + (k + 1) * P], ident[:, :])
                last.then_inc(S("p_ps"), 1)
            pe.wait_ge(S("p_op"), 9)
            product("ple")
            pe.wait_ge(S("fin_done"), 9)
            for c in range(9):
                b = c % 2
                if c >= 2:
                    pe.wait_ge(S("y_scaled"), c - 1)
                for k in range(KD):
                    last = pe.transpose(PS[:, 2 * b + k // 4, (k % 4) * P:(k % 4 + 1) * P],
                                        h_fin[:, k * T + c * P:k * T + (c + 1) * P], ident[:, :])
                last.then_inc(S("fin_ps"), 1)

        @block.scalar
        def _(act):
            own = Done(act, S("act_own"))
            for s in range(2):
                act.sem_inc(ps_free[s], 1)
            for name in ("v_store", "xbc_store0", "xbc_store1", "yin_store0", "yin_store1", "gate_store0",
                         "gate_store1", "ys_store", "y_store0", "y_store1", "acc_store0", "acc_store1", "h_store0", "h_store1"):
                act.sem_inc(S(name), 16)

            def split_next(name, t, i):
                n, _, body, qb = phases[name]
                ln, k = len(body), qb + t + 1
                act.wait_ge(tile_done, i * ln + k)
                act.wait_ge(w_loaded[k % 2], i * (8 * ln) + 16 * (k // 2 + 1))
                act.activation(w_hi[k % 2][:, :], w_raw[k % 2][:, :], ACT.Copy).then_inc(w_hi_done, 1)

            def store(name, dst, src):
                act.dma_start(dst, src).then_inc(S(name), 16)

            act.dma_start(g_row[:, :], A["g_mix"][0].rearrange("(a n) -> a n", a=1).to_broadcast([P, D]))\
                .then_inc(step("small_in"), 16)
            act.dma_start(dtb[0:HEADS, :], A["ssm_dt_bias"][0].rearrange("(n a) -> n a", a=1)).then_inc(step("small_in"), 16)
            act.dma_start(a_neg[0:HEADS, :], A["ssm_a_log"][0].rearrange("(n a) -> n a", a=1)).then_inc(step("small_in"), 16)
            for r in range(2):
                src = A["ssm_d"][0].rearrange("(a j r) -> a r j", a=1, r=2)[:, r, :]
                act.dma_start(d_col[64 * r:64 * r + 64, :], src.to_broadcast([64, 16]),
                              allow_slow_non_contiguous=True).then_inc(step("small_in"), 16)
            for c, src in CHUNK_TOKENS[:2]:
                act.dma_start(x_tok[c][:, :], src).then_inc(S(f"x_in{c}"), 16)
            act.wait_ge(w_loaded[0], 16)
            act.activation(w_hi[0][:, :], w_raw[0][:, :], ACT.Copy).then_inc(w_hi_done, 1)
            act.wait_ge(step("eps_done"), past("eps_done") + 1)

            def x_square(c):
                b = c % 2
                act.wait_ge(S(f"x_in{b}"), 16 * (c // 2 + 1))
                own.do(act.activation(x_junk[:, :], x_tok[b][:, :], ACT.Square, accum_out=x_ms[:, c:c + 1]))
                act.activation(x_ms[:, 9 + c:10 + c], x_ms[:, c:c + 1], ACT.Sqrt, bias=eps[:, 0:1], scale=1.0 / D)\
                    .then_inc(S("x_rms"), 1)

            def x_out(c):
                b = c % 2
                act.wait_ge(S("xt_done"), c + 1)
                if c >= 2:
                    act.wait_ge(S(f"xt_store{b}"), 16 * (c // 2))
                act.activation(xt_out[b][:, :], flat(4 * b, 2), ACT.Copy).then_inc(S("xt_evac"), 1)
                act.wait_ge(S("xt_evac"), c + 1)
                dst = xt_d.rearrange("(k p) n -> p k n", p=P)[:, :, c * P:(c + 1) * P]
                act.dma_start(dst, xt_out[b][:, :].rearrange("p (k n) -> p k n", k=KD)).then_inc(S(f"xt_store{b}"), 16)
                act.wait_ge(S("xnt_done"), c + 1)
                act.activation(n_hi[:, :].rearrange("p (k n) -> p k n", k=KD)[:, :, c * P:(c + 1) * P],
                               flat(4 * b + 2, 2).rearrange("p (k n) -> p k n", k=KD), ACT.Copy).then_inc(S("nhi_done"), 1)

            for c in range(9):
                x_square(c)
                if c:
                    x_out(c - 1)
                if 1 <= c < 8:
                    act.wait_ge(S("xt_done"), c)
                    act.wait_ge(S("xn_done"), c)
                    b, src = (c + 1) % 2, CHUNK_TOKENS[c + 1][1]
                    act.dma_start(x_tok[b][:, :], src).then_inc(S(f"x_in{b}"), 16)
            x_out(8)

            act.wait_ge(step("cf_state"), past("cf_state") + 1)
            act.wait_ge(S("n_ready"), 9)
            with act.Fori(0, 8) as i:
                split_next("cf", 0, i)
                split_next("cf", 1, i)
                wait_tile(act, 2 * i + 1)
                act.wait_ge(ps_free[0], i + 1)
                act.activation(tile3(row0[:, :]), pset(1), ACT.Sigmoid).then_inc(ps_free[1], 1)

            def cf_tap(c):
                act.wait_ge(S("v_store"), c * 16 + 16)
                act.wait_ge(S("cf_summed"), c + 1)
                w = t_cf[:, ds(c * 32 + CK - 1, 1)]
                bias = t_cf[:, ds(c * 32 + CK, 1)]
                act.activation(v_acc[:, 0:TP], cols(v_in, c * CFW + CPAD, TP), ACT.Identity, bias=bias, scale=w)
                act.activation(tail(v_acc[:, TP:T]), seqs(v_in, c * CFW, CPAD), ACT.Identity, bias=bias, scale=w)\
                    .then_inc(S("cf_tap"), 1)

            def cf_out(c):
                act.wait_ge(S("cf_conv"), c + 1)
                store("v_store", chunk(v_d, c), v_acc[:, :])

            act.wait_ge(step("tables"), past("tables") + 1)
            with act.Fori(0, 4) as i:
                for t in range(6):
                    j = i * 6 + t
                    split_next("xbc", t, i)
                    if t == 0:
                        cf_tap(i)
                    wait_tile(act, j + first("xbc"))
                    pad, acc = wcol(t % 2), wcol(2 + t % 2)
                    act.wait_ge(S("xbc_state"), j + 1)
                    for src, dst in pieces(slot("xbc", t), wide, pad, PAD):
                        act.activation(dst, src, ACT.Copy)
                    act.wait_ge(S(f"xbc_store{t % 2}"), i * 48 + 16 * (t // 2 + 1))
                    act.activation(tile3(wide[:, acc:acc + T]), pset(slot("xbc", t)), ACT.Identity,
                                   scale=t_xbc[:, ds(i * 192 + t * 32 + TC_TAPS + 3, 1)],
                                   bias=t_xbc[:, ds(i * 192 + t * 32 + TC_BIAS, 1)]).then_inc(free("xbc", t), 1)
                    act.wait_ge(S("xbc_conv"), j + 3)
                    act.activation(wide[:, acc:acc + T], wide[:, acc:acc + T], ACT.Silu).then_inc(S("xbc_silu"), 1)
                    act.wait_ge(S("xbc_silu"), j + 1)
                    store(f"xbc_store{t % 2}", chunk(xbc_d, j), wide[:, acc:acc + T])
                    if t == 5:
                        cf_out(i)

            split_next("dt", 0, 0)
            wait_tile(act, first("dt"))
            x_ = tile3(dt_t[0:HEADS, :])
            act.activation(x_, pset(slot("dt", 0), HEADS), ACT.Identity, bias=dtb[0:HEADS, :]).then_inc(free("dt", 0), 1)
            wait_freed(act, "dt", 0, 0)
            act.wait_ge(step("cf_new_out"), past("cf_new_out") + 16 * 36)
            own.do(act.activation(row0[0:HEADS, :], dt_t[0:HEADS, :], ACT.Abs))
            own.do(act.activation(row0[0:HEADS, :], row0[0:HEADS, :], ACT.Exp, scale=-1.0))
            act.activation(a_neg[0:HEADS, :], a_neg[0:HEADS, :], ACT.Exp).then_inc(step("dt_exp"), 1)
            act.wait_ge(step("dt_one_plus"), past("dt_one_plus") + 1)
            act.activation(da_t[0:HEADS, :], row1[0:HEADS, :], ACT.Ln).then_inc(step("dt_log"), 1)

            with act.Fori(0, 4) as i:
                for t in range(6):
                    h = t // 3
                    split_next("sc", t, i)
                    if t == 0:
                        cf_tap(i + 4)
                    if t % 3 == 0:
                        wait_tile(act, i * 6 + t + first("sc"))
                        s_, b_, per_ = freed("sc", t + 1)
                        act.wait_ge(ps_free[s_], i * per_ + b_ - per_)
                        if t == 0:
                            act.wait_ge(step("dt_done"), past("dt_done") + 2)
                        act.activation(tile3(rows[h][:, :]), pset(slot("sc", t)), ACT.Copy).then_inc(free("sc", t), 1)
                    elif t % 3 == 1:
                        wait_freed(act, "sc", t, i)
                        acc = wcol(2 + h)
                        act.wait_ge(S(f"yin_store{h}"), i * 16 + 16)
                        w = t_sc[:, ds(i * 64 + h * 32 + TB_TAPS + 2, 1)]
                        act.activation(wide[:, acc:acc + TP], wide[:, wcol(h) + PAD:wcol(h) + PAD + TP],
                                       ACT.Identity, scale=w)
                        act.activation(tail(wide[:, acc + TP:acc + T]), seqs(wide, wcol(h), PAD), ACT.Identity, scale=w)\
                            .then_inc(S("sc_tap"), 1)
                    else:
                        wait_freed(act, "sc", t, i)
                        acc = wcol(2 + h)
                        store(f"yin_store{h}", chunk(yin_d, i * 2 + h), wide[:, acc:acc + T])
                        if t == 5:
                            cf_out(i + 4)
            act.wait_ge(S("cf_summed"), 9)
            act.dma_start(vs_d[:, :], v_sum[:, :]).then_inc(step("vs_store"), 16)

            act.wait_ge(S("v_store"), 16 * 9)
            act.wait_ge(S("xbc_store0"), 16 * 13)
            act.wait_ge(S("xbc_store1"), 16 * 13)
            act.wait_ge(step("vs_store"), past("vs_store") + 16)
            act.wait_ge(step("ssd_region"), past("ssd_region") + 1)

            def load_block(c, b):
                src = xbc_d.rearrange("(k p) n -> p k n", p=P)[:, :, ds(c * P, P)]
                act.dma_start(xbc_blk[b][:, :].rearrange("p (k n) -> p k n", k=24), src).then_inc(S(f"blk_in{b}"), 16)

            def y_rows(c, g):
                return y_d.rearrange("(k p) n -> p k n", p=P)[:, 4 * g:4 * g + 4, ds(c * P, P)]

            def ssd_head(c):
                act.wait_ge(S("acs_ps"), c + 1)
                act.wait_ge(S("blk_done"), c + 1)
                act.wait_ge(S("acs_done"), c + 1)
                act.activation(dec_col[:, :], PS[:, 4, HEADS:2 * HEADS], ACT.Exp).then_inc(S("dec_done"), 1)
                act.wait_ge(S("b_ps"), c + 1)
                act.activation(b_tok[:, :], PS[:, 5, :], ACT.Copy).then_inc(S("btok_done"), 1)

            load_block(0, 0)
            with act.Fori(0, 4) as i:
                for b in range(2):
                    c = i * 2 + b
                    act.wait_ge(S("blk_done"), c + 1)
                    act.wait_ge(S("y_done"), c * 4 + 1)
                    load_block(c + 1, 1 - b)
                    ssd_head(c)
                    for g in range(GROUPS):
                        k = c * 4 + g
                        act.wait_ge(S("cum_ps"), k + 1)
                        act.wait_ge(S("y_ps"), k + 1)
                        act.activation(ec[g % 2][:, :], flat(2 * (g % 2), 2), ACT.Exp).then_inc(S("e_done"), 1)
                        act.wait_ge(S("diff_done"), k + 1)
                        act.activation(lm[g % 2][:, :], lm[g % 2][:, :], ACT.Exp).then_inc(S("l_done"), 1)
                        if g:
                            act.wait_ge(S("y_done"), k + 1)
                            store(f"y_store{(g - 1) % 2}", y_rows(c, g - 1), y_out[(g - 1) % 2][:, :].rearrange("p (j n) -> p j n", j=4))
                    act.wait_ge(S("y_done"), c * 4 + 5)
                    store("y_store1", y_rows(c, 3), y_out[1][:, :].rearrange("p (j n) -> p j n", j=4))
            act.wait_ge(step("hout_ps"), past("hout_ps") + 1)
            act.activation(h_out[:, :], flat(0, 4), ACT.Copy).then_inc(step("hout_done"), 1)
            act.wait_ge(step("hout_done"), past("hout_done") + 1)
            act.dma_start(O["ssm_p"][0, 0].rearrange("(j r) p n -> (r p) j n", r=2),
                          h_out[:, :].rearrange("p (j n) -> p j n", j=16)).then_inc(step("out_ssm_p"), 16)
            states = A["state_ssm"][0].rearrange("b (j r) p n -> j (r p) b n", r=2)
            new_states = O["ssm_s"][0].rearrange("b (j r) p n -> j (r p) b n", r=2)

            def load_state(j):
                act.dma_start(s_in[j % 2][:, :].rearrange("p (b n) -> p b n", b=NS), states[j])\
                    .then_inc(S(f"s_in_sem{j % 2}"), 16)

            act.wait_ge(step("conv_new_out"), past("conv_new_out") + 16 * 16)
            load_state(0)
            load_state(1)
            ssd_head(8)
            act.wait_ge(step("ea_ps"), past("ea_ps") + 1)
            act.activation(ea_seq[:, :], PS[:, 7, 0:P], ACT.Exp).then_inc(step("ea_done"), 1)
            for g in range(GROUPS):
                k = 32 + g
                act.wait_ge(S("cum_ps"), k + 1)
                if g:
                    act.wait_ge(S("ys_ps"), 4 * g)
                else:
                    act.wait_ge(S("y_ps"), 34)
                act.activation(ec[0][:, :], flat(0, 2), ACT.Exp).then_inc(S("e_done"), 1)
                act.wait_ge(S("diff_done"), k + 1)
                act.activation(lm[0][:, :], lm[0][:, :], ACT.Exp).then_inc(S("l_done"), 1)
                for pr in range(4):
                    j = 4 * g + pr
                    act.wait_ge(S("st_ps"), j + 1)
                    if j:
                        act.wait_ge(S("ys_ps"), j)
                    act.activation(s_t[:, :], flat(2, 2), ACT.Copy).then_inc(S("st_done"), 1)
                    act.wait_ge(S("sout_done"), j + 1)
                    act.dma_start(new_states[j], s_out[j % 2][:, :].rearrange("p (b n) -> p b n", b=NS))\
                        .then_inc(S(f"out_ssm_s{j % 2}"), 16)
                    if j + 2 < 16:
                        load_state(j + 2)
                act.wait_ge(S("y_done"), 34 + g)
                store(f"y_store{g % 2}", y_rows(8, g), y_out[g % 2][:, :].rearrange("p (j n) -> p j n", j=4))
            act.wait_ge(S("y_store0"), 16 * 19)
            act.wait_ge(S("y_store1"), 16 * 19)

            act.wait_ge(step("out_ssm_p"), past("out_ssm_p") + 16)
            for b in range(2):
                act.wait_ge(S(f"out_ssm_s{b}"), 16 * 8)
            with act.Fori(0, 4) as i:
                for t in range(4):
                    j = i * 4 + t
                    split_next("z", t, i)
                    act.wait_ge(S("ys_store"), j * 16 + 16)
                    act.wait_ge(S("grp_sum"), j + 1)
                    act.dma_start(row0[:, :], chunk(y_d, j)).then_inc(S("y_in"), 16)
                    wait_tile(act, j + first("z"))
                    act.activation(tile3(row1[:, :]), pset(slot("z", t)), ACT.Silu).then_inc(free("z", t), 1)
                    act.wait_ge(S("ys_done"), j + 1)
                    store("ys_store", chunk(ys_d, j), row0[:, :])
                    act.activation(row1[:, :], row0[:, :], ACT.Square).then_inc(S("grp_sq"), 1)

            n_stat = [0]

            def stat(dst, rstd, scale=1.0):
                for b in range(NB):
                    k = 3 * n_stat[0] + b
                    act.wait_ge(S("stat_ps"), k + 1)
                    o = dst[:, b * BW:(b + 1) * BW]
                    if rstd:
                        act.activation(o, PS[:, 6 + k % 2, 0:BW], ACT.Sqrt, bias=eps[:, 0:1], scale=scale)\
                            .then_inc(S("stat_out"), 1)
                    else:
                        act.activation(o, PS[:, 6 + k % 2, 0:BW], ACT.Copy).then_inc(S("stat_out"), 1)
                n_stat[0] += 1

            act.wait_ge(S("ys_store"), 16 * 17)
            act.wait_ge(S("grp_sum"), 17)
            act.dma_start(row0[:, :], vs_d[:, :]).then_inc(step("vs_in"), 16)
            for g in range(GROUPS):
                stat(wide[:, wcol(g):wcol(g) + T], True, scale=float(D) / (INNER // GROUPS))
            for g in range(GROUPS):
                act.wait_ge(step("rstd_done"), past("rstd_done") + g + 1)
                act.dma_start(rg_d[g * P:(g + 1) * P, :], wide[:, wcol(g):wcol(g) + T]).then_inc(S("rg_store"), 16)
            act.wait_ge(S("rg_store"), 64)
            stat(wide[:, 0:T], False)

            with act.Fori(0, 4) as i:
                for t in range(6):
                    split_next("gate", t, i)
                    if t % 3 == 1:
                        k = i * 2 + t // 3
                        act.wait_ge(S("var_sum"), k + 1)
                        act.dma_start(cols(wide, wcol(2), T), chunk(v_d, k)).then_inc(S("v_in_sem"), 16)
                        act.wait_ge(S("v_cent"), k + 1)
                        act.activation(cols(wide, wcol(2), T), cols(wide, wcol(2), T), ACT.Square)\
                            .then_inc(S("v_sq"), 1)
                    if t % 3 == 2:
                        k = i * 2 + t // 3
                        act.wait_ge(step("ya_op"), past("ya_op") + k + 1)
                        act.dma_start(cols(wide, wcol(3), T), chunk(yin_d, k)).then_inc(step("ya_in"), 16)
                        act.wait_ge(step("ya_in"), past("ya_in") + k * 16 + 16)
                        act.activation(cols(m_hi, k * T, T), cols(wide, wcol(3), T), ACT.Copy).then_inc(step("ya_hi"), 1)
                    wait_tile(act, i * 6 + t + first("gate"))
                    act.wait_ge(S(f"gate_store{t % 2}"), i * 48 + 16 * (t // 2 + 1))
                    act.activation(tile3(rows[t % 2][:, :]), pset(slot("gate", t)), ACT.Sigmoid).then_inc(free("gate", t), 1)
                    wait_freed(act, "gate", t, i)
                    store(f"gate_store{t % 2}", chunk(gate_d, i * 6 + t), rows[t % 2][:, :])
            act.wait_ge(S("var_sum"), 9)
            stat(wide[:, wcol(1):wcol(1) + T], True)
            for s in range(2):
                act.wait_ge(S(f"gate_store{s}"), 16 * 13)

            def sum_rows(name, t):
                if name == "ya":
                    return rows[t % 2][:, :], None
                return (row0[:, :], row1[:, :]) if t % 2 == 0 else (cols(wide, wcol(3), T), cols(wide, wcol(0), T))

            done = 0
            for b, name, nxt, op in ((0, "ya", "yc", "ya_op"), (2, "yc", "yb1", "yc_op"),
                                     (1, "yb1", "yb2", "yb1_op"), (1, "yb2", "wo", "yb2_op")):
                ln = body_len(name)
                act.wait_ge(step(op), past(op) + 9)
                if name == "yc":
                    for z in range(2):
                        act.wait_ge(S(f"acc_store{z}"), 16 * 5)
                with act.Fori(0, phases[name][0]) as i:
                    for t in range(ln):
                        k = i * ln + t
                        gate_row, acc_row = sum_rows(name, t)
                        if name == "yb2":
                            act.wait_ge(step("wo_op"), past("wo_op") + k)
                        n_store = i * (16 * ln // 2) + 16 * (t // 2 + done // 2 + 1)
                        act.wait_ge(S(f"acc_store{t % 2}"), 16 * 13 if name == "yb2" else n_store)
                        act.dma_start(gate_row, chunk(gate_d, k + 8 * b)).then_inc(S(f"gate_in{t % 2}"), 16)
                        if name != "ya":
                            act.dma_start(acc_row, chunk(acc_d, k)).then_inc(S(f"acc_in{t % 2}"), 16)
                        if name == "ya":
                            act.wait_ge(step("yc_op"), past("yc_op") + k + 1)
                            act.dma_start(cols(wide, wcol(2), T), chunk(v_d, k)).then_inc(step("yc_in"), 16)
                        elif name in ("yc", "yb1"):
                            half = 0 if name == "yc" else 1
                            act.wait_ge(step(f"{nxt}_op"), past(f"{nxt}_op") + k + 1)
                            act.dma_start(cols(wide, wcol(2), T), chunk(ys_d, k + 8 * half)).then_inc(step(f"{nxt}_in"), 16)
                            if t == 0:
                                act.dma_start(cols(wide, wcol(1), T), chunk(rg_d, i + 2 * half)).then_inc(step(f"{nxt}_rg"), 16)
                        split_next(name, t, i)
                        if name == "ya":
                            act.wait_ge(step("yc_norm"), past("yc_norm") + k + 1)
                            act.activation(cols(wide, wcol(2), T), cols(wide, wcol(2), T), ACT.Silu,
                                           scale=t_sc[:, ds(k * 32 + TB_LNG, 1)],
                                           bias=t_sc[:, ds(k * 32 + TB_LNB, 1)]).then_inc(S("yc_silu"), 1)
                            act.wait_ge(S("yc_silu"), k + 1)
                            act.activation(cols(n_hi, k * T, T), cols(wide, wcol(2), T), ACT.Copy).then_inc(step("yc_hi"), 1)
                        elif name in ("yc", "yb1"):
                            act.wait_ge(step(f"{nxt}_norm"), past(f"{nxt}_norm") + k + 1)
                            hi = m_hi if name == "yc" else n_hi
                            act.activation(cols(hi, k * T, T), cols(wide, wcol(2), T), ACT.Copy).then_inc(step(f"{nxt}_hi"), 1)
                        act.wait_ge(S("acc_done"), k + done + 1)
                        if name == "yb2":
                            act.activation(cols(m_hi, k * T, T), acc_row, ACT.Copy).then_inc(step("wo_hi"), 1)
                        else:
                            store(f"acc_store{t % 2}", chunk(acc_d, k), gate_row if name == "ya" else acc_row)
                done += 8
            act.wait_ge(step("wo_op"), past("wo_op") + 9)

            n_res = [0]

            def residual(name, src_d, squares=None):
                with act.Fori(0, 4) as i:
                    for t in range(2):
                        k = i * 2 + t
                        split_next(name, t, i)
                        act.wait_ge(S(f"h_store{t}"), i * 16 + 16 * (n_res[0] // 2 + 1))
                        act.dma_start(rows[t][:, :], chunk(src_d, k)).then_inc(S(f"res_in{t}"), 16)
                        act.wait_ge(S("res_done"), k + n_res[0] + 1)
                        store(f"h_store{t}", chunk(h_d, k), rows[t][:, :])
                        if squares is not None:
                            act.wait_ge(S("sq_sum"), k + squares + 1)
                            act.activation(wide[:, wcol(1):wcol(1) + T], rows[t][:, :], ACT.Square).then_inc(S("sq_done"), 1)
                n_res[0] += 8

            def norm(n_before):
                stat(wide[:, 0:T], True)
                for t in range(2):
                    act.wait_ge(S(f"h_store{t}"), 16 * (n_res[0] // 2 + 1))
                for k in range(KD):
                    m = n_before + k
                    if k >= 2:
                        act.wait_ge(S("np_scaled"), m - 1)
                    act.dma_start(rows[k % 2][:, :], chunk(h_d, k)).then_inc(S(f"np_in{k % 2}"), 16)
                    if k:
                        norm_hi(m - 1)
                norm_hi(n_before + KD - 1)

            def norm_hi(m):
                k = m % KD
                act.wait_ge(S("np_scaled"), m + 1)
                act.activation(n_hi[:, k * T:(k + 1) * T], cols(wide, wcol(2 + k % 2), T), ACT.Copy).then_inc(S("np_hi"), 1)

            residual("wo", xt_d, 0)
            norm(0)

            f0 = 0
            for p, n in enumerate(FF_PARTS):
                with act.Fori(0, n) as i:
                    for t in range(2):
                        split_next(f"up{p}", t, i)
                        if t == 1:
                            act.wait_ge(S("ff_conv"), i * 2 + 2 * f0 + 3)
                            act.activation(cols(wide, wcol(2), T), cols(wide, wcol(2), T), ACT.Silu).then_inc(S("ff_silu"), 1)
                        wait_tile(act, i * 2 + t + first(f"up{p}"))
                        act.wait_ge(S("ff_state"), i * 2 + 2 * f0 + t + 1)
                        for src, dst in pieces(slot(f"up{p}", t), wide, wcol(t), PAD):
                            act.activation(dst, src, ACT.Copy)
                        act.wait_ge(S("ff_op"), i + f0 + 1)
                        c0 = (f0 + t * FK) * 32
                        act.activation(tile3(wide[:, wcol(2 + t):wcol(2 + t) + T]), pset(slot(f"up{p}", t)), ACT.Identity,
                                       scale=t_ff[:, ds(i * 32 + c0 + TF_TAPS + 2, 1)],
                                       bias=t_ff[:, ds(i * 32 + c0 + TF_BIAS, 1)]).then_inc(free(f"up{p}", t), 1)
                    act.wait_ge(S("ff_prod"), i + f0 + 1)
                    act.activation(cols(m_hi, i * T, T), cols(wide, wcol(2), T), ACT.Copy).then_inc(S("ff_hi"), 1)
                f0 += n
                residual(f"dn{p}", h_d, 9 if p == 2 else None)

            for c, src in enumerate(P_TOKENS):
                act.dma_start(p_tok[:, c * PLE:(c + 1) * PLE], src).then_inc(S("p_in"), 16)
            act.dma_start(gf_row[:, :], A["g_final"].rearrange("(a n) -> a n", a=1).to_broadcast([P, D]))\
                .then_inc(step("gf_in"), 16)
            norm(8)
            for c in range(9):
                act.wait_ge(S("p_ps"), c + 1)
                act.activation(p_hi[:, :].rearrange("p (k n) -> p k n", k=2)[:, :, c * P:(c + 1) * P],
                               PS[:, 6 + c % 2, 0:2 * P].rearrange("p (k n) -> p k n", k=2), ACT.Copy).then_inc(S("p_hi_done"), 1)

            def ple(i, last):
                split_next("ple", 0, i)
                act.wait_ge(S("fin_done"), i + 1)
                act.dma_start(row0[:, :], chunk(h_d, i)).then_inc(S("hf_in"), 16)
                wait_tile(act, i * 2 + first("ple"))
                act.activation(tile3(row1[:, :]), pset(slot("ple", 0)), ACT.Sigmoid).then_inc(free("ple", 0), 1)
                if not last:
                    split_next("ple", 1, i)

            with act.Fori(0, 7) as i:
                ple(i, False)
            ple(7, True)

            for c in range(9):
                act.wait_ge(S("fin_ps"), c + 1)
                act.activation(y_junk[:, :], flat(2 * (c % 2), 2), ACT.Square, accum_out=x_ms[:, c:c + 1]).then_inc(S("y_ms"), 1)
                act.wait_ge(S("y_ms"), c + 1)
                act.activation(x_ms[:, 9 + c:10 + c], x_ms[:, c:c + 1], ACT.Sqrt, bias=eps[:, 0:1], scale=1.0 / D)\
                    .then_inc(S("y_rms"), 1)
                act.wait_ge(S("y_scaled"), c + 1)
                dst = O["y_prompt"][0][c * P:(c + 1) * P, :] if c < 8 else O["y_sample"].rearrange("s t d -> (s t) d")
                act.dma_start(dst, y_tok[c % 2][:, :]).then_inc(S(f"out_y{c % 2}"), 16)
            act.wait_ge(S("out_y0"), 16 * 5)
            act.wait_ge(S("out_y1"), 16 * 4)

        @block.gpsimd
        def _(pool):
            own = Done(pool, S("pool_own"))
            pool.sem_inc(w_lo_done, 2)
            for name in ("xbc_state", "sc_state", "ff_state"):
                pool.sem_inc(S(name), 2)
            for name in ("cf_summed", "grp_sum"):
                pool.sem_inc(S(name), 1)

            def lo_next(name, t, i):
                _, _, body, qb = phases[name]
                k = qb + t + 1
                pool.wait_ge(w_hi_done, i * len(body) + k + 1)
                s = k % 2
                pool.tensor_tensor(w_lo[s][:, :], w_raw[s][:, :], w_hi[s][:, :].bitcast(F32), ALU.subtract)\
                    .then_inc(w_lo_done, 1)

            def at_register():
                pool.sem_inc(S("pool_waits"), 1)

            pool.memset(cf_stage[:, :], 0.0).then_inc(step("stage_zero"), 1)
            pool.memset(wide[:, 0:2688], 0.0).then_inc(step("stage_zero"), 1)
            pool.memset(eps[:, :], EPS).then_inc(step("eps_done"), 1)
            own.do(pool.memset(ident[:, :], 0.0))
            pool.affine_select(out=ident[:, :], in_=ident[:, :], compare_op=ALU.not_equal, fill=1.0, base=0,
                               pattern=[[-1, P]], channel_multiplier=1).then_inc(step("ident_done"), 1)
            pool.memset(ones[:, :], 1.0 / D).then_inc(step("ones_done"), 1)
            pool.wait_ge(w_hi_done, 1)
            pool.tensor_tensor(w_lo[0][:, :], w_raw[0][:, :], w_hi[0][:, :].bitcast(F32), ALU.subtract).then_inc(w_lo_done, 1)

            pool.wait_ge(S("n_ready"), 9)
            for b in range(2):
                pool.wait_ge(S(f"xt_store{b}"), 16 * (5 - b))
            pool.memset(v_in[:, :].rearrange("p (j n) -> p j n", j=KD)[:, :, 0:CPAD], 0.0).then_inc(step("v_pads"), 1)
            pool.memset(v_sum[:, :], 0.0).then_inc(step("vs_zero"), 1)
            pool.wait_ge(step("cf_state"), past("cf_state") + 1)
            with own.loop(8, 3) as i:
                for t in range(2):
                    lo_next("cf", t, i)
                old = cols(s_cf, i * 256, 256).rearrange("p (s n) -> p s n", s=NS)[:, :, 0:CPAD]
                at_register()
                own.do(pool.tensor_copy(seqs(v_in, i * CFW, CPAD, CPAD, CPAD), old))
                pool.wait_ge(ps_free[0], i + 2)
                at_register()
                own.mark(pool.tensor_copy(old, seqs(v_in, i * CFW, CPAD, CPAD - TS, CPAD)))
                own.mark(pool.tensor_copy(cols(s_cfp, i * 32, CPAD), cols(v_in, i * CFW + TP, CPAD)))
            own.wait()
            pool.sem_inc(S("cf_saved"), 1)

            pool.wait_ge(step("tables"), past("tables") + 1)
            for m in range(2):
                pool.memset(wide[:, wcol(m):wcol(m) + PAD], 0.0).then_inc(step("pads1"), 1)

            def sum_cf(c):
                pool.wait_ge(S("cf_conv"), c + 1)
                pool.tensor_tensor(v_sum[:, :], v_sum[:, :], v_acc[:, :], ALU.add).then_inc(S("cf_summed"), 1)

            with own.loop(4, 12) as i:
                for t in range(6):
                    j = i * 6 + t
                    lo_next("xbc", t, i)
                    rows_ = cols(t_xbc, j * 32 + TC_STATE, 24).rearrange("p (s n) -> p s n", s=NS)
                    pool.wait_ge(S("xbc_conv"), j + 1)
                    at_register()
                    own.mark(pool.tensor_copy(seqs(wide, wcol(t % 2), PAD, 3, 3), rows_))
                    own.wait()
                    pool.sem_inc(S("xbc_pads"), 1)
                    wait_freed(pool, "xbc", t, i)
                    at_register()
                    own.mark(pool.tensor_copy(rows_, seqs(wide, wcol(t % 2), PAD, PAD - TS, 3)))
                    pool.tensor_copy(cols(t_xbc, j * 32 + TC_PROMPT, 3), wide[:, wcol(t % 2) + TP:wcol(t % 2) + TP + 3])\
                        .then_inc(S("xbc_state"), 1)
                    if t == 5:
                        sum_cf(i)
            lo_next("dt", 0, 0)

            with own.loop(4, 4) as i:
                for t in range(6):
                    h = t // 3
                    j = i * 2 + h
                    lo_next("sc", t, i)
                    if t % 3 == 1:
                        rows_ = cols(t_sc, j * 32 + TB_STATE, 16).rearrange("p (s n) -> p s n", s=NS)
                        pool.wait_ge(S("sc_conv"), j + 1)
                        at_register()
                        own.do(pool.tensor_copy(seqs(wide, wcol(h), PAD, 2, 2), rows_))
                        pool.sem_inc(S("sc_pads"), 1)
                        wait_freed(pool, "sc", t, i)
                        at_register()
                        own.mark(pool.tensor_copy(rows_, seqs(wide, wcol(h), PAD, 2 - TS, 2)))
                        pool.tensor_copy(cols(t_sc, j * 32 + TB_PROMPT, 2), wide[:, wcol(h) + PAD + TP - 2:wcol(h) + PAD + TP])\
                            .then_inc(S("sc_state"), 1)
                    if t == 5:
                        sum_cf(i + 4)

            for h in range(2):
                pool.wait_ge(S(f"yin_store{h}"), 16 * 5)
            for m in range(2):
                own.do(pool.memset(tri[m][:, :], 1.0))
                own.do(pool.memset(after[m][:, :], 1.0))
                own.do(pool.affine_select(out=tri[m][:, :], in_=tri[m][:, :], compare_op=ALU.is_ge, fill=0.0, base=0,
                                          pattern=[[1, P]], channel_multiplier=-1))
                own.do(pool.affine_select(out=after[m][:, :], in_=after[m][:, :], compare_op=ALU.is_gt, fill=0.0, base=0,
                                          pattern=[[-1, P]], channel_multiplier=1))
                if m:
                    for w in (tri[1], after[1]):
                        own.do(pool.affine_select(out=w[:, :], in_=w[:, :], compare_op=ALU.is_ge, fill=0.0, base=0,
                                                  pattern=[[-TS, NS], [0, TS]], channel_multiplier=1))
                        own.do(pool.affine_select(out=w[:, :], in_=w[:, :], compare_op=ALU.is_ge, fill=0.0, base=TS - 1,
                                                  pattern=[[TS, NS], [0, TS]], channel_multiplier=-1))
                own.do(pool.tensor_scalar(bar[m][:, :], tri[m][:, :], 1.0, 1e30, ALU.subtract, ALU.mult))
            own.do(pool.memset(sel[:, :], 1.0))
            own.do(pool.affine_select(out=sel[:, :], in_=sel[:, :], compare_op=ALU.is_ge, fill=0.0, base=0,
                                      pattern=[[-TS, NS]], channel_multiplier=1))
            own.do(pool.affine_select(out=sel[:, :], in_=sel[:, :], compare_op=ALU.is_ge, fill=0.0, base=TS - 1,
                                      pattern=[[TS, NS]], channel_multiplier=-1))
            pool.sem_inc(step("ssd_consts"), 7)

            def decay_x(c):
                pool.wait_ge(S("blk_done"), c + 1)
                pool.wait_ge(S("xdt_done"), c + 1)
                pool.wait_ge(S("dec_done"), c + 1)
                pool.tensor_tensor(xdd[:, :].rearrange("p (h n) -> p h n", h=HEADS),
                                   xdt[:, :].rearrange("p (h n) -> p h n", h=HEADS),
                                   dec_col[:, :].unsqueeze(2).to_broadcast([P, HEADS, HD]), ALU.mult).then_inc(S("xdd_done"), 1)

            def decay_c(k, g, par, blk):
                pool.wait_ge(S("e_done"), k + 1)
                pool.wait_ge(S("ea_last_done"), k + 1)
                e = ec[par][:, :].rearrange("p (h n) -> p h n", h=HG)
                c_ = blk[:, (20 + g) * P:(21 + g) * P].unsqueeze(1).to_broadcast([P, HG, P])
                pool.tensor_tensor(e, e, c_, ALU.mult).then_inc(S("ec_done"), 1)

            with pool.Fori(0, 4) as i:
                for b in range(2):
                    c = i * 2 + b
                    decay_x(c)
                    for g in range(GROUPS):
                        decay_c(c * 4 + g, g, g % 2, xbc_blk[b])
            decay_x(8)
            for g in range(GROUPS):
                if g:
                    pool.wait_ge(S("sb_ps"), 4 * g)
                pool.wait_ge(S("btok_done"), 9)
                pool.tensor_tensor(b_msk[:, :].rearrange("p (b n) -> p b n", b=NS),
                                   b_tok[:, g * P:(g + 1) * P].unsqueeze(1).to_broadcast([P, NS, P]),
                                   sel[:, :].unsqueeze(2).to_broadcast([P, NS, P]), ALU.mult).then_inc(S("bmsk_done"), 1)
                decay_c(32 + g, g, 0, xbc_blk[0])

            with pool.Fori(0, 4) as i:
                for t in range(4):
                    j = i * 4 + t
                    lo_next("z", t, i)
                    pool.wait_ge(S("grp_sq"), j + 1)
                    dst = cols(wide, i * PADW, T)
                    at_register()
                    ins = pool.tensor_copy(dst, row1[:, :]) if t == 0 else pool.tensor_tensor(dst, dst, row1[:, :], ALU.add)
                    ins.then_inc(S("grp_sum"), 1)
                    pool.wait_ge(S("grp_sum"), j + 2)
            pool.wait_ge(S("rg_store"), 64)
            pool.memset(cols(wide, wcol(1), T), 0.0).then_inc(S("var_sum"), 1)
            with pool.Fori(0, 4) as i:
                for t in range(6):
                    lo_next("gate", t, i)
                    if t % 3 == 1:
                        k = i * 2 + t // 3
                        pool.wait_ge(S("v_sq"), k + 1)
                        pool.wait_ge(S("var_sum"), k + 1)
                        v = cols(wide, wcol(1), T)
                        pool.tensor_tensor(v, v, cols(wide, wcol(2), T), ALU.add).then_inc(S("var_sum"), 1)
            for name in ("ya", "yc", "yb1", "yb2"):
                with pool.Fori(0, phases[name][0]) as i:
                    for t in range(body_len(name)):
                        lo_next(name, t, i)

            def squares(name, before):
                pool.memset(cols(wide, 0, T), 0.0).then_inc(S("sq_sum"), 1)
                with pool.Fori(0, 4) as i:
                    for t in range(2):
                        lo_next(name, t, i)
                        k = i * 2 + t + before
                        pool.wait_ge(S("sq_done"), i * 2 + t + (before // 9) * 8 + 1)
                        pool.wait_ge(S("sq_sum"), k + 1)
                        pool.tensor_tensor(wide[:, 0:T], wide[:, 0:T], wide[:, wcol(1):wcol(1) + T], ALU.add)\
                            .then_inc(S("sq_sum"), 1)

            pool.wait_ge(S("rg_store"), 64)
            pool.wait_ge(step("wo_op"), past("wo_op") + 9)
            squares("wo", 0)
            pool.wait_ge(S("norm_op"), 8)
            for m in range(2):
                pool.memset(wide[:, wcol(m):wcol(m) + PAD], 0.0).then_inc(step("pads2"), 1)
            f0 = 0
            for p, n in enumerate(FF_PARTS):
                with own.loop(n, 4) as i:
                    for t in range(2):
                        lo_next(f"up{p}", t, i)
                        m = i * 2 + 2 * f0 + t
                        rows_ = cols(t_ff, i * 32 + (f0 + t * FK) * 32 + TF_STATE, 16).rearrange("p (s n) -> p s n", s=NS)
                        pool.wait_ge(S("ff_conv"), m + 1)
                        at_register()
                        own.do(pool.tensor_copy(seqs(wide, wcol(t), PAD, 2, 2), rows_))
                        pool.sem_inc(S("ff_pads"), 1)
                        wait_freed(pool, f"up{p}", t, i)
                        at_register()
                        own.mark(pool.tensor_copy(rows_, seqs(wide, wcol(t), PAD, 2 - TS, 2)))
                        pool.tensor_copy(cols(t_ff, i * 32 + (f0 + t * FK) * 32 + TF_PROMPT, 2),
                                         wide[:, wcol(t) + PAD + TP - 2:wcol(t) + PAD + TP]).then_inc(S("ff_state"), 1)
                f0 += n
                if p < 2:
                    with pool.Fori(0, 4) as i:
                        for t in range(2):
                            lo_next(f"dn{p}", t, i)
                else:
                    pool.wait_ge(S("ff_op"), FK + 1)
                    squares("dn2", 9)
            with pool.Fori(0, 7) as i:
                for t in range(2):
                    lo_next("ple", t, i)
            lo_next("ple", 0, 7)

        @block.vector
        def _(v):
            own = Done(v, S("dve_own"))
            for name in ("xbc_conv", "sc_conv", "ff_conv"):
                v.sem_inc(S(name), 2)
            for name in ("op_done", "ff_op", "fin_done", "y_done", "h_done"):
                v.sem_inc(S(name), 1)

            def older_taps(buf, at_, pad, acc, taps, w_col):
                out = []
                for w, shift in taps:
                    scalar = w_col(w)
                    out.append((acc[0], cols(buf, at_ + pad - shift, TP), scalar))
                    out.append((acc[1], seqs(buf, at_, pad, shift), scalar))
                return out

            def add_taps(ops, sem_=None, goes_on=False):
                for n_, (acc, src, scalar) in enumerate(ops):
                    if n_ >= 2 or goes_on:
                        own.wait(but=1)
                    ins = v.scalar_tensor_tensor(out=acc, in0=src, scalar=scalar, in1=acc, op0=ALU.mult, op1=ALU.add)
                    if sem_ is not None and n_ == len(ops) - 1:
                        ins.then_inc(S(sem_), 1)
                    else:
                        own.mark(ins)

            def low(dst, src, hi):
                return v.tensor_tensor(dst, src, hi.bitcast(F32), ALU.subtract)

            v.wait_ge(step("small_in"), past("small_in") + 80)
            for c in range(9):
                b = c % 2
                v.wait_ge(S("x_rms"), c + 1)
                own.do(v.reciprocal(x_ms[:, 18 + c:19 + c], x_ms[:, 9 + c:10 + c]))
                v.wait_ge(S(f"x_in{b}"), 16 * (c // 2 + 1))
                if c >= 2:
                    v.wait_ge(S("xnt_done"), c - 1)
                v.scalar_tensor_tensor(out=xn_tok[b][:, :], in0=x_tok[b][:, :], scalar=x_ms[:, 18 + c:19 + c],
                                       in1=g_row[:, :], op0=ALU.mult, op1=ALU.mult).then_inc(S("xn_done"), 1)
                v.wait_ge(S("nhi_done"), c + 1)
                hi, lo = (x[:, :].rearrange("p (k n) -> p k n", k=KD)[:, :, c * P:(c + 1) * P] for x in (n_hi, n_lo))
                low(lo, flat(4 * b + 2, 2).rearrange("p (k n) -> p k n", k=KD), hi).then_inc(S("n_ready"), 1)
            v.wait_ge(S("cf_state_in"), 16 * 32)
            own.mark(v.memset(s_cfp[:, :], 0.0))
            own.do(v.transpose(s_cf[:, :], cf_stage[:, :]))
            v.sem_inc(step("cf_state"), 1)

            v.wait_ge(step("v_pads"), past("v_pads") + 1)
            with v.Fori(0, 8) as i:
                wait_tile(v, 2 * i)
                v.wait_ge(ps_free[1], i + 2)
                gate = [row0[:, 0:2 * BW].rearrange("p (b n) -> p b n", b=2), row0[:, 2 * BW:TP],
                        row0[:, TP:T].rearrange("p (s n) -> p s n", n=TS)]
                for z, ((src, dst), g_) in enumerate(zip(pieces(0, v_in, i * CFW, CPAD), gate)):
                    ins = v.tensor_tensor(dst, src, g_, ALU.mult)
                ins.then_inc(ps_free[0], 1)
            v.wait_ge(S("tables_in"), 16 * 4 * len(TABLES))
            own.mark(v.transpose(t_xbc[:, :], wide[:, stage_xbc:stage_xbc + 768]))
            own.mark(v.transpose(t_cf[:, :], wide[:, stage_cf:stage_cf + 256]))
            own.mark(v.transpose(t_sc[:, :], wide[:, stage_sc:stage_sc + 256]))
            own.do(v.transpose(t_ff[:, :], wide[:, stage_ff:stage_ff + 2 * FK * 32]))
            v.sem_inc(step("tables"), 1)
            v.wait_ge(S("cf_saved"), 1)
            v.transpose(cf_new[:, 0:2048], s_cf[:, :]).then_inc(step("cf_new"), 1)
            v.transpose(cf_new[:, 2048:2304], s_cfp[:, :]).then_inc(step("cf_new"), 1)

            def cf_taps(c, t):
                if t == 0:
                    v.wait_ge(S("cf_tap"), c + 1)
                taps = [(CPAD - s_, s_) for s_ in range(5 * t + 1, 5 * t + 6)]
                add_taps(older_taps(v_in, c * CFW, CPAD, (v_acc[:, 0:TP], tail(v_acc[:, TP:T])), taps,
                                    lambda w: t_cf[:, ds(c * 32 + w, 1)]), "cf_conv" if t == 5 else None, goes_on=t > 0)

            def acc_row(m):
                return wide[:, wcol(m):wcol(m) + TP], tail(wide[:, wcol(m) + TP:wcol(m) + T])

            v.wait_ge(step("pads1"), past("pads1") + 2)
            with own.loop(4, 89) as i:
                for t in range(6):
                    j = i * 6 + t
                    wait_freed(v, "xbc", t, i)
                    v.wait_ge(S("xbc_pads"), j + 1)
                    taps = [(TC_TAPS + 3 - s_, s_) for s_ in range(1, 4)]
                    add_taps(older_taps(wide, wcol(t % 2), PAD, acc_row(2 + t % 2), taps,
                                        lambda w: t_xbc[:, ds(i * 192 + t * 32 + w, 1)]), "xbc_conv")
                    cf_taps(i, t)

            v.wait_ge(step("dt_exp"), past("dt_exp") + 1)
            h_ = slice(0, HEADS)
            own.mark(v.tensor_scalar(a_neg[h_, :], a_neg[h_, :], -1.0, None, ALU.mult))
            own.do(v.tensor_scalar(row1[h_, :], row0[h_, :], 1.0, None, ALU.add))
            v.sem_inc(step("dt_one_plus"), 1)
            v.wait_ge(S("xbc_state"), 26)
            d_, r_ = (wide[h_, wcol(m) + PAD:wcol(m) + PAD + T] for m in range(2))
            own.do(v.tensor_scalar(d_, row1[h_, :], 1.0, None, ALU.subtract))
            own.do(v.scalar_tensor_tensor(out=r_, in0=d_, scalar=0.0, in1=d_, op0=ALU.is_equal, op1=ALU.add))
            own.do(v.reciprocal(r_, r_))
            own.do(v.tensor_tensor(r_, r_, row0[h_, :], ALU.mult))
            v.wait_ge(step("dt_log"), past("dt_log") + 1)
            own.do(v.scalar_tensor_tensor(out=da_t[h_, :], in0=d_, scalar=0.0, in1=da_t[h_, :],
                                          op0=ALU.is_equal, op1=ALU.add))
            own.do(v.tensor_tensor(da_t[h_, :], da_t[h_, :], r_, ALU.mult))
            v.scalar_tensor_tensor(out=dt_t[h_, :], in0=dt_t[h_, :], scalar=0.0, in1=da_t[h_, :],
                                   op0=ALU.max, op1=ALU.add).then_inc(step("dt_done"), 1)
            v.wait_ge(step("dt_done"), past("dt_done") + 1)
            v.tensor_scalar(da_t[h_, :], dt_t[h_, :], a_neg[h_, 0:1], None, ALU.mult).then_inc(step("dt_done"), 1)

            with own.loop(4, 65) as i:
                for t in range(6):
                    h = t // 3
                    j = i * 2 + h
                    if t % 3 == 1:
                        wait_tile(v, i * 6 + t + first("sc"))
                        wait_freed(v, "sc", t - 1, i)
                        v.wait_ge(S("sc_state"), j + 1)
                        c_ = [rows[h][:, 0:2 * BW].rearrange("p (b n) -> p b n", b=2), rows[h][:, 2 * BW:TP],
                              rows[h][:, TP:T].rearrange("p (s n) -> p s n", n=TS)]
                        for (src, dst), x in zip(pieces(slot("sc", t), wide, wcol(h), PAD), c_):
                            ins = v.tensor_tensor(dst, src, x, ALU.mult)
                        ins.then_inc(free("sc", t), 1)
                    if t % 3 == 2:
                        v.wait_ge(S("sc_tap"), j + 1)
                        v.wait_ge(S("sc_pads"), j + 1)
                        taps = [(TB_TAPS + 2 - s_, s_) for s_ in range(1, 3)]
                        add_taps(older_taps(wide, wcol(h), PAD, acc_row(2 + h), taps,
                                            lambda w: t_sc[:, ds(i * 64 + h * 32 + w, 1)]), "sc_conv")
                        wait_tile(v, i * 6 + t + first("sc"))
                        v.wait_ge(S("sc_conv"), j + 3)
                        acc = tile3(wide[:, wcol(2 + h):wcol(2 + h) + T])
                        v.tensor_tensor(acc, acc, pset(slot("sc", t)), ALU.mult).then_inc(free("sc", t), 1)
                    cf_taps(i + 4, t)
            v.wait_ge(S("sc_state"), 10)
            own.mark(v.transpose(conv_new[:, 0:768], t_xbc[:, :]))
            own.do(v.transpose(conv_new[:, 768:1024], t_sc[:, :]))
            v.sem_inc(step("conv_new"), 2)

            v.wait_ge(step("dt_tok_ps"), past("dt_tok_ps") + 1)
            own.mark(v.tensor_copy(dt_tok[:, :], PS[:, 0, 0:9 * HEADS]))
            own.mark(v.tensor_copy(da_tok[:, :], PS[:, 1, 0:9 * HEADS]))
            v.wait_ge(S("cf_summed"), 9)
            own.do(v.memset(h_t[:, :], 0.0))
            v.sem_inc(step("ssd_region"), 1)
            v.sem_inc(S("blk_done"), 1)

            def by_head(x, n=HEADS):
                return x.rearrange("p (h n) -> p h n", h=n)

            def ssd_block_head(c):
                v.tensor_copy(da_cur[:, :], da_tok[:, ds(c * HEADS, HEADS)]).then_inc(S("da_cur_done"), 1)
                v.wait_ge(S("acs_ps"), c + 1)
                v.tensor_copy(acs_col[:, :], PS[:, 4, 0:HEADS]).then_inc(S("acs_done"), 1)
                v.wait_ge(S("x_ps"), c + 1)
                v.tensor_tensor(by_head(xdt[:, :]), by_head(flat(0, 4)),
                                dt_tok[:, ds(c * HEADS, HEADS)].unsqueeze(2).to_broadcast([P, HEADS, HD]), ALU.mult)\
                    .then_inc(S("xdt_done"), 1)
                v.wait_ge(S("acs_done"), c + 1)

            def exponents(sample, g, par, b0):
                for r in range(HG):
                    h = g * HG + r
                    ins = v.scalar_tensor_tensor(out=lm[par][:, r * P:(r + 1) * P],
                                                 in0=PS[:, b0 + r // 4, (r % 4) * P:(r % 4 + 1) * P],
                                                 scalar=acs_col[:, h:h + 1], in1=bar[sample][:, :],
                                                 op0=ALU.subtract, op1=ALU.min)
                ins.then_inc(S("diff_done"), 1)

            def scores(k, g, par):
                v.wait_ge(S("l_done"), k + 1)
                m = by_head(lm[par][:, :], HG)
                v.tensor_tensor(m, m, PS[:, 6, g * P:(g + 1) * P].unsqueeze(1).to_broadcast([P, HG, P]), ALU.mult)\
                    .then_inc(S("lm_done"), 1)

            def y_tokens(g, blk, bank):
                for pr in range(4):
                    j = 4 * g + pr
                    ins = v.scalar_tensor_tensor(out=y_out[g % 2][:, pr * P:(pr + 1) * P], in0=blk[:, j * P:(j + 1) * P],
                                                 scalar=d_col[:, j:j + 1], in1=PS[:, bank, pr * P:(pr + 1) * P],
                                                 op0=ALU.mult, op1=ALU.add)
                ins.then_inc(S("y_done"), 1)

            v.wait_ge(step("ssd_consts"), past("ssd_consts") + 7)
            v.wait_ge(step("small_in"), past("small_in") + 80)
            with own.loop(4, 8) as i:
                for b in range(2):
                    c = 2 * i + b

                    def front(g):
                        k = c * 4 + g
                        v.wait_ge(S("cum_ps"), k + 1)
                        v.wait_ge(S("y_ps"), k + 1)
                        v.wait_ge(S("e_done"), k + 1)
                        exponents(0, g, g % 2, 2 * (g % 2))
                        v.tensor_copy(ea_last[:, g * HG:(g + 1) * HG].unsqueeze(2), by_head(ec[g % 2][:, :], HG)[:, :, P - 1:P])\
                            .then_inc(S("ea_last_done"), 1)
                        if g == 0:
                            v.wait_ge(S("b_ps"), c + 1)
                        scores(k, g, g % 2)

                    def back(g):
                        k = c * 4 + g
                        v.wait_ge(S("y_ps"), k + 3)
                        v.wait_ge(S(f"y_store{g % 2}"), 32 * c + 16 * (g // 2 + 1))
                        y_tokens(g, xbc_blk[b], 4 + g % 2)
                        v.wait_ge(S("ea_last_done"), k + 1)
                        if g == 0:
                            v.wait_ge(S("h_done"), 4 * c + 1)
                        st = h_t[:, g * 512:(g + 1) * 512]
                        own.do(v.tensor_tensor(by_head(st, HG), by_head(st, HG),
                                               ea_last[:, g * HG:(g + 1) * HG].unsqueeze(2).to_broadcast([P, HG, HD]), ALU.mult))
                        v.wait_ge(S("h_ps"), k + 1)
                        v.tensor_tensor(st, st, PS[:, 7, :], ALU.add).then_inc(S("h_done"), 1)

                    ssd_block_head(c)
                    front(0)
                    for g in range(GROUPS):
                        if g + 1 < GROUPS:
                            front(g + 1)
                        back(g)
                    v.wait_ge(S("h_done"), 4 * c + 5)
                    v.sem_inc(S("blk_done"), 1)
            v.sem_inc(S("ea_last_done"), 4)
            ssd_block_head(8)
            for g in range(GROUPS):
                v.wait_ge(S("cum_ps"), 33 + g)
                if g:
                    v.wait_ge(S("ys_ps"), 4 * g)
                v.wait_ge(S("e_done"), 33 + g)
                exponents(1, g, 0, 0)
                v.wait_ge(S("b_ps"), 9)
                scores(32 + g, g, 0)
                for pr in range(4):
                    j = 4 * g + pr
                    v.wait_ge(S("sb_ps"), j + 1)
                    v.wait_ge(S(f"s_in_sem{j % 2}"), 16 * (j // 2 + 1))
                    v.wait_ge(step("ea_done"), past("ea_done") + 1)
                    if j >= 2:
                        v.wait_ge(S(f"out_ssm_s{j % 2}"), 16 * (j // 2))
                    for s_ in range(NS):
                        ins = v.scalar_tensor_tensor(out=s_out[j % 2][:, s_ * P:(s_ + 1) * P],
                                                     in0=s_in[j % 2][:, s_ * P:(s_ + 1) * P],
                                                     scalar=ea_seq[:, j * NS + s_:j * NS + s_ + 1],
                                                     in1=PS[:, 4 + s_ // 4, (s_ % 4) * P:(s_ % 4 + 1) * P],
                                                     op0=ALU.mult, op1=ALU.add)
                    ins.then_inc(S("sout_done"), 1)
                v.wait_ge(S("ys_ps"), 4 * g + 4)
                v.wait_ge(S(f"y_store{g % 2}"), 16 * (17 + g // 2))
                y_tokens(g, xbc_blk[0], 7)

            with v.Fori(0, 4) as i:
                for t in range(4):
                    j = i * 4 + t
                    v.wait_ge(S("y_in"), j * 16 + 16)
                    wait_freed(v, "z", t, i)
                    v.tensor_tensor(row0[:, :], row0[:, :], row1[:, :], ALU.mult).then_inc(S("ys_done"), 1)

            def wrow(m):
                return wide[:, wcol(m):wcol(m) + T]

            for g in range(GROUPS):
                v.wait_ge(S("stat_out"), 3 * g + 3)
                v.reciprocal(wrow(g), wrow(g)).then_inc(step("rstd_done"), 1)

            v.wait_ge(S("stat_out"), 15)
            with v.Fori(0, 4) as i:
                for h in range(2):
                    k = i * 2 + h
                    v.wait_ge(S("v_in_sem"), k * 16 + 16)
                    v.tensor_tensor(wrow(2), wrow(2), wrow(0), ALU.subtract).then_inc(S("v_cent"), 1)
                    v.wait_ge(step("ya_hi"), past("ya_hi") + k + 1)
                    low(cols(m_lo, k * T, T), wrow(3), cols(m_hi, k * T, T)).then_inc(step("ya_op"), 1)
            v.wait_ge(S("stat_out"), 18)
            own.do(v.reciprocal(wrow(1), wrow(1)))

            done = 0
            for name, nxt in (("ya", "yc"), ("yc", "yb1"), ("yb1", "yb2"), ("yb2", "wo")):
                n, _, body, _ = phases[name]
                ln = len(body)
                with own.loop(n, ln if name == "ya" else 0) as i:
                    for t in range(ln):
                        k = i * ln + t
                        if name == "ya":
                            v.wait_ge(step("yc_in"), past("yc_in") + k * 16 + 16)
                            own.do(v.tensor_tensor(wrow(2), wrow(2), wrow(0), ALU.subtract))
                            v.tensor_tensor(wrow(2), wrow(2), wrow(1), ALU.mult).then_inc(step("yc_norm"), 1)
                        elif name != "yb2":
                            half = 0 if name == "yc" else 1
                            v.wait_ge(step(f"{nxt}_in"), past(f"{nxt}_in") + k * 16 + 16)
                            v.wait_ge(step(f"{nxt}_rg"), past(f"{nxt}_rg") + i * 16 + 16)
                            v.scalar_tensor_tensor(out=wrow(2), in0=wrow(2), scalar=t_sc[:, ds(k * 32 + TB_NORM + half, 1)],
                                                   in1=wrow(1), op0=ALU.mult, op1=ALU.mult).then_inc(step(f"{nxt}_norm"), 1)
                        if name != "yb2":
                            hi, lo = (m_hi, m_lo) if name == "yc" else (n_hi, n_lo)
                            v.wait_ge(step(f"{nxt}_hi"), past(f"{nxt}_hi") + k + 1)
                            low(cols(lo, k * T, T), wrow(2), cols(hi, k * T, T)).then_inc(step(f"{nxt}_op"), 1)
                        if name == "ya":
                            gate_row = rows[t % 2][:, :]
                        else:
                            gate_row, acc = (row0[:, :], row1[:, :]) if t % 2 == 0 else (wrow(3), wrow(0))
                        wait_tile(v, k + first(name))
                        v.wait_ge(S(f"gate_in{t % 2}"), i * (8 * ln) + 16 * (t // 2 + done // 2 + 1))
                        v.tensor_tensor(tile3(gate_row), tile3(gate_row), pset(slot(name, t)), ALU.mult)\
                            .then_inc(free(name, t), 1)
                        wait_freed(v, name, t, i)
                        if name == "ya":
                            v.sem_inc(S("acc_done"), 1)
                        else:
                            v.wait_ge(S(f"acc_in{t % 2}"), i * (8 * ln) + 16 * (t // 2 + done // 2 - 3))
                            v.tensor_tensor(acc, gate_row, acc, ALU.add).then_inc(S("acc_done"), 1)
                        if name == "yb2":
                            v.wait_ge(step("wo_hi"), past("wo_hi") + k + 1)
                            low(cols(m_lo, k * T, T), acc, cols(m_hi, k * T, T)).then_inc(step("wo_op"), 1)
                done += 8

            n_res = [0]

            def residual(name):
                with v.Fori(0, 4) as i:
                    for t in range(2):
                        wait_tile(v, i * 2 + t + first(name))
                        v.wait_ge(S(f"res_in{t}"), i * 16 + 16 * (n_res[0] // 2 + 1))
                        v.tensor_tensor(tile3(rows[t][:, :]), tile3(rows[t][:, :]), pset(slot(name, t)), ALU.add)\
                            .then_inc(free(name, t), 1)
                        wait_freed(v, name, t, i)
                        v.sem_inc(S("res_done"), 1)
                n_res[0] += 8

            def norm(before, n_stat, gain):
                v.wait_ge(S("stat_out"), 3 * n_stat + 3)
                own.do(v.reciprocal(wrow(0), wrow(0)))

                def norm_lo(k):
                    v.wait_ge(S("np_hi"), before + k + 1)
                    low(n_lo[:, k * T:(k + 1) * T], wrow(2 + k % 2), n_hi[:, k * T:(k + 1) * T]).then_inc(S("norm_op"), 1)

                for k in range(KD):
                    if k >= 2:
                        v.wait_ge(S("norm_op"), before + k - 1)
                    v.wait_ge(S(f"np_in{k % 2}"), 16 * ((before + k) // 2 + 1))
                    v.scalar_tensor_tensor(out=wrow(2 + k % 2), in0=rows[k % 2][:, :],
                                           scalar=t_sc[:, k * 32 + gain:k * 32 + gain + 1], in1=wrow(0),
                                           op0=ALU.mult, op1=ALU.mult).then_inc(S("np_scaled"), 1)
                    if k:
                        norm_lo(k - 1)
                norm_lo(KD - 1)

            residual("wo")
            norm(0, 6, TB_GFFN)

            v.wait_ge(step("pads2"), past("pads2") + 2)
            f0 = 0
            for p, n in enumerate(FF_PARTS):
                with own.loop(n, 6) as i:
                    for t in range(2):
                        m = i * 2 + 2 * f0 + t
                        c0 = (f0 + t * FK) * 32
                        wait_freed(v, f"up{p}", t, i)
                        v.wait_ge(S("ff_pads"), m + 1)
                        taps = [(TF_TAPS + 2 - s_, s_) for s_ in range(1, 3)]
                        add_taps(older_taps(wide, wcol(t), PAD, acc_row(2 + t), taps,
                                            lambda w: t_ff[:, ds(i * 32 + c0 + w, 1)]), "ff_conv")
                    v.wait_ge(S("ff_silu"), i + f0 + 1)
                    v.wait_ge(S("ff_conv"), i * 2 + 2 * f0 + 4)
                    v.tensor_tensor(wrow(2), wrow(2), wrow(3), ALU.mult).then_inc(S("ff_prod"), 1)
                    v.wait_ge(S("ff_hi"), i + f0 + 1)
                    low(cols(m_lo, i * T, T), wrow(2), cols(m_hi, i * T, T)).then_inc(S("ff_op"), 1)
                f0 += n
                if p == 2:
                    v.wait_ge(S("ff_state"), 2 + 2 * FK)
                    v.wait_ge(S("ff_op"), FK + 1)
                    v.transpose(ff_new[:, :], t_ff[:, :]).then_inc(step("ff_new"), 1)
                residual(f"dn{p}")

            v.wait_ge(step("ff_new_out"), past("ff_new_out") + 16 * 8)
            norm(8, 7, TB_GPLE)
            for c in range(9):
                v.wait_ge(S("p_hi_done"), c + 1)
                hi, lo = (x[:, :].rearrange("p (k n) -> p k n", k=2)[:, :, c * P:(c + 1) * P] for x in (p_hi, p_lo))
                low(lo, PS[:, 6 + c % 2, 0:2 * P].rearrange("p (k n) -> p k n", k=2), hi).then_inc(S("p_op"), 1)
            with v.Fori(0, 8) as i:
                wait_tile(v, i * 2 + 1 + first("ple"))
                wait_freed(v, "ple", 0, i)
                v.tensor_tensor(tile3(row1[:, :]), tile3(row1[:, :]), pset(slot("ple", 1)), ALU.mult)\
                    .then_inc(free("ple", 1), 1)
                wait_freed(v, "ple", 1, i)
                v.wait_ge(S("hf_in"), i * 16 + 16)
                v.tensor_tensor(cols(h_fin, i * T, T), row0[:, :], row1[:, :], ALU.add).then_inc(S("fin_done"), 1)

            v.wait_ge(step("gf_in"), past("gf_in") + 16)
            for c in range(9):
                v.wait_ge(S("y_rms"), c + 1)
                own.do(v.reciprocal(x_ms[:, 18 + c:19 + c], x_ms[:, 9 + c:10 + c]))
                if c >= 2:
                    v.wait_ge(S(f"out_y{c % 2}"), 16 * (c // 2))
                v.scalar_tensor_tensor(out=y_tok[c % 2][:, :], in0=flat(2 * (c % 2), 2), scalar=x_ms[:, 18 + c:19 + c],
                                       in1=gf_row[:, :], op0=ALU.mult, op1=ALU.mult).then_inc(S("y_scaled"), 1)


OUTPUTS = {"y_prompt": (1, TP, D), "y_sample": (NS, TS, D),
           "sc_p": (1, 1, 2, D), "xbc_p": (1, 1, 3, XBC), "ssm_p": (1, 1, HEADS, HD, NST), "cf_p": (1, 1, CPAD, D),
           "ff_p": (1, 1, 2, 2 * FF),
           "sc_s": (1, NS, 2, D), "xbc_s": (1, NS, 3, XBC), "ssm_s": (1, NS, HEADS, HD, NST), "cf_s": (1, NS, CPAD, D),
           "ff_s": (1, NS, 2, 2 * FF)}


def kernel(**inputs):
    import numpy as np
    import concourse.bacc as bacc
    from concourse.bass_utils import run_bass_kernel_spmd

    nc = bacc.Bacc("TRN2", target_bir_lowering=False, num_devices=1)
    arrays, A, O = {}, {}, {}
    for name, x in inputs.items():
        arrays[f"in_{name}"] = np.ascontiguousarray(x)
        A[name] = nc.dram_tensor(f"in_{name}", x.shape, F32, kind="ExternalInput").ap()
    for name, shape in OUTPUTS.items():
        O[name] = nc.dram_tensor(f"out_{name}", shape, F32, kind="ExternalOutput").ap()
    build(nc, A, O)
    r = run_bass_kernel_spmd(nc, [arrays], core_ids=[0])
    return tuple(r.results[0][f"out_{name}"] for name in OUTPUTS)
```

```python
from contextlib import ExitStack, contextmanager

import concourse.bass as bass
from concourse import mybir

F32 = mybir.dt.float32
F32R = mybir.dt.float32r
ALU = mybir.AluOpType
ACT = mybir.ActivationFunctionType
ds = bass.ds

P = 128
D = 1024
TP = 1024
NS, TS = 8, 16
T = TP + NS * TS
NB, BW = 3, T // 3
KD = D // P
HEADS, HD, GROUPS, NST = 32, 64, 4, 128
HG = HEADS // GROUPS
INNER = HEADS * HD
XBC = INNER + 2 * GROUPS * NST
FF = 2816
FK = FF // P
PLE = 256
EPS = 1e-6
OFF_SC = 3 * D
OFF_Z = OFF_SC + 3 * D
OFF_XBC = OFF_Z + INNER
OFF_DT = OFF_XBC + XBC
OFF_CF = OFF_DT + HEADS
PAD = 3
SEG = PAD + TS
PADW = PAD + TP + NS * SEG + 2
CK = 31
CPAD = CK - 1
CSEG = CPAD + TS
CFW = CPAD + TP + NS * CSEG
FF_PARTS = (8, 8, 6)

TB_STATE, TB_TAPS, TB_LNG, TB_LNB, TB_GFFN, TB_GPLE, TB_NORM, TB_PROMPT = 0, 16, 19, 20, 21, 22, 23, 25
TC_STATE, TC_TAPS, TC_BIAS, TC_PROMPT = 0, 24, 28, 29
TF_STATE, TF_TAPS, TF_BIAS, TF_PROMPT = 0, 16, 19, 20

STEPS = {
    "pool_steps": (("stage_zero", 2), ("eps_done", 1), ("ident_done", 1), ("ones_done", 1), ("v_pads", 1), ("vs_zero", 1), ("acc_zero", 1), ("pads1", 2), ("ssd_consts", 7), ("pads2", 2)),
    "dve_steps": (("cf_state", 1), ("tables", 1), ("cf_new", 2), ("dt_one_plus", 1), ("dt_done", 2), ("conv_new", 2), ("ssd_region", 1), ("rstd_done", 5), ("ff_new", 1)),
    "pe_steps": (("dt_tok_ps", 1), ("hout_ps", 1), ("ea_ps", 1)),
    "act_steps": (("dt_exp", 1), ("dt_log", 1), ("hout_done", 1), ("ea_done", 1)),
    "once_in": (("small_in", 80), ("vs_store", 16), ("out_ssm_p", 16), ("vs_in", 16), ("gf_in", 16)),
    "states_out": (("cf_new_out", 576), ("conv_new_out", 256), ("ff_new_out", 128)),
    "op_in": (("ya_in", 128), ("yc_in", 128), ("yb1_in", 128), ("yb2_in", 128)),
    "op_rg": (("yb1_rg", 32), ("yb2_rg", 32)),
    "op_norm": (("yc_norm", 8), ("yb1_norm", 8), ("yb2_norm", 8)),
    "op_hi": (("ya_hi", 8), ("yc_hi", 8), ("yb1_hi", 8), ("yb2_hi", 8), ("wo_hi", 8)),
    "op_done": (("ya_op", 8), ("yc_op", 8), ("yb1_op", 8), ("yb2_op", 8), ("wo_op", 8)),
}


def gemm_phases():
    out = []
    out.append(("cf", 8, "N", [("w_in", 0, 8, OFF_CF + D, P), ("w_in", 0, 8, OFF_CF, P)]))
    out.append(("xbc", 2, "N", [("w_in", 0, 8, OFF_XBC + t * P, 12 * P) for t in range(12)]))
    out.append(("dt", 1, "N", [("w_in", 0, 8, OFF_DT, 0)]))
    sc = []
    for h in range(4):
        for part in (1, 2, 0):
            sc.append(("w_in", 0, 8, OFF_SC + part * D + h * P, 4 * P))
    out.append(("sc", 2, "N", sc))
    for half in range(2):
        out.append((f"side{half}", 4, "N", [("w_in", 0, 8, half * D + t * P, 2 * P) for t in range(2)]))
    out.append(("z", 4, "N", [("w_in", 0, 8, OFF_Z + t * P, 4 * P) for t in range(4)]))
    out.append(("gate", 4, "N", [("w_in", 0, 8, 2 * D + t * P, 2 * P) for t in range(2)]))
    out.append(("ya", 4, "M", [("w_sc_out", 0, 8, t * P, 2 * P) for t in range(2)]))
    out.append(("yc", 2, "N", [("w_cf_out", 0, 8, t * P, 4 * P) for t in range(4)]))
    out.append(("yb1", 2, "M", [("w_ssm_out", 0, 8, t * P, 4 * P) for t in range(4)]))
    out.append(("yb2", 4, "N", [("w_ssm_out", 8, 8, t * P, 2 * P) for t in range(2)]))
    out.append(("wo", 4, "M", [("w_o", 0, 8, t * P, 2 * P) for t in range(2)]))
    first = 0
    for p, n in enumerate(FF_PARTS):
        out.append((f"up{p}", n, "N", [("w_up", 0, 8, (first + a * FK) * P, P) for a in range(2)]))
        out.append((f"dn{p}", 4, "M", [("w_down", first, n, t * P, 2 * P) for t in range(2)]))
        first += n
    out.append(("ple", 8, "N", [("w_ple_gate", 0, 8, 0, P), ("w_ple_proj", 0, 2, 0, P)]))
    return out


def shared(name):
    for sem, steps in STEPS.items():
        count = 0
        for step, adds in steps:
            if step == name:
                return sem, count
            count += adds
    raise KeyError(name)


def past(name):
    return shared(name)[1]


class Done:

    def __init__(self, eng, sem):
        self.eng, self.sem, self.n, self.i, self.per = eng, sem, 0, None, 0

    def mark(self, ins):
        ins.then_inc(self.sem, 1)
        self.n += 1

    def wait(self, but=0):
        v = self.n - but
        self.eng.wait_ge(self.sem, v if self.i is None else self.i * self.per + v)

    def do(self, ins):
        self.mark(ins)
        self.wait()

    @contextmanager
    def loop(self, n, per):
        first = self.n
        with self.eng.Fori(0, n) as i:
            self.i, self.per = i, per
            yield i
            assert self.n - first == per, f"{self.n - first} instructions in an iteration"
        self.i, self.n = None, first + n * per


def cols(t, base, n):
    return t[:, ds(base, n)]


def seqs(t, base, pad, shift=0, n=TS):
    seg = pad + TS
    return cols(t, base + pad + TP, NS * seg).rearrange("p (s n) -> p s n", s=NS)[:, :, pad - shift:pad - shift + n]


def tile3(ap):
    return ap.rearrange("p (b n) -> p b n", b=NB)


def tail(ap):
    return ap.rearrange("p (s n) -> p s n", n=TS)


def build(nc, A, O):
    with ExitStack() as ctx:
        sems = {}

        def S(name):
            if name not in sems:
                sems[name] = ctx.enter_context(nc.semaphore(name))
            return sems[name]

        def step(name):
            return S(shared(name)[0])

        base = (nc.sbuf_base + 63) // 64 * 64
        top = [base]

        def at(name, shape, dt, offset):
            return nc.alloc_sbuf_tensor_at(name, shape, dt, offset=offset)

        def take(name, cols_, dt=F32):
            off = top[0]
            top[0] += -(-cols_ * 4 // 32) * 32
            assert top[0] <= nc.sbuf_usable_end, (name, top[0])
            return at(name, [P, cols_], dt, off), off

        n_hi, _ = take("n_hi", KD * T, F32R)
        n_lo, n_lo_at = take("n_lo", KD * T, F32R)
        m_hi, m_at = take("m_hi", KD * T, F32R)
        m_lo, m_lo_at = take("m_lo", KD * T, F32R)
        w_raw = [take(f"w_raw{s}", KD * P)[0] for s in range(2)]
        w_hi = [take(f"w_hi{s}", KD * P, F32R)[0] for s in range(2)]
        w_lo = [take(f"w_lo{s}", KD * P, F32R)[0] for s in range(2)]
        t_cf, _ = take("t_cf", KD * 32)
        t_sc, _ = take("t_sc", KD * 32)
        t_xbc, _ = take("t_xbc", XBC // P * 32)
        t_ff, _ = take("t_ff", 2 * FK * 32)
        wide, wide_at = take("wide", 4 * PADW)
        row0, row0_at = take("row0", T)
        row1, _ = take("row1", T)
        ident, _ = take("ident", P)
        ones, _ = take("ones", P)
        d_col, _ = take("d_col", INNER // P)
        eps, _ = take("eps", 1)
        dtb, _ = take("dtb", 1)
        a_neg, _ = take("a_neg", 1)
        rows = [row0, row1]

        def wcol(k):
            return k * PADW

        v_in = at("v_in", [P, KD * CFW], F32, m_at)
        s_cf = at("s_cf", [P, KD * NS * 32], F32, m_at + KD * CFW * 4)
        s_cfp = at("s_cfp", [P, KD * 32], F32, m_at + KD * CFW * 4 + 8192)
        v_acc = [at(f"v_acc{b}", [P, T], F32, m_at + KD * CFW * 4 + (9216, 0)[b]) for b in range(2)]
        v_sum = at("v_sum", [P, T], F32, m_at + KD * CFW * 4 + 9216 + 4608)
        dt_t = at("dt_t", [P, T], F32, m_at + KD * CFW * 4 + 9216 + 2 * 4608)
        da_t = at("da_t", [P, T], F32, m_at + KD * CFW * 4 + 9216 + 3 * 4608)
        assert KD * CFW * 4 + 9216 + 4 * 4608 <= KD * T * 8
        x_tok = at("x_tok", [P, 9 * D], F32, m_at)
        xn_tok = [at(f"xn_tok{b}", [P, D], F32, m_at + 4096 * (9 + b)) for b in range(2)]
        xt_out = [at(f"xt_out{b}", [P, D], F32, m_at + 54784 + 4096 * b) for b in range(2)]
        g_row = at("g_row", [P, D], F32, m_at + 54784 + 4096 * 2)
        x_junk = at("x_junk", [P, D], F32, m_at + 54784 + 4096 * 3)
        x_ms = at("x_ms", [P, 32], F32, m_at + 54784 + 4096 * 4)
        X_LOADS = ((0, 1), (1, 4), (4, 8), (8, 9))

        def x_arrived(eng, c):
            eng.wait_ge(S(f"x_in{sum(c >= lo for lo, _ in X_LOADS) - 1}"), 16)
        xbc_blk = [at(f"xbc_blk{b}", [P, 24 * P], F32, m_at + 12288 * b) for b in range(2)]
        xdt = at("xdt", [P, INNER], F32, m_at + 24576)
        xdd = at("xdd", [P, INNER], F32, m_at + 32768)
        b_tok = at("b_tok", [P, GROUPS * NST], F32, m_at + 40960)
        h_t = at("h_t", [P, INNER], F32, m_at + 43008)
        y_out = [at(f"y_out{b}", [P, 4 * P], F32, m_at + 51200 + 2048 * b) for b in range(2)]
        lm = [at(f"lm{b}", [P, HG * P], F32, m_at + 55296 + 4096 * b) for b in range(2)]
        ec = [at(f"ec{b}", [P, HG * P], F32, m_at + 63488 + 4096 * b) for b in range(2)]
        off = [wide_at]

        def small(name, n):
            t = at(name, [P, n], F32, off[0])
            off[0] += -(-n * 4 // 32) * 32
            assert off[0] <= wide_at + 16 * PADW
            return t

        tri = [small(f"tri{m}", P) for m in range(2)]
        after = [small(f"after{m}", P) for m in range(2)]
        bar = [small(f"bar{m}", P) for m in range(2)]
        sel = small("sel", NS)
        dt_tok = small("dt_tok", 9 * HEADS)
        da_tok = small("da_tok", 9 * HEADS)
        da_cur = small("da_cur", HEADS)
        acs_col = small("acs_col", HEADS)
        dec_col = small("dec_col", HEADS)
        ea_last = small("ea_last", HEADS)
        ea_seq = small("ea_seq", 16 * NS)
        b_msk = small("b_msk", NS * NST)
        s_in = [at(f"s_in{b}", [P, NS * NST], F32, row0_at + 4096 * b) for b in range(2)]
        s_t = at("s_t", [P, NS * NST], F32, m_at + 43008)
        h_out = at("h_out", [P, INNER], F32, m_at + 12288)
        s_out = [at(f"s_out{b}", [P, NS * NST], F32, m_at + (20480, 59392)[b]) for b in range(2)]
        side_row = at("side_row", [P, T], F32, wide_at + 10560)
        assert off[0] <= wide_at + 10560, off[0] - wide_at
        p_hi = at("p_hi", [P, 2 * T], F32R, m_at)
        p_lo = at("p_lo", [P, 2 * T], F32R, m_at + 9216)
        p_tok = at("p_tok", [P, 9 * PLE], F32, n_lo_at)
        y_ms = at("y_ms", [P, 32], F32, m_at + 32768)
        h_fin = at("h_fin", [P, KD * T], F32, m_lo_at)
        y_tok = [at(f"y_tok{b}", [P, D], F32, m_at + 4096 * b) for b in range(4)]
        gf_row = at("gf_row", [P, D], F32, m_at + 18432 + 8192)
        y_junk = at("y_junk", [P, D], F32, wide_at)

        PS = ctx.enter_context(nc.psum_tensor("PS", [P, 8, 512], F32))

        def pset(s, n=P):
            return PS[0:n, 3 * s:3 * s + 3, 0:BW]

        def flat(b0, nb):
            return PS[:, b0:b0 + nb, :].rearrange("p b n -> p (b n)")

        def pieces(s, buf, at_, pad):
            two = PS[:, 3 * s:3 * s + 2, 0:BW]
            return [(two, cols(buf, at_ + pad, 2 * BW).rearrange("p (b n) -> p b n", b=2)),
                    (PS[:, 3 * s + 2, 0:TP - 2 * BW], cols(buf, at_ + pad + 2 * BW, TP - 2 * BW)),
                    (PS[:, 3 * s + 2, TP - 2 * BW:BW].rearrange("p (s n) -> p s n", n=TS), seqs(buf, at_, pad))]

        def scratch(name, rows_, n=T):
            return nc.dram_tensor(name, (rows_, n), F32, kind="Internal").ap()

        xt_d = scratch("xt_d", D)
        xbc_d = scratch("xbc_d", XBC)
        yin_d = scratch("yin_d", D)
        v_d = scratch("v_d", P + D)
        vs_d = scratch("vs_d", P)
        y_d = scratch("y_d", INNER)
        ys_d = scratch("ys_d", INNER)
        rg_d = scratch("rg_d", (GROUPS + 1) * P)
        gate_d = scratch("gate_d", 3 * D)
        acc_d = scratch("acc_d", D)
        h_d = scratch("h_d", D)

        def chunk(t, j):
            return t[ds(j * P, P), :]

        W = {n: A[n][0].rearrange("(k p) n -> p k n", p=P) for n in
             ("w_in", "w_sc_out", "w_cf_out", "w_ssm_out", "w_o", "w_up", "w_down", "w_ple_gate", "w_ple_proj")}
        phases, q = {}, 0
        for name, n, operand, body in gemm_phases():
            phases[name] = (n, operand, body, q)
            q += n * len(body)
        n_tiles = q

        def first(name):
            return phases[name][3]

        def body_len(name):
            return len(phases[name][2])

        w_loaded = [S("w_loaded0"), S("w_loaded1")]
        w_hi_done = S("w_hi_done")
        w_lo_done = S("w_lo_done")
        tile_done = S("tile_done")
        ps_free = [S("ps_free0"), S("ps_free1")]

        def wait_tile(eng, q):
            eng.wait_ge(tile_done, q + 2)

        def freed(name, t):
            qb = first(name) + t
            return qb % 2, qb // 2 + 2, body_len(name) // 2

        def wait_freed(eng, name, t, i):
            s, b, per = freed(name, t)
            eng.wait_ge(ps_free[s], i * per + b)

        def free(name, t):
            return ps_free[(first(name) + t) % 2]

        def last_free(name, s):
            end = first(name) + phases[name][0] * body_len(name)
            return (end + 1 - s) // 2 + 1

        def slot(name, t):
            return (first(name) + t) % 2

        SIDE_BANK = 5
        block = ctx.enter_context(nc.Block())
        P_TOKENS = [A["p_prompt"][0, 0][c * P:(c + 1) * P, :] for c in range(8)] + \
            [A["p_sample"][0].rearrange("s t d -> (s t) d")]

        stage_cf, stage_sc, stage_xbc, stage_ff = 0, 256, 512, 512 + 768

        def one(x):
            return x.rearrange("(a n) -> a n", a=1)

        norm_rows = A["ssm_norm_g"][0].rearrange("(a n) -> a n", a=2)
        TABLES = [
            (stage_xbc, 24, A["ssm_conv_w"][0], TC_TAPS), (stage_xbc, 24, one(A["ssm_conv_b"][0]), TC_BIAS),
            (stage_xbc, 24, A["state_ssm_conv"][0].rearrange("s r c -> (s r) c"), TC_STATE),
            (stage_cf, 8, A["cf_conv_w"][0], 0), (stage_cf, 8, one(A["cf_conv_b"][0]), CK),
            (stage_sc, 8, A["state_short_conv"][0].rearrange("s r c -> (s r) c"), TB_STATE),
            (stage_sc, 8, A["sc_conv_w"][0], TB_TAPS), (stage_sc, 8, one(A["cf_ln_g"][0]), TB_LNG),
            (stage_sc, 8, one(A["cf_ln_b"][0]), TB_LNB), (stage_sc, 8, one(A["g_ffn"][0]), TB_GFFN),
            (stage_sc, 8, one(A["g_ple"][0]), TB_GPLE), (stage_sc, 8, norm_rows, TB_NORM),
            (stage_ff, 44, A["state_ffn_conv"][0].rearrange("s r c -> (s r) c"), TF_STATE),
            (stage_ff, 44, A["ff_conv_w"][0], TF_TAPS), (stage_ff, 44, one(A["ff_conv_b"][0]), TF_BIAS),
        ]

        cf_new = at("cf_new", [P, 2304], F32, row0_at)
        conv_new = at("conv_new", [P, 1024], F32, row0_at)
        ff_new = wide[:, 2 * PADW:2 * PADW + 2 * FK * 32]
        cf_stage = at("cf_stage", [P, KD * NS * 32], F32, row0_at)

        @block.sync
        def _(sp):
            def load_w(name, t, i):
                n, _, body, qb = phases[name]
                weight, k0, nk, col, step = body[t]
                s = slot(name, t)
                sp.wait_ge(w_lo_done, i * len(body) + qb + t + 1)
                src = W[weight][:, k0:k0 + nk, ds(i * step + col, P)]
                sp.dma_start(w_raw[s][:, 0:nk * P].rearrange("p (k n) -> p k n", k=nk), src).then_inc(w_loaded[s], 16)

            for t in range(2):
                load_w("cf", t, 0)
            sp.wait_ge(step("stage_zero"), past("stage_zero") + 2)
            for b in range(NS):
                src = A["state_cf_conv"][0, b].rearrange("r (j q c) -> r j q c", q=4, c=32)
                for qd in range(4):
                    dst = cf_stage[32 * qd:32 * qd + CPAD, :].rearrange("r (j s c) -> r j s c", j=KD, s=NS)[:, :, b, :]
                    sp.dma_start(dst, src[:, :, qd, :]).then_inc(S("cf_state_in"), 16)
            for stage, n_, src, r0 in TABLES:
                r = src.shape[0]
                src_q = src.rearrange("r (j q c) -> r j q c", q=4, c=32)
                for qd in range(4):
                    dst = wide[32 * qd + r0:32 * qd + r0 + r, stage:stage + n_ * 32].rearrange("r (j c) -> r j c", c=32)
                    sp.dma_start(dst, src_q[:, :, qd, :]).then_inc(S("tables_in"), 16)

            def save_rows(sem_, stage, n_, r0, dst):
                r = dst.shape[0]
                for qd in range(4):
                    sp.dma_start(dst.rearrange("r (j q c) -> r j q c", q=4, c=32)[:, :, qd, :],
                                 stage[32 * qd + r0:32 * qd + r0 + r, 0:n_ * 32].rearrange("r (j c) -> r j c", c=32))\
                        .then_inc(step(sem_), 16)

            def after_loads(name):
                if name == "xbc0":
                    sp.wait_ge(step("cf_new"), past("cf_new") + 2)
                if name[:3] == "xbc" and name != "xbc3":
                    z = int(name[3])
                    for b in range(3 * z, min(3 * z + 3, NS)):
                        dst = O["cf_s"][0, b].rearrange("r (j q c) -> r j q c", q=4, c=32)
                        for qd in range(4):
                            src = cf_new[32 * qd:32 * qd + CPAD, 0:2048].rearrange("r (j s c) -> r j s c", j=KD, s=NS)
                            sp.dma_start(dst[:, :, qd, :], src[:, :, b, :]).then_inc(step("cf_new_out"), 16)
                if name == "xbc2":
                    save_rows("cf_new_out", cf_new[:, 2048:2304], KD, 0, O["cf_p"][0, 0])
                if name == "side0":
                    sp.wait_ge(step("conv_new"), past("conv_new") + 2)
                    save_rows("conv_new_out", conv_new[:, 0:768], 24, TC_STATE, O["xbc_s"][0].rearrange("s r c -> (s r) c"))
                    save_rows("conv_new_out", conv_new[:, 0:768], 24, TC_PROMPT, O["xbc_p"][0, 0])
                    save_rows("conv_new_out", conv_new[:, 768:1024], KD, TB_STATE, O["sc_s"][0].rearrange("s r c -> (s r) c"))
                    save_rows("conv_new_out", conv_new[:, 768:1024], KD, TB_PROMPT, O["sc_p"][0, 0])
                if name == "dn2":
                    sp.wait_ge(step("ff_new"), past("ff_new") + 1)
                    save_rows("ff_new_out", ff_new, 2 * FK, TF_STATE, O["ff_s"][0].rearrange("s r c -> (s r) c"))
                    save_rows("ff_new_out", ff_new, 2 * FK, TF_PROMPT, O["ff_p"][0, 0])

            for name, (n, operand, body, qb) in phases.items():
                if n == 1:
                    load_w(name, 0, 0)
                    continue
                if name == "xbc":
                    for z in range(n):
                        for t in range(len(body)):
                            load_w(name, t, z)
                            if t % 6 == 5:
                                after_loads(f"xbc{2 * z + t // 6}")
                    continue
                with sp.Fori(1 if name == "cf" else 0, n) as i:
                    for t in range(len(body)):
                        load_w(name, t, i)
                after_loads(name)
            sp.wait_ge(step("cf_new_out"), past("cf_new_out") + 16 * 36)
            sp.wait_ge(step("conv_new_out"), past("conv_new_out") + 16 * 16)
            sp.wait_ge(step("ff_new_out"), past("ff_new_out") + 16 * 8)

        @block.tensor
        def _(pe):
            pe.sem_inc(tile_done, 1)
            pe.sem_inc(S("y_ps"), 2)

            def operand_count(name):
                if name in ("ya", "yc", "yb1", "yb2", "wo"):
                    return step(f"{name}_op"), past(f"{name}_op") + 1
                if name.startswith("dn"):
                    return S("ff_op"), sum(FF_PARTS[:int(name[2])]) + 1
                return None, 0

            def tile(name, t, i):
                split, before = operand_count(name)
                n, operand, body, qb = phases[name]
                nk = body[t][2]
                s = slot(name, t)
                x_hi, x_lo = (p_hi, p_lo) if body[t][0] == "w_ple_proj" else (n_hi, n_lo) if operand == "N" else (m_hi, m_lo)
                pe.wait_ge(w_lo_done, i * len(body) + qb + t + 3)
                fs, fb, per = freed(name, t)
                pe.wait_ge(ps_free[fs], i * per + fb - 1)
                for k in range(nk):
                    if name in ("up0", "ple") and t == 0:
                        pe.wait_ge(S(f"norm_op{k % 2}"), (0 if name == "up0" else KD // 2) + k // 2 + 1)
                    if split is not None and t == 0:
                        pe.wait_ge(split, before + k + 1)
                    w_h, w_l = (x[:, k * P:(k + 1) * P] for x in (w_hi[s], w_lo[s]))
                    for w, x, z in ((w_h, x_hi, 0), (w_h, x_lo, 1), (w_l, x_hi, 2)):
                        for b in range(NB):
                            at_ = k * T + b * BW
                            last = pe.matmul(PS[:, 3 * s + b, 0:BW], w, x[:, at_:at_ + BW],
                                             start=(k == 0 and z == 0), stop=(k == nk - 1 and z == 2))
                last.then_inc(tile_done, 1)

            def side_unit(name, t, i, u):
                _, _, body, qb = phases[name]
                s = slot(name, t)
                if u == 0:
                    pe.wait_ge(w_lo_done, i * 2 + qb + t + 3)
                    fs, fb, per = freed(name, 1 - t)
                    pe.wait_ge(ps_free[fs], i * per + fb - (per if t == 0 else 0))
                else:
                    pe.wait_ge(S("side_out"), i * 4 + (8 if name == "side1" else 0) * 2 + 2 * t + u)
                for k in range(KD):
                    w_h, w_l = (x[:, k * P:(k + 1) * P] for x in (w_hi[s], w_lo[s]))
                    for w, x, z in ((w_h, n_hi, 0), (w_h, n_lo, 1), (w_l, n_hi, 2)):
                        at_ = k * T + u * BW
                        last = pe.matmul(PS[:, SIDE_BANK, 0:BW], w, x[:, at_:at_ + BW],
                                         start=(k == 0 and z == 0), stop=(k == KD - 1 and z == 2))
                last.then_inc(tile_done if u == 2 else S("side_ps"), 1)

            def product(name):
                n, operand, body, qb = phases[name]
                if n == 1:
                    tile(name, 0, 0)
                    return
                with pe.Fori(0, n) as i:
                    for t in range(len(body)):
                        tile(name, t, i)

            pe.wait_ge(step("ident_done"), past("ident_done") + 1)
            for c in range(9):
                b = c % 2
                if c >= 2:
                    pe.wait_ge(S("xt_evac"), c - 1)
                    pe.wait_ge(S("n_ready"), c - 1)
                x_arrived(pe, c)
                for k in range(KD):
                    last = pe.transpose(PS[:, 4 * b + k // 4, (k % 4) * P:(k % 4 + 1) * P],
                                        x_tok[:, c * D + k * P:c * D + (k + 1) * P], ident[:, :])
                last.then_inc(S("xt_done"), 1)
                pe.wait_ge(S("xn_done"), c + 1)
                for k in range(KD):
                    last = pe.transpose(PS[:, 4 * b + 2 + k // 4, (k % 4) * P:(k % 4 + 1) * P],
                                        xn_tok[b][:, k * P:(k + 1) * P], ident[:, :])
                last.then_inc(S("xnt_done"), 1)
            pe.wait_ge(S("n_ready"), 9)
            pe.wait_ge(S("xt_evac"), 9)
            product("cf")
            product("xbc")
            product("dt")
            product("sc")

            for s in range(2):
                pe.wait_ge(ps_free[s], last_free("sc", s))
            pe.wait_ge(step("ssd_consts"), past("ssd_consts") + 7)
            pe.wait_ge(step("dt_done"), past("dt_done") + 2)
            for m, src in enumerate((dt_t, da_t)):
                for c in range(9):
                    last = pe.transpose(PS[:, m, c * HEADS:(c + 1) * HEADS], src[0:HEADS, c * P:(c + 1) * P],
                                        ident[0:HEADS, 0:HEADS])
            last.then_inc(step("dt_tok_ps"), 1)

            def block_head(sample, c, b):
                blk = xbc_blk[b]
                pe.wait_ge(S(f"blk_in{b}"), 8 * (c - b) + 16)
                pe.wait_ge(S("blk_done"), c + 1)
                pe.wait_ge(S("da_cur_done"), c + 1)
                for m, w in enumerate((tri[sample], after[sample])):
                    last = pe.matmul(PS[:, 4, m * HEADS:(m + 1) * HEADS], w[:, :], da_cur[:, :], start=True, stop=True)
                last.then_inc(S("acs_ps"), 1)
                for g in range(GROUPS):
                    last = pe.transpose(PS[:, 7, g * P:(g + 1) * P], blk[:, (16 + g) * P:(17 + g) * P], ident[:, :])
                for g in range(GROUPS):
                    last = pe.matmul(PS[:, 6, g * P:(g + 1) * P], blk[:, (16 + g) * P:(17 + g) * P],
                                     blk[:, (20 + g) * P:(21 + g) * P], start=True, stop=True)
                last.then_inc(S("b_ps"), 1)
                for j in range(16):
                    last = pe.transpose(PS[:, j // 4, (j % 4) * P:(j % 4 + 1) * P], blk[:, j * P:(j + 1) * P], ident[:, :])
                last.then_inc(S("x_ps"), 1)

            def cum_rows(sample, g, b0):
                for r in range(HG):
                    h = g * HG + r
                    last = pe.matmul(PS[:, b0 + r // 4, (r % 4) * P:(r % 4 + 1) * P],
                                     da_cur[:, h:h + 1].to_broadcast([P, P]), tri[sample][:, :], start=True, stop=True)
                last.then_inc(S("cum_ps"), 1)

            def prompt_block(i, b):
                c = 2 * i + b
                block_head(0, c, b)
                side_unit("side0", b, i, 0)
                pe.wait_ge(S("xdt_done"), c + 1)
                for g in range(2):
                    cum_rows(0, g, 2 * g)
                side_unit("side0", b, i, 1)
                for g in range(GROUPS):
                    pe.wait_ge(S("ec_done"), c * 4 + g + 1)
                    pe.wait_ge(S("lm_done"), c * 4 + g + 1)
                    if g == 0:
                        pe.wait_ge(S("acs_done"), c + 1)
                        pe.wait_ge(S("dec_done"), c + 1)
                        pe.wait_ge(S("btok_done"), c + 1)
                    pe.wait_ge(S("y_done"), c * 4 + g + 1)
                    for r in range(HG):
                        h = g * HG + r
                        o = PS[64 * (r % 2):64 * (r % 2) + 64, 4, (r // 2) * P:(r // 2 + 1) * P]
                        pe.matmul(o, xdt[:, h * HD:(h + 1) * HD], lm[g % 2][:, r * P:(r + 1) * P], start=True, stop=False)
                        last = pe.matmul(o, h_t[:, h * HD:(h + 1) * HD], ec[g % 2][:, r * P:(r + 1) * P],
                                         start=False, stop=True)
                    last.then_inc(S("y_ps"), 1)
                    if g + 2 < GROUPS:
                        cum_rows(0, g + 2, 2 * (g % 2))
                    pe.wait_ge(S("xdd_done"), c + 1)
                    pe.wait_ge(S("h_done"), c * 4 + g + 1)
                    pe.matmul(PS[:, 7, :], b_tok[:, g * P:(g + 1) * P], xdd[:, g * 512:(g + 1) * 512],
                              start=True, stop=True).then_inc(S("h_ps"), 1)
                side_unit("side0", b, i, 2)

            with pe.Fori(0, 4) as i:
                for b in range(2):
                    prompt_block(i, b)
            pe.wait_ge(S("h_done"), 33)
            pe.wait_ge(S("y_done"), 33)
            for j in range(16):
                last = pe.transpose(PS[:, j // 4, (j % 4) * P:(j % 4 + 1) * P], h_t[:, j * P:(j + 1) * P], ident[:, :])
            last.then_inc(step("hout_ps"), 1)
            pe.wait_ge(step("hout_done"), past("hout_done") + 1)

            block_head(1, 8, 0)
            pe.wait_ge(S("xdt_done"), 9)
            pe.wait_ge(S("btok_done"), 9)
            for h in range(HEADS):
                r = h % 2
                last = pe.matmul(PS[64 * r:64 * r + 64, 7, h // 2 * NS:(h // 2 + 1) * NS],
                                 da_cur[:, h:h + 1].to_broadcast([P, HD]), sel[:, :], start=True, stop=True)
            last.then_inc(step("ea_ps"), 1)
            for g in range(GROUPS):
                if g:
                    pe.wait_ge(S("lm_done"), 32 + g)
                    pe.wait_ge(S("ec_done"), 32 + g)
                    pe.wait_ge(S("sout_done"), 4 * g)
                cum_rows(1, g, 0)
                for u in range(2):
                    side_unit("side1", 0, g, u)
                pe.wait_ge(S("lm_done"), 33 + g)
                pe.wait_ge(S("ec_done"), 33 + g)
                if g == 0:
                    pe.wait_ge(step("ea_done"), past("ea_done") + 1)
                else:
                    pe.wait_ge(S("y_done"), 33 + g)
                for r in range(HG):
                    h = g * HG + r
                    o = PS[64 * (r % 2):64 * (r % 2) + 64, 7, (r // 2) * P:(r // 2 + 1) * P]
                    last = pe.matmul(o, xdt[:, h * HD:(h + 1) * HD], lm[0][:, r * P:(r + 1) * P],
                                     start=(r < 2), stop=True, skip_group_check=True)
                for pr in range(4):
                    j = 4 * g + pr
                    pe.wait_ge(S(f"s_in_sem{j % 2}"), 16 * (j // 2 + 1))
                    if j:
                        pe.wait_ge(S("st_done"), j)
                    for b in range(NS):
                        last = pe.transpose(PS[:, 2 + b // 4, (b % 4) * P:(b % 4 + 1) * P],
                                            s_in[j % 2][:, b * P:(b + 1) * P], ident[:, :])
                    last.then_inc(S("st_ps"), 1)
                    if pr == 0:
                        pe.wait_ge(S("bmsk_done"), g + 1)
                    if j == 0:
                        pe.wait_ge(S("xdd_done"), 9)
                        pe.wait_ge(S("btok_done"), 9)
                    if j:
                        pe.wait_ge(S("sout_done"), j)
                    for z in range(2):
                        last = pe.matmul(PS[:, z, :], xdd[:, j * P:(j + 1) * P], b_msk[:, z * 512:(z + 1) * 512],
                                         start=True, stop=True)
                    last.then_inc(S("sb_ps"), 1)
                    side_unit("side1", (pr + 2) // 3, g, (pr + 2) % 3)
                    pe.wait_ge(S("st_done"), j + 1)
                    for r in range(2):
                        for b in range(NS):
                            o = PS[64 * r:64 * r + 64, 7, pr * P + b * TS:pr * P + (b + 1) * TS]
                            e = (2 * pr + r) * P + b * TS
                            last = pe.matmul(o, s_t[:, b * P + r * HD:b * P + (r + 1) * HD], ec[0][:, e:e + TS],
                                             start=False, stop=True, skip_group_check=True)
                    last.then_inc(S("ys_ps"), 1)
            pe.wait_ge(S("y_done"), 37)
            pe.wait_ge(S("sout_done"), 16)
            for s in range(2):
                pe.wait_ge(ps_free[s], last_free("side1", s))

            def stat(src, n):
                for b in range(NB):
                    pe.wait_ge(S("stat_out"), 3 * n + (2, 1, 3)[b])
                    pe.matmul(PS[:, 6 + b % 2, 0:BW], ones[:, :], src[:, b * BW:(b + 1) * BW],
                              start=True, stop=True).then_inc(S("stat_ps"), 1)

            def wrow(m):
                return wide[:, wcol(m):wcol(m) + T]

            with pe.Fori(0, 4) as i:
                for t in range(4):
                    tile("z", t, i)
                    if t == 0:
                        pe.wait_ge(S("grp_sum"), i * 4 + 1)
                        stat(wrow(0), i)
            pe.wait_ge(step("vs_in"), past("vs_in") + 16)
            stat(wrow(3), 4)
            pe.wait_ge(S("grp_sum"), 17)
            stat(wrow(0), 5)
            product("gate")
            pe.wait_ge(S("var_sum"), 9)
            stat(wrow(1), 6)
            for name in ("ya", "yc", "yb1", "yb2", "wo"):
                product(name)
            pe.wait_ge(S("sq_sum"), 9)
            stat(wrow(0), 7)
            for p, n in enumerate(FF_PARTS):
                product(f"up{p}")
                product(f"dn{p}")
            pe.wait_ge(S("p_in"), 16 * 9)
            pe.wait_ge(S("stat_out"), 3 * 8 + 2)
            for c in range(9):
                if c >= 2:
                    pe.wait_ge(S("p_op"), c - 1)
                for k in range(2):
                    last = pe.transpose(PS[:, 6 + c % 2, k * P:(k + 1) * P],
                                        p_tok[:, c * PLE + k * P:c * PLE + (k + 1) * P], ident[:, :])
                last.then_inc(S("p_ps"), 1)
            pe.wait_ge(S("p_op"), 9)
            pe.wait_ge(S("sq_sum"), 18)
            stat(wrow(0), 8)
            product("ple")
            pe.wait_ge(S("fin_done"), 9)
            for c in range(9):
                b = c % 4
                if c >= 4:
                    pe.wait_ge(S("y_scaled"), c - 3)
                for k in range(KD):
                    last = pe.transpose(PS[:, 2 * b + k // 4, (k % 4) * P:(k % 4 + 1) * P],
                                        h_fin[:, k * T + c * P:k * T + (c + 1) * P], ident[:, :])
                last.then_inc(S("fin_ps"), 1)

        @block.scalar
        def _(act):
            own = Done(act, S("act_own"))
            for s in range(2):
                act.sem_inc(ps_free[s], 1)
            for name in ("v_store", "xbc_store0", "xbc_store1", "yin_store0", "yin_store1", "gate_store0",
                         "gate_store1", "ys_store", "side_store", "rg_store", "y_store0", "y_store1", "acc_store0", "acc_store1", "h_store0", "h_store1"):
                act.sem_inc(S(name), 16)

            def split_after(name, t, i):
                n, _, body, qb = phases[name]
                ln, k = len(body), qb + t + 2
                act.wait_ge(tile_done, i * ln + k)
                act.wait_ge(w_loaded[k % 2], i * (8 * ln) + 16 * (k // 2 + 1))
                act.activation(w_hi[k % 2][:, :], w_raw[k % 2][:, :], ACT.Copy).then_inc(w_hi_done, 1)

            def store(name, dst, src):
                act.dma_start(dst, src).then_inc(S(name), 16)

            act.dma_start(g_row[:, :], A["g_mix"][0].rearrange("(a n) -> a n", a=1).to_broadcast([P, D]))\
                .then_inc(step("small_in"), 16)
            act.dma_start(dtb[0:HEADS, :], A["ssm_dt_bias"][0].rearrange("(n a) -> n a", a=1)).then_inc(step("small_in"), 16)
            act.dma_start(a_neg[0:HEADS, :], A["ssm_a_log"][0].rearrange("(n a) -> n a", a=1)).then_inc(step("small_in"), 16)
            for r in range(2):
                src = A["ssm_d"][0].rearrange("(a j r) -> a r j", a=1, r=2)[:, r, :]
                act.dma_start(d_col[64 * r:64 * r + 64, :], src.to_broadcast([64, 16]),
                              allow_slow_non_contiguous=True).then_inc(step("small_in"), 16)
            for z, (lo, hi) in enumerate(X_LOADS):
                src = A["x_sample"].rearrange("s t d -> (s t) d").unsqueeze(1) if lo == 8 else \
                    A["x_prompt"][0][lo * P:hi * P, :].rearrange("(c p) d -> p c d", p=P)
                act.dma_start(x_tok[:, lo * D:hi * D].rearrange("p (c d) -> p c d", d=D), src).then_inc(S(f"x_in{z}"), 16)
            for s in range(2):
                act.wait_ge(w_loaded[s], 16)
                act.activation(w_hi[s][:, :], w_raw[s][:, :], ACT.Copy).then_inc(w_hi_done, 1)
            act.wait_ge(step("eps_done"), past("eps_done") + 1)

            def x_square(c):
                x_arrived(act, c)
                own.do(act.activation(x_junk[:, :], x_tok[:, c * D:(c + 1) * D], ACT.Square, accum_out=x_ms[:, c:c + 1]))
                act.activation(x_ms[:, 9 + c:10 + c], x_ms[:, c:c + 1], ACT.Sqrt, bias=eps[:, 0:1], scale=1.0 / D)\
                    .then_inc(S("x_rms"), 1)

            def x_out(c):
                b = c % 2
                act.wait_ge(S("xt_done"), c + 1)
                if c >= 2:
                    act.wait_ge(S(f"xt_store{b}"), 16 * (c // 2))
                act.activation(xt_out[b][:, :], flat(4 * b, 2), ACT.Copy).then_inc(S("xt_evac"), 1)
                act.wait_ge(S("xt_evac"), c + 1)
                dst = xt_d.rearrange("(k p) n -> p k n", p=P)[:, :, c * P:(c + 1) * P]
                act.dma_start(dst, xt_out[b][:, :].rearrange("p (k n) -> p k n", k=KD)).then_inc(S(f"xt_store{b}"), 16)
                act.wait_ge(S("xnt_done"), c + 1)
                act.activation(n_hi[:, :].rearrange("p (k n) -> p k n", k=KD)[:, :, c * P:(c + 1) * P],
                               flat(4 * b + 2, 2).rearrange("p (k n) -> p k n", k=KD), ACT.Copy).then_inc(S("nhi_done"), 1)

            x_square(0)
            x_square(1)
            for c in range(9):
                x_out(c)
                if c + 2 < 9:
                    x_square(c + 2)

            act.wait_ge(step("cf_state"), past("cf_state") + 1)
            act.wait_ge(S("n_ready"), 9)
            with act.Fori(0, 8) as i:
                split_after("cf", 0, i)
                act.wait_ge(ps_free[1], i + 1)
                act.activation(tile3(row0[:, :]), pset(0), ACT.Sigmoid).then_inc(ps_free[0], 1)
                split_after("cf", 1, i)

            def cf_tap(c, par):
                act.wait_ge(S("v_store"), c * 16 + 16)
                act.wait_ge(S("cf_summed"), c + 1)
                w = t_cf[:, ds(c * 32 + CK - 1, 1)]
                bias = t_cf[:, ds(c * 32 + CK, 1)]
                act.activation(v_acc[par][:, 0:TP], cols(v_in, c * CFW + CPAD, TP), ACT.Identity, bias=bias, scale=w)
                act.activation(tail(v_acc[par][:, TP:T]), seqs(v_in, c * CFW, CPAD), ACT.Identity, bias=bias, scale=w)\
                    .then_inc(S("cf_tap"), 1)

            def cf_out(c, par):
                act.wait_ge(S("cf_conv"), c + 1)
                store("v_store", chunk(v_d, c), v_acc[par][:, :])

            act.wait_ge(step("cf_new"), past("cf_new") + 2)
            act.wait_ge(step("acc_zero"), past("acc_zero") + 1)
            with act.Fori(0, 2) as i:
                for t in range(12):
                    j = i * 12 + t
                    par = t // 6
                    if t % 6 == 0:
                        cf_tap(2 * i + par, par)
                    split_after("xbc", t, i)
                    pad, acc = wcol(t % 2), wcol(2 + t % 2)
                    act.wait_ge(S("xbc_state"), j + 1)
                    for src, dst in pieces(slot("xbc", t), wide, pad, PAD):
                        act.activation(dst, src, ACT.Copy)
                    act.wait_ge(S(f"xbc_store{t % 2}"), i * 96 + 16 * (t // 2 + 1))
                    act.activation(tile3(wide[:, acc:acc + T]), pset(slot("xbc", t)), ACT.Identity,
                                   scale=t_xbc[:, ds(i * 384 + t * 32 + TC_TAPS + 3, 1)],
                                   bias=t_xbc[:, ds(i * 384 + t * 32 + TC_BIAS, 1)]).then_inc(free("xbc", t), 1)
                    act.wait_ge(S("xbc_conv"), j + 3)
                    act.activation(wide[:, acc:acc + T], wide[:, acc:acc + T], ACT.Silu).then_inc(S("xbc_silu"), 1)
                    act.wait_ge(S("xbc_silu"), j + 1)
                    store(f"xbc_store{t % 2}", chunk(xbc_d, j), wide[:, acc:acc + T])
                    if t % 6 == 2:
                        cf_out(2 * i + par, 1 - par)

            split_after("dt", 0, 0)
            x_ = tile3(dt_t[0:HEADS, :])
            act.activation(x_, pset(slot("dt", 0), HEADS), ACT.Identity, bias=dtb[0:HEADS, :]).then_inc(free("dt", 0), 1)
            wait_freed(act, "dt", 0, 0)
            act.wait_ge(step("cf_new_out"), past("cf_new_out") + 16 * 36)
            own.do(act.activation(row0[0:HEADS, :], dt_t[0:HEADS, :], ACT.Abs))
            own.do(act.activation(row0[0:HEADS, :], row0[0:HEADS, :], ACT.Exp, scale=-1.0))
            act.activation(a_neg[0:HEADS, :], a_neg[0:HEADS, :], ACT.Exp).then_inc(step("dt_exp"), 1)
            act.wait_ge(step("dt_one_plus"), past("dt_one_plus") + 1)
            act.activation(da_t[0:HEADS, :], row1[0:HEADS, :], ACT.Ln).then_inc(step("dt_log"), 1)

            with act.Fori(0, 2) as i:
                for t in range(12):
                    par = t // 6
                    h4 = t // 3
                    h = h4 % 2
                    if t % 6 == 0:
                        cf_tap(2 * i + 4 + par, par)
                    if t % 3 == 0:
                        split_after("sc", t, i)
                        s_, b_, per_ = freed("sc", t + 1)
                        act.wait_ge(ps_free[s_], i * per_ + b_ - 3)
                        if t == 0:
                            act.wait_ge(step("dt_done"), past("dt_done") + 2)
                        act.activation(tile3(rows[h][:, :]), pset(slot("sc", t)), ACT.Copy).then_inc(free("sc", t), 1)
                    elif t % 3 == 1:
                        split_after("sc", t, i)
                        wait_freed(act, "sc", t, i)
                        acc = wcol(2 + h)
                        act.wait_ge(S(f"xbc_store{h}"), 16 * 13)
                        act.wait_ge(S(f"yin_store{h}"), i * 32 + 16 * (h4 // 2 + 1))
                        w = t_sc[:, ds(i * 128 + h4 * 32 + TB_TAPS + 2, 1)]
                        act.activation(wide[:, acc:acc + TP], wide[:, wcol(h) + PAD:wcol(h) + PAD + TP],
                                       ACT.Identity, scale=w)
                        act.activation(tail(wide[:, acc + TP:acc + T]), seqs(wide, wcol(h), PAD), ACT.Identity, scale=w)\
                            .then_inc(S("sc_tap"), 1)
                    else:
                        split_after("sc", t, i)
                        wait_freed(act, "sc", t, i)
                        acc = wcol(2 + h)
                        store(f"yin_store{h}", chunk(yin_d, i * 4 + h4), wide[:, acc:acc + T])
                    if t % 6 == 2:
                        cf_out(2 * i + 4 + par, 1 - par)

            def load_block(c, b):
                src = xbc_d.rearrange("(k p) n -> p k n", p=P)[:, :, ds(c * P, P)]
                act.dma_start(xbc_blk[b][:, :].rearrange("p (k n) -> p k n", k=24), src).then_inc(S(f"blk_in{b}"), 16)

            def y_rows(c, g):
                return y_d.rearrange("(k p) n -> p k n", p=P)[:, 4 * g:4 * g + 4, ds(c * P, P)]

            def side_out(name, t, i, u):
                chunks = 8 if name == "side1" else 0
                if u < 2:
                    act.wait_ge(S("side_ps"), i * 4 + 2 * (chunks + t) + u + 1)
                else:
                    wait_tile(act, i * 2 + t + first(name))
                if u == 0:
                    act.wait_ge(S("side_store"), i * 32 + 16 * (chunks + t + 1))
                act.activation(side_row[:, u * BW:(u + 1) * BW], PS[:, SIDE_BANK, 0:BW], ACT.Copy)\
                    .then_inc(free(name, t) if u == 2 else S("side_out"), 1)
                if u == 2:
                    split_after(name, t, i)
                    wait_freed(act, name, t, i)
                    store("side_store", chunk(gate_d, i * 2 + t + chunks), side_row[:, :])

            def ssd_head(c):
                act.wait_ge(S("acs_ps"), c + 1)
                act.wait_ge(S("blk_done"), c + 1)
                act.wait_ge(S("acs_done"), c + 1)
                act.activation(dec_col[:, :], PS[:, 4, HEADS:2 * HEADS], ACT.Exp).then_inc(S("dec_done"), 1)
                act.wait_ge(S("b_ps"), c + 1)
                act.activation(b_tok[:, :], PS[:, 7, :], ACT.Copy).then_inc(S("btok_done"), 1)

            def exp_rows(k, par):
                act.wait_ge(S("cum_ps"), k + 1)
                act.wait_ge(S("y_ps"), k + 1)
                act.activation(ec[par][:, :], flat(2 * par, 2), ACT.Exp).then_inc(S("e_done"), 1)

            def exp_diffs(k, par):
                act.wait_ge(S("diff_done"), k + 1)
                act.activation(lm[par][:, :], lm[par][:, :], ACT.Exp).then_inc(S("l_done"), 1)

            act.wait_ge(S("cf_conv"), 5)
            act.wait_ge(S("xbc_store0"), 16 * 13)
            act.wait_ge(S("xbc_store1"), 16 * 13)
            load_block(0, 0)
            cf_out(8, 1)
            act.wait_ge(S("cf_summed"), 10)
            act.dma_start(vs_d[:, :], v_sum[:, :]).then_inc(step("vs_store"), 16)
            act.wait_ge(S("v_store"), 16 * 10)
            act.wait_ge(step("vs_store"), past("vs_store") + 16)
            act.wait_ge(step("ssd_region"), past("ssd_region") + 1)
            with act.Fori(0, 4) as i:
                for b in range(2):
                    c = i * 2 + b
                    act.wait_ge(S("blk_done"), c + 1)
                    act.wait_ge(S("y_done"), c * 4 + 1)
                    load_block(c + 1, 1 - b)
                    ssd_head(c)
                    side_out("side0", b, i, 0)
                    for g in range(2):
                        exp_rows(c * 4 + g, g)
                    for g in range(2):
                        exp_diffs(c * 4 + g, g)
                    side_out("side0", b, i, 1)
                    for g in range(GROUPS):
                        act.wait_ge(S("y_done"), c * 4 + g + 2)
                        store(f"y_store{g % 2}", y_rows(c, g), y_out[g % 2][:, :].rearrange("p (j n) -> p j n", j=4))
                        if g + 2 < GROUPS:
                            exp_rows(c * 4 + g + 2, g % 2)
                            exp_diffs(c * 4 + g + 2, g % 2)
                    side_out("side0", b, i, 2)
            act.wait_ge(step("hout_ps"), past("hout_ps") + 1)
            act.activation(h_out[:, :], flat(0, 4), ACT.Copy).then_inc(step("hout_done"), 1)
            act.wait_ge(step("hout_done"), past("hout_done") + 1)
            act.dma_start(O["ssm_p"][0, 0].rearrange("(j r) p n -> (r p) j n", r=2),
                          h_out[:, :].rearrange("p (j n) -> p j n", j=16)).then_inc(step("out_ssm_p"), 16)
            act.wait_ge(step("out_ssm_p"), past("out_ssm_p") + 16)
            states = A["state_ssm"][0].rearrange("b (j r) p n -> j (r p) b n", r=2)
            new_states = O["ssm_s"][0].rearrange("b (j r) p n -> j (r p) b n", r=2)

            def load_state(j):
                act.dma_start(s_in[j % 2][:, :].rearrange("p (b n) -> p b n", b=NS), states[j])\
                    .then_inc(S(f"s_in_sem{j % 2}"), 16)

            act.wait_ge(step("conv_new_out"), past("conv_new_out") + 16 * 16)
            load_state(0)
            load_state(1)
            ssd_head(8)
            act.wait_ge(step("ea_ps"), past("ea_ps") + 1)
            act.activation(ea_seq[:, :], PS[:, 7, 0:P], ACT.Exp).then_inc(step("ea_done"), 1)
            for g in range(GROUPS):
                k = 32 + g
                act.wait_ge(S("cum_ps"), k + 1)
                if g:
                    act.wait_ge(S("ys_ps"), 4 * g)
                else:
                    act.wait_ge(S("y_ps"), 34)
                act.activation(ec[0][:, :], flat(0, 2), ACT.Exp).then_inc(S("e_done"), 1)
                act.wait_ge(S("diff_done"), k + 1)
                act.activation(lm[0][:, :], lm[0][:, :], ACT.Exp).then_inc(S("l_done"), 1)
                for u in range(2):
                    side_out("side1", 0, g, u)
                for pr in range(4):
                    j = 4 * g + pr
                    act.wait_ge(S("st_ps"), j + 1)
                    if j:
                        act.wait_ge(S("ys_ps"), j)
                    act.activation(s_t[:, :], flat(2, 2), ACT.Copy).then_inc(S("st_done"), 1)
                    side_out("side1", (pr + 2) // 3, g, (pr + 2) % 3)
                    act.wait_ge(S("sout_done"), j + 1)
                    act.dma_start(new_states[j], s_out[j % 2][:, :].rearrange("p (b n) -> p b n", b=NS))\
                        .then_inc(S(f"out_ssm_s{j % 2}"), 16)
                    if j + 2 < 16:
                        load_state(j + 2)
                act.wait_ge(S("y_done"), 34 + g)
                store(f"y_store{g % 2}", y_rows(8, g), y_out[g % 2][:, :].rearrange("p (j n) -> p j n", j=4))
            act.wait_ge(S("y_store0"), 16 * 19)
            act.wait_ge(S("y_store1"), 16 * 19)

            for b in range(2):
                act.wait_ge(S(f"out_ssm_s{b}"), 16 * 8)
            act.wait_ge(S("side_store"), 16 * 17)
            act.dma_start(wide[:, wcol(3):wcol(3) + T], vs_d[:, :]).then_inc(step("vs_in"), 16)

            def stat(dst, n, rstd=True, scale=1.0):
                for b in range(NB):
                    act.wait_ge(S("stat_ps"), 3 * n + b + 1)
                    o = dst[:, b * BW:(b + 1) * BW]
                    if rstd:
                        act.activation(o, PS[:, 6 + b % 2, 0:BW], ACT.Sqrt, bias=eps[:, 0:1], scale=scale)\
                            .then_inc(S("stat_out"), 1)
                    else:
                        act.activation(o, PS[:, 6 + b % 2, 0:BW], ACT.Copy).then_inc(S("stat_out"), 1)

            def wrow(m):
                return wide[:, wcol(m):wcol(m) + T]

            def group_rstd(g):
                act.wait_ge(step("rstd_done"), past("rstd_done") + g + 1)
                store("rg_store", chunk(rg_d, g), wrow(1))

            GROUP_SCALE = float(D) / (INNER // GROUPS)
            with act.Fori(0, 4) as i:
                for t in range(4):
                    j = i * 4 + t
                    act.wait_ge(S("ys_store"), j * 16 + 16)
                    act.wait_ge(S("grp_sum"), j + 1)
                    act.dma_start(row0[:, :], chunk(y_d, j)).then_inc(S("y_in"), 16)
                    if t == 0:
                        act.wait_ge(S("rg_store"), i * 16 + 16)
                        stat(wrow(1), i, scale=GROUP_SCALE)
                    split_after("z", t, i)
                    if t == 2:
                        group_rstd(i)
                    act.activation(tile3(row1[:, :]), pset(slot("z", t)), ACT.Silu).then_inc(free("z", t), 1)
                    act.wait_ge(S("ys_done"), j + 1)
                    store("ys_store", chunk(ys_d, j), row0[:, :])
                    act.activation(row1[:, :], row0[:, :], ACT.Square).then_inc(S("grp_sq"), 1)
            stat(wrow(3), 4, rstd=False)
            act.wait_ge(S("rg_store"), 16 * 5)
            stat(wrow(1), 5, scale=GROUP_SCALE)
            group_rstd(4)
            act.wait_ge(S("ys_store"), 16 * 17)
            act.wait_ge(S("grp_sum"), 17)

            with act.Fori(0, 4) as i:
                for t in range(2):
                    k = i * 2 + t
                    act.wait_ge(S("var_sum"), k + 1)
                    act.dma_start(wrow(2), chunk(v_d, k + 1)).then_inc(S("v_in_sem"), 16)
                    act.wait_ge(step("ya_op"), past("ya_op") + k + 1)
                    act.dma_start(wrow(0), chunk(yin_d, k)).then_inc(step("ya_in"), 16)
                    act.wait_ge(step("ya_in"), past("ya_in") + k * 16 + 16)
                    act.activation(cols(m_hi, k * T, T), wrow(0), ACT.Copy).then_inc(step("ya_hi"), 1)
                    act.wait_ge(S("v_cent"), k + 1)
                    act.activation(wrow(2), wrow(2), ACT.Square).then_inc(S("v_sq"), 1)
                    split_after("gate", t, i)
                    act.wait_ge(S(f"gate_store{t}"), i * 16 + 16)
                    act.activation(tile3(rows[t][:, :]), pset(slot("gate", t)), ACT.Copy).then_inc(free("gate", t), 1)
                    wait_freed(act, "gate", t, i)
                    store(f"gate_store{t}", chunk(gate_d, k + 16), rows[t][:, :])
            act.wait_ge(S("var_sum"), 9)
            stat(wrow(1), 6)
            for s in range(2):
                act.wait_ge(S(f"gate_store{s}"), 16 * 5)

            def sum_rows(name, t):
                if name == "ya":
                    return rows[t % 2][:, :], None
                return (row0[:, :], row1[:, :]) if t % 2 == 0 else (cols(wide, wcol(3), T), cols(wide, wcol(0), T))

            done = 0
            for b, name, nxt, op in ((0, "ya", "yc", "ya_op"), (2, "yc", "yb1", "yc_op"),
                                     (1, "yb1", "yb2", "yb1_op"), (1, "yb2", "wo", "yb2_op")):
                ln = body_len(name)
                act.wait_ge(step(op), past(op) + 9)
                if name == "yc":
                    for z in range(2):
                        act.wait_ge(S(f"acc_store{z}"), 16 * 5)
                with act.Fori(0, phases[name][0]) as i:
                    for t in range(ln):
                        k = i * ln + t
                        gate_row, acc_row = sum_rows(name, t)
                        if name == "ya":
                            act.wait_ge(step("yc_op"), past("yc_op") + k + 1)
                            act.dma_start(cols(wide, wcol(2), T), chunk(v_d, k + 1)).then_inc(step("yc_in"), 16)
                        elif name in ("yc", "yb1"):
                            half = 0 if name == "yc" else 1
                            act.wait_ge(step(f"{nxt}_op"), past(f"{nxt}_op") + k + 1)
                            act.dma_start(cols(wide, wcol(2), T), chunk(ys_d, k + 8 * half)).then_inc(step(f"{nxt}_in"), 16)
                            if t == 0:
                                act.dma_start(cols(wide, wcol(1), T), chunk(rg_d, i + 2 * half + 1)).then_inc(step(f"{nxt}_rg"), 16)
                        if name == "yb2":
                            act.wait_ge(step("wo_op"), past("wo_op") + k)
                        n_store = i * (16 * ln // 2) + 16 * (t // 2 + done // 2 + 1)
                        act.wait_ge(S(f"acc_store{t % 2}"), 16 * 13 if name == "yb2" else n_store)
                        act.dma_start(gate_row, chunk(gate_d, k + 8 * b)).then_inc(S(f"gate_in{t % 2}"), 16)
                        if name != "ya":
                            act.dma_start(acc_row, chunk(acc_d, k)).then_inc(S(f"acc_in{t % 2}"), 16)
                        act.wait_ge(S(f"gate_in{t % 2}"), i * (8 * ln) + 16 * (t // 2 + done // 2 + 1))
                        act.activation(gate_row, gate_row, ACT.Sigmoid).then_inc(S("gate_sig"), 1)
                        if name == "ya":
                            act.wait_ge(step("yc_norm"), past("yc_norm") + k + 1)
                            act.activation(cols(wide, wcol(2), T), cols(wide, wcol(2), T), ACT.Silu,
                                           scale=t_sc[:, ds(k * 32 + TB_LNG, 1)],
                                           bias=t_sc[:, ds(k * 32 + TB_LNB, 1)]).then_inc(S("yc_silu"), 1)
                            act.wait_ge(S("yc_silu"), k + 1)
                            act.activation(cols(n_hi, k * T, T), cols(wide, wcol(2), T), ACT.Copy).then_inc(step("yc_hi"), 1)
                        elif name in ("yc", "yb1"):
                            act.wait_ge(step(f"{nxt}_norm"), past(f"{nxt}_norm") + k + 1)
                            hi = m_hi if name == "yc" else n_hi
                            act.activation(cols(hi, k * T, T), cols(wide, wcol(2), T), ACT.Copy).then_inc(step(f"{nxt}_hi"), 1)
                        split_after(name, t, i)
                        act.wait_ge(S("acc_done"), k + done + 1)
                        if name == "yb2":
                            act.activation(cols(m_hi, k * T, T), acc_row, ACT.Copy).then_inc(step("wo_hi"), 1)
                        else:
                            store(f"acc_store{t % 2}", chunk(acc_d, k), gate_row if name == "ya" else acc_row)
                done += 8
            act.wait_ge(step("wo_op"), past("wo_op") + 9)

            n_res = [0]

            def residual(name, src_d, squares=None):
                with act.Fori(0, 4) as i:
                    for t in range(2):
                        k = i * 2 + t
                        act.wait_ge(S(f"h_store{t}"), i * 16 + 16 * (n_res[0] // 2 + 1))
                        act.dma_start(rows[t][:, :], chunk(src_d, k)).then_inc(S(f"res_in{t}"), 16)
                        split_after(name, t, i)
                        act.wait_ge(S("res_done"), k + n_res[0] + 1)
                        store(f"h_store{t}", chunk(h_d, k), rows[t][:, :])
                        if squares is not None:
                            act.wait_ge(S("sq_sum"), k + squares + 1)
                            act.activation(wide[:, wcol(1):wcol(1) + T], rows[t][:, :], ACT.Square).then_inc(S("sq_done"), 1)
                n_res[0] += 8

            def norm(n_before):
                for half in range(2):
                    for t in range(2):
                        act.wait_ge(S(f"h_store{t}"), 16 * (n_res[0] // 2 - 1 + 2 * half))
                    src = h_d[half * 4 * P:(half + 1) * 4 * P, :].rearrange("(k p) n -> p k n", p=P)
                    act.dma_start(h_fin[:, half * 4 * T:(half + 1) * 4 * T].rearrange("p (k n) -> p k n", k=4), src)\
                        .then_inc(S(f"np_in{half}"), 16)
                stat(wrow(0), 7 + n_before // KD)
                for k in range(1, KD):
                    norm_hi(n_before + k - 1)
                norm_hi(n_before + KD - 1)

            def norm_hi(m):
                k = m % KD
                act.wait_ge(S("np_scaled"), m + 1)
                act.activation(n_hi[:, k * T:(k + 1) * T], cols(wide, wcol(2 + k % 2), T), ACT.Copy).then_inc(S("np_hi"), 1)

            residual("wo", xt_d, 0)
            norm(0)

            f0 = 0
            for p, n in enumerate(FF_PARTS):
                with act.Fori(0, n) as i:
                    for t in range(2):
                        if t == 1:
                            act.wait_ge(S("ff_conv"), i * 2 + 2 * f0 + 3)
                            act.activation(cols(wide, wcol(2), T), cols(wide, wcol(2), T), ACT.Silu).then_inc(S("ff_silu"), 1)
                        split_after(f"up{p}", t, i)
                        act.wait_ge(S("ff_state"), i * 2 + 2 * f0 + t + 1)
                        for src, dst in pieces(slot(f"up{p}", t), wide, wcol(t), PAD):
                            act.activation(dst, src, ACT.Copy)
                        act.wait_ge(S("ff_op"), i + f0 + 1)
                        c0 = (f0 + t * FK) * 32
                        act.activation(tile3(wide[:, wcol(2 + t):wcol(2 + t) + T]), pset(slot(f"up{p}", t)), ACT.Identity,
                                       scale=t_ff[:, ds(i * 32 + c0 + TF_TAPS + 2, 1)],
                                       bias=t_ff[:, ds(i * 32 + c0 + TF_BIAS, 1)]).then_inc(free(f"up{p}", t), 1)
                    act.wait_ge(S("ff_prod"), i + f0 + 1)
                    act.activation(cols(m_hi, i * T, T), cols(wide, wcol(2), T), ACT.Copy).then_inc(S("ff_hi"), 1)
                f0 += n
                if p == 2:
                    for c, src in enumerate(P_TOKENS):
                        act.dma_start(p_tok[:, c * PLE:(c + 1) * PLE], src).then_inc(S("p_in"), 16)
                residual(f"dn{p}", h_d, 9 if p == 2 else None)

            act.dma_start(gf_row[:, :], A["g_final"].rearrange("(a n) -> a n", a=1).to_broadcast([P, D]))\
                .then_inc(step("gf_in"), 16)
            for c in range(9):
                act.wait_ge(S("p_ps"), c + 1)
                act.activation(p_hi[:, :].rearrange("p (k n) -> p k n", k=2)[:, :, c * P:(c + 1) * P],
                               PS[:, 6 + c % 2, 0:2 * P].rearrange("p (k n) -> p k n", k=2), ACT.Copy).then_inc(S("p_hi_done"), 1)

            norm(8)

            def ple(i, last):
                act.wait_ge(S("fin_done"), i + 1)
                if last:
                    wait_tile(act, i * 2 + first("ple"))
                else:
                    split_after("ple", 0, i)
                act.activation(tile3(row1[:, :]), pset(slot("ple", 0)), ACT.Sigmoid).then_inc(free("ple", 0), 1)
                if not last:
                    split_after("ple", 1, i)

            with act.Fori(0, 7) as i:
                ple(i, False)
            ple(7, True)

            def y_store(c):
                act.wait_ge(S("y_scaled"), c + 1)
                dst = O["y_prompt"][0][c * P:(c + 1) * P, :] if c < 8 else O["y_sample"].rearrange("s t d -> (s t) d")
                act.dma_start(dst, y_tok[c % 4][:, :]).then_inc(S(f"out_y{c % 4}"), 16)

            for c in range(9):
                act.wait_ge(S("fin_ps"), c + 1)
                act.activation(y_junk[:, :], flat(2 * (c % 4), 2), ACT.Square, accum_out=y_ms[:, c:c + 1]).then_inc(S("y_ms"), 1)
                act.wait_ge(S("y_ms"), c + 1)
                act.activation(y_ms[:, 9 + c:10 + c], y_ms[:, c:c + 1], ACT.Sqrt, bias=eps[:, 0:1], scale=1.0 / D)\
                    .then_inc(S("y_rms"), 1)
                if c:
                    y_store(c - 1)
            y_store(8)
            for b in range(4):
                act.wait_ge(S(f"out_y{b}"), 16 * (3 if b == 0 else 2))

        @block.gpsimd
        def _(pool):
            own = Done(pool, S("pool_own"))
            pool.sem_inc(w_lo_done, 2)
            for name in ("xbc_state", "sc_state", "ff_state"):
                pool.sem_inc(S(name), 2)
            pool.sem_inc(S("cf_summed"), 1)

            def lo_next(name, t, i):
                _, _, body, qb = phases[name]
                k = qb + t + 1
                pool.wait_ge(w_hi_done, i * len(body) + k + 1)
                s = k % 2
                pool.tensor_tensor(w_lo[s][:, :], w_raw[s][:, :], w_hi[s][:, :].bitcast(F32), ALU.subtract)\
                    .then_inc(w_lo_done, 1)

            def at_register():
                pool.sem_inc(S("pool_waits"), 1)

            pool.memset(cf_stage[:, :], 0.0).then_inc(step("stage_zero"), 1)
            pool.memset(wide[:, 0:2688], 0.0).then_inc(step("stage_zero"), 1)
            pool.memset(eps[:, :], EPS).then_inc(step("eps_done"), 1)
            own.do(pool.memset(ident[:, :], 0.0))
            pool.affine_select(out=ident[:, :], in_=ident[:, :], compare_op=ALU.not_equal, fill=1.0, base=0,
                               pattern=[[-1, P]], channel_multiplier=1).then_inc(step("ident_done"), 1)
            pool.memset(ones[:, :], 1.0 / D).then_inc(step("ones_done"), 1)
            pool.wait_ge(w_hi_done, 1)
            pool.tensor_tensor(w_lo[0][:, :], w_raw[0][:, :], w_hi[0][:, :].bitcast(F32), ALU.subtract).then_inc(w_lo_done, 1)

            pool.wait_ge(S("n_ready"), 9)
            for b in range(2):
                pool.wait_ge(S(f"xt_store{b}"), 16 * (5 - b))
            pool.memset(v_in[:, :].rearrange("p (j n) -> p j n", j=KD)[:, :, 0:CPAD], 0.0).then_inc(step("v_pads"), 1)
            pool.memset(v_sum[:, :], 0.0).then_inc(step("vs_zero"), 1)
            pool.wait_ge(step("cf_state"), past("cf_state") + 1)
            with own.loop(8, 3) as i:
                for t in range(2):
                    lo_next("cf", t, i)
                old = cols(s_cf, i * 256, 256).rearrange("p (s n) -> p s n", s=NS)[:, :, 0:CPAD]
                at_register()
                own.do(pool.tensor_copy(seqs(v_in, i * CFW, CPAD, CPAD, CPAD), old))
                pool.wait_ge(ps_free[1], i + 2)
                at_register()
                own.mark(pool.tensor_copy(old, seqs(v_in, i * CFW, CPAD, CPAD - TS, CPAD)))
                own.mark(pool.tensor_copy(cols(s_cfp, i * 32, CPAD), cols(v_in, i * CFW + TP, CPAD)))
            own.wait()
            pool.sem_inc(S("cf_saved"), 1)

            pool.wait_ge(step("tables"), past("tables") + 1)
            pool.wait_ge(step("cf_new"), past("cf_new") + 2)
            pool.memset(v_acc[1][:, :], 0.0).then_inc(step("acc_zero"), 1)
            for m in range(2):
                pool.memset(wide[:, wcol(m):wcol(m) + PAD], 0.0).then_inc(step("pads1"), 1)

            def sum_cf(c, par):
                pool.wait_ge(S("cf_conv"), c + 1)
                pool.wait_ge(step("acc_zero"), past("acc_zero") + 1)
                pool.wait_ge(S("cf_summed"), c + 1)
                pool.tensor_tensor(v_sum[:, :], v_sum[:, :], v_acc[par][:, :], ALU.add).then_inc(S("cf_summed"), 1)

            with own.loop(2, 24) as i:
                for t in range(12):
                    j = i * 12 + t
                    lo_next("xbc", t, i)
                    rows_ = cols(t_xbc, j * 32 + TC_STATE, 24).rearrange("p (s n) -> p s n", s=NS)
                    pool.wait_ge(S("xbc_conv"), j + 1)
                    at_register()
                    own.mark(pool.tensor_copy(seqs(wide, wcol(t % 2), PAD, 3, 3), rows_))
                    own.wait()
                    pool.sem_inc(S("xbc_pads"), 1)
                    wait_freed(pool, "xbc", t, i)
                    at_register()
                    own.mark(pool.tensor_copy(rows_, seqs(wide, wcol(t % 2), PAD, PAD - TS, 3)))
                    pool.tensor_copy(cols(t_xbc, j * 32 + TC_PROMPT, 3), wide[:, wcol(t % 2) + TP:wcol(t % 2) + TP + 3])\
                        .then_inc(S("xbc_state"), 1)
                    if t % 6 == 2:
                        sum_cf(2 * i + t // 6, 1 - t // 6)
            lo_next("dt", 0, 0)

            with own.loop(2, 8) as i:
                for t in range(12):
                    h = t // 3 % 2
                    j = i * 4 + t // 3
                    lo_next("sc", t, i)
                    if t % 3 == 1:
                        rows_ = cols(t_sc, j * 32 + TB_STATE, 16).rearrange("p (s n) -> p s n", s=NS)
                        pool.wait_ge(step("dt_done"), past("dt_done") + 2)
                        pool.wait_ge(S("sc_conv"), j + 1)
                        at_register()
                        own.do(pool.tensor_copy(seqs(wide, wcol(h), PAD, 2, 2), rows_))
                        pool.sem_inc(S("sc_pads"), 1)
                        wait_freed(pool, "sc", t, i)
                        at_register()
                        own.mark(pool.tensor_copy(rows_, seqs(wide, wcol(h), PAD, 2 - TS, 2)))
                        pool.tensor_copy(cols(t_sc, j * 32 + TB_PROMPT, 2), wide[:, wcol(h) + PAD + TP - 2:wcol(h) + PAD + TP])\
                            .then_inc(S("sc_state"), 1)
                    if t % 6 == 2:
                        sum_cf(2 * i + 4 + t // 6, 1 - t // 6)

            for h in range(2):
                pool.wait_ge(S(f"yin_store{h}"), 16 * 5)
            for m in range(2):
                own.do(pool.memset(tri[m][:, :], 1.0))
                own.do(pool.memset(after[m][:, :], 1.0))
                own.do(pool.affine_select(out=tri[m][:, :], in_=tri[m][:, :], compare_op=ALU.is_ge, fill=0.0, base=0,
                                          pattern=[[1, P]], channel_multiplier=-1))
                own.do(pool.affine_select(out=after[m][:, :], in_=after[m][:, :], compare_op=ALU.is_gt, fill=0.0, base=0,
                                          pattern=[[-1, P]], channel_multiplier=1))
                if m:
                    for w in (tri[1], after[1]):
                        own.do(pool.affine_select(out=w[:, :], in_=w[:, :], compare_op=ALU.is_ge, fill=0.0, base=0,
                                                  pattern=[[-TS, NS], [0, TS]], channel_multiplier=1))
                        own.do(pool.affine_select(out=w[:, :], in_=w[:, :], compare_op=ALU.is_ge, fill=0.0, base=TS - 1,
                                                  pattern=[[TS, NS], [0, TS]], channel_multiplier=-1))
                own.do(pool.tensor_scalar(bar[m][:, :], tri[m][:, :], 1.0, 1e30, ALU.subtract, ALU.mult))
            own.do(pool.memset(sel[:, :], 1.0))
            own.do(pool.affine_select(out=sel[:, :], in_=sel[:, :], compare_op=ALU.is_ge, fill=0.0, base=0,
                                      pattern=[[-TS, NS]], channel_multiplier=1))
            own.do(pool.affine_select(out=sel[:, :], in_=sel[:, :], compare_op=ALU.is_ge, fill=0.0, base=TS - 1,
                                      pattern=[[TS, NS]], channel_multiplier=-1))
            pool.sem_inc(step("ssd_consts"), 7)
            sum_cf(8, 1)

            def decay_x(c):
                pool.wait_ge(S("blk_done"), c + 1)
                pool.wait_ge(S("xdt_done"), c + 1)
                pool.wait_ge(S("dec_done"), c + 1)
                pool.tensor_tensor(xdd[:, :].rearrange("p (h n) -> p h n", h=HEADS),
                                   xdt[:, :].rearrange("p (h n) -> p h n", h=HEADS),
                                   dec_col[:, :].unsqueeze(2).to_broadcast([P, HEADS, HD]), ALU.mult).then_inc(S("xdd_done"), 1)

            def decay_c(k, g, par, blk):
                pool.wait_ge(S("e_done"), k + 1)
                pool.wait_ge(S("ea_last_done"), k + 1)
                e = ec[par][:, :].rearrange("p (h n) -> p h n", h=HG)
                c_ = blk[:, (20 + g) * P:(21 + g) * P].unsqueeze(1).to_broadcast([P, HG, P])
                pool.tensor_tensor(e, e, c_, ALU.mult).then_inc(S("ec_done"), 1)

            with pool.Fori(0, 4) as i:
                for b in range(2):
                    c = i * 2 + b
                    decay_x(c)
                    for g in range(GROUPS):
                        decay_c(c * 4 + g, g, g % 2, xbc_blk[b])
                        if g == 1:
                            lo_next("side0", b, i)
            decay_x(8)
            for g in range(GROUPS):
                if g:
                    pool.wait_ge(S("sb_ps"), 4 * g)
                pool.wait_ge(S("btok_done"), 9)
                pool.tensor_tensor(b_msk[:, :].rearrange("p (b n) -> p b n", b=NS),
                                   b_tok[:, g * P:(g + 1) * P].unsqueeze(1).to_broadcast([P, NS, P]),
                                   sel[:, :].unsqueeze(2).to_broadcast([P, NS, P]), ALU.mult).then_inc(S("bmsk_done"), 1)
                decay_c(32 + g, g, 0, xbc_blk[0])
                for t in range(2):
                    lo_next("side1", t, g)

            pool.wait_ge(S("y_done"), 37)
            pool.memset(wide[:, 0:T], 0.0).then_inc(S("grp_sum"), 1)
            with pool.Fori(0, 4) as i:
                for t in range(4):
                    j = i * 4 + t
                    lo_next("z", t, i)
                    pool.wait_ge(S("grp_sq"), j + 1)
                    if t == 0:
                        pool.wait_ge(S("stat_ps"), 3 * i + 3)
                        at_register()
                    dst = wide[:, 0:T]
                    ins = pool.tensor_copy(dst, row1[:, :]) if t == 0 else pool.tensor_tensor(dst, dst, row1[:, :], ALU.add)
                    ins.then_inc(S("grp_sum"), 1)
                    pool.wait_ge(S("grp_sum"), j + 2)
            pool.wait_ge(S("rg_store"), 16 * 6)
            pool.memset(wide[:, wcol(1):wcol(1) + T], 0.0).then_inc(S("var_sum"), 1)
            with pool.Fori(0, 4) as i:
                for t in range(2):
                    k = i * 2 + t
                    lo_next("gate", t, i)
                    pool.wait_ge(S("v_sq"), k + 1)
                    pool.wait_ge(S("var_sum"), k + 1)
                    var = wide[:, wcol(1):wcol(1) + T]
                    pool.tensor_tensor(var, var, wide[:, wcol(2):wcol(2) + T], ALU.add).then_inc(S("var_sum"), 1)
            for name in ("ya", "yc", "yb1", "yb2"):
                with pool.Fori(0, phases[name][0]) as i:
                    for t in range(body_len(name)):
                        lo_next(name, t, i)

            def norm_odd(before):
                for k in range(1, KD, 2):
                    pool.wait_ge(S("np_hi"), before + k + 1)
                    hi = n_hi[:, k * T:(k + 1) * T]
                    pool.tensor_tensor(n_lo[:, k * T:(k + 1) * T], wide[:, wcol(3):wcol(3) + T], hi.bitcast(F32), ALU.subtract)\
                        .then_inc(S("norm_op1"), 1)

            def squares(name, before):
                pool.memset(cols(wide, 0, T), 0.0).then_inc(S("sq_sum"), 1)
                with pool.Fori(0, 4) as i:
                    for t in range(2):
                        lo_next(name, t, i)
                        k = i * 2 + t + before
                        pool.wait_ge(S("sq_done"), i * 2 + t + (before // 9) * 8 + 1)
                        pool.wait_ge(S("sq_sum"), k + 1)
                        pool.tensor_tensor(wide[:, 0:T], wide[:, 0:T], wide[:, wcol(1):wcol(1) + T], ALU.add)\
                            .then_inc(S("sq_sum"), 1)

            pool.wait_ge(step("wo_op"), past("wo_op") + 9)
            squares("wo", 0)
            norm_odd(0)
            pool.wait_ge(S("norm_op0"), 4)
            for m in range(2):
                pool.memset(wide[:, wcol(m):wcol(m) + PAD], 0.0).then_inc(step("pads2"), 1)
            f0 = 0
            for p, n in enumerate(FF_PARTS):
                with own.loop(n, 4) as i:
                    for t in range(2):
                        lo_next(f"up{p}", t, i)
                        m = i * 2 + 2 * f0 + t
                        rows_ = cols(t_ff, i * 32 + (f0 + t * FK) * 32 + TF_STATE, 16).rearrange("p (s n) -> p s n", s=NS)
                        pool.wait_ge(S("ff_conv"), m + 1)
                        at_register()
                        own.do(pool.tensor_copy(seqs(wide, wcol(t), PAD, 2, 2), rows_))
                        pool.sem_inc(S("ff_pads"), 1)
                        wait_freed(pool, f"up{p}", t, i)
                        at_register()
                        own.mark(pool.tensor_copy(rows_, seqs(wide, wcol(t), PAD, 2 - TS, 2)))
                        pool.tensor_copy(cols(t_ff, i * 32 + (f0 + t * FK) * 32 + TF_PROMPT, 2),
                                         wide[:, wcol(t) + PAD + TP - 2:wcol(t) + PAD + TP]).then_inc(S("ff_state"), 1)
                f0 += n
                if p < 2:
                    with pool.Fori(0, 4) as i:
                        for t in range(2):
                            lo_next(f"dn{p}", t, i)
                else:
                    pool.wait_ge(S("ff_op"), FK + 1)
                    squares("dn2", 9)
                    norm_odd(KD)
            with pool.Fori(0, 7) as i:
                for t in range(2):
                    lo_next("ple", t, i)
            lo_next("ple", 0, 7)

        @block.vector
        def _(v):
            own = Done(v, S("dve_own"))
            for name in ("xbc_conv", "sc_conv", "ff_conv", "stat_out"):
                v.sem_inc(S(name), 2)
            for name in ("cf_conv", "op_done", "ff_op", "fin_done", "y_done", "h_done"):
                v.sem_inc(S(name), 1)

            def older_taps(buf, at_, pad, acc, taps, w_col):
                out = []
                for w, shift in taps:
                    scalar = w_col(w)
                    out.append((acc[0], cols(buf, at_ + pad - shift, TP), scalar))
                    out.append((acc[1], seqs(buf, at_, pad, shift), scalar))
                return out

            def add_taps(ops, sem_=None, goes_on=False):
                for n_, (acc, src, scalar) in enumerate(ops):
                    if n_ >= 2 or goes_on:
                        own.wait(but=1)
                    ins = v.scalar_tensor_tensor(out=acc, in0=src, scalar=scalar, in1=acc, op0=ALU.mult, op1=ALU.add)
                    if sem_ is not None and n_ == len(ops) - 1:
                        ins.then_inc(S(sem_), 1)
                    else:
                        own.mark(ins)

            def low(dst, src, hi):
                return v.tensor_tensor(dst, src, hi.bitcast(F32), ALU.subtract)

            v.wait_ge(step("small_in"), past("small_in") + 80)

            def x_normed(c):
                v.wait_ge(S("x_rms"), c + 1)
                own.do(v.reciprocal(x_ms[:, 18 + c:19 + c], x_ms[:, 9 + c:10 + c]))
                x_arrived(v, c)
                if c >= 2:
                    v.wait_ge(S("xnt_done"), c - 1)
                v.scalar_tensor_tensor(out=xn_tok[c % 2][:, :], in0=x_tok[:, c * D:(c + 1) * D], scalar=x_ms[:, 18 + c:19 + c],
                                       in1=g_row[:, :], op0=ALU.mult, op1=ALU.mult).then_inc(S("xn_done"), 1)

            x_normed(0)
            for c in range(9):
                if c + 1 < 9:
                    x_normed(c + 1)
                v.wait_ge(S("nhi_done"), c + 1)
                hi, lo = (x[:, :].rearrange("p (k n) -> p k n", k=KD)[:, :, c * P:(c + 1) * P] for x in (n_hi, n_lo))
                low(lo, flat(4 * (c % 2) + 2, 2).rearrange("p (k n) -> p k n", k=KD), hi).then_inc(S("n_ready"), 1)
            v.wait_ge(S("cf_state_in"), 16 * 32)
            own.mark(v.memset(s_cfp[:, :], 0.0))
            own.do(v.transpose(s_cf[:, :], cf_stage[:, :]))
            v.sem_inc(step("cf_state"), 1)

            v.wait_ge(step("v_pads"), past("v_pads") + 1)
            with v.Fori(0, 8) as i:
                wait_tile(v, 2 * i + 1)
                v.wait_ge(ps_free[0], i + 2)
                gate = [row0[:, 0:2 * BW].rearrange("p (b n) -> p b n", b=2), row0[:, 2 * BW:TP],
                        row0[:, TP:T].rearrange("p (s n) -> p s n", n=TS)]
                for z, ((src, dst), g_) in enumerate(zip(pieces(1, v_in, i * CFW, CPAD), gate)):
                    ins = v.tensor_tensor(dst, src, g_, ALU.mult)
                ins.then_inc(ps_free[1], 1)
            v.wait_ge(S("tables_in"), 16 * 4 * len(TABLES))
            own.mark(v.transpose(t_xbc[:, :], wide[:, stage_xbc:stage_xbc + 768]))
            own.mark(v.transpose(t_cf[:, :], wide[:, stage_cf:stage_cf + 256]))
            own.mark(v.transpose(t_sc[:, :], wide[:, stage_sc:stage_sc + 256]))
            own.do(v.transpose(t_ff[:, :], wide[:, stage_ff:stage_ff + 2 * FK * 32]))
            v.sem_inc(step("tables"), 1)
            v.wait_ge(S("cf_saved"), 1)
            v.transpose(cf_new[:, 0:2048], s_cf[:, :]).then_inc(step("cf_new"), 1)
            v.transpose(cf_new[:, 2048:2304], s_cfp[:, :]).then_inc(step("cf_new"), 1)

            def cf_taps(c, t, par):
                if t == 0:
                    v.wait_ge(S("cf_tap"), c + 1)
                taps = [(CPAD - s_, s_) for s_ in range(5 * t + 1, 5 * t + 6)]
                add_taps(older_taps(v_in, c * CFW, CPAD, (v_acc[par][:, 0:TP], tail(v_acc[par][:, TP:T])), taps,
                                    lambda w: t_cf[:, ds(c * 32 + w, 1)]), "cf_conv" if t == 5 else None, goes_on=t > 0)

            def acc_row(m):
                return wide[:, wcol(m):wcol(m) + TP], tail(wide[:, wcol(m) + TP:wcol(m) + T])

            v.wait_ge(step("pads1"), past("pads1") + 2)
            with own.loop(2, 178) as i:
                for t in range(12):
                    j = i * 12 + t
                    wait_freed(v, "xbc", t, i)
                    v.wait_ge(S("xbc_pads"), j + 1)
                    taps = [(TC_TAPS + 3 - s_, s_) for s_ in range(1, 4)]
                    add_taps(older_taps(wide, wcol(t % 2), PAD, acc_row(2 + t % 2), taps,
                                        lambda w: t_xbc[:, ds(i * 384 + t * 32 + w, 1)]), "xbc_conv")
                    cf_taps(2 * i + t // 6, t % 6, t // 6)

            v.wait_ge(step("dt_exp"), past("dt_exp") + 1)
            h_ = slice(0, HEADS)
            own.mark(v.tensor_scalar(a_neg[h_, :], a_neg[h_, :], -1.0, None, ALU.mult))
            own.do(v.tensor_scalar(row1[h_, :], row0[h_, :], 1.0, None, ALU.add))
            v.sem_inc(step("dt_one_plus"), 1)
            v.wait_ge(S("xbc_state"), 26)
            d_, r_ = (wide[h_, wcol(m) + PAD:wcol(m) + PAD + T] for m in range(2))
            own.do(v.tensor_scalar(d_, row1[h_, :], 1.0, None, ALU.subtract))
            own.do(v.scalar_tensor_tensor(out=r_, in0=d_, scalar=0.0, in1=d_, op0=ALU.is_equal, op1=ALU.add))
            own.do(v.reciprocal(r_, r_))
            own.do(v.tensor_tensor(r_, r_, row0[h_, :], ALU.mult))
            v.wait_ge(step("dt_log"), past("dt_log") + 1)
            own.do(v.scalar_tensor_tensor(out=da_t[h_, :], in0=d_, scalar=0.0, in1=da_t[h_, :],
                                          op0=ALU.is_equal, op1=ALU.add))
            own.do(v.tensor_tensor(da_t[h_, :], da_t[h_, :], r_, ALU.mult))
            v.scalar_tensor_tensor(out=dt_t[h_, :], in0=dt_t[h_, :], scalar=0.0, in1=da_t[h_, :],
                                   op0=ALU.max, op1=ALU.add).then_inc(step("dt_done"), 1)
            v.wait_ge(step("dt_done"), past("dt_done") + 1)
            v.tensor_scalar(da_t[h_, :], dt_t[h_, :], a_neg[h_, 0:1], None, ALU.mult).then_inc(step("dt_done"), 1)

            with own.loop(2, 130) as i:
                for t in range(12):
                    h = t // 3 % 2
                    j = i * 4 + t // 3
                    if t % 3 == 1:
                        wait_tile(v, i * 12 + t + first("sc"))
                        wait_freed(v, "sc", t - 1, i)
                        v.wait_ge(S("sc_state"), j + 1)
                        c_ = [rows[h][:, 0:2 * BW].rearrange("p (b n) -> p b n", b=2), rows[h][:, 2 * BW:TP],
                              rows[h][:, TP:T].rearrange("p (s n) -> p s n", n=TS)]
                        for (src, dst), x in zip(pieces(slot("sc", t), wide, wcol(h), PAD), c_):
                            ins = v.tensor_tensor(dst, src, x, ALU.mult)
                        ins.then_inc(free("sc", t), 1)
                    if t % 3 == 2:
                        v.wait_ge(S("sc_tap"), j + 1)
                        v.wait_ge(S("sc_pads"), j + 1)
                        taps = [(TB_TAPS + 2 - s_, s_) for s_ in range(1, 3)]
                        add_taps(older_taps(wide, wcol(h), PAD, acc_row(2 + h), taps,
                                            lambda w: t_sc[:, ds(i * 128 + t // 3 * 32 + w, 1)]), "sc_conv")
                        wait_tile(v, i * 12 + t + first("sc"))
                        v.wait_ge(S("sc_conv"), j + 3)
                        acc = tile3(wide[:, wcol(2 + h):wcol(2 + h) + T])
                        v.tensor_tensor(acc, acc, pset(slot("sc", t)), ALU.mult).then_inc(free("sc", t), 1)
                    cf_taps(2 * i + 4 + t // 6, t % 6, t // 6)
            v.wait_ge(S("sc_state"), 10)
            own.mark(v.transpose(conv_new[:, 0:768], t_xbc[:, :]))
            own.mark(v.transpose(conv_new[:, 768:1024], t_sc[:, :]))

            v.wait_ge(step("dt_tok_ps"), past("dt_tok_ps") + 1)
            own.mark(v.tensor_copy(dt_tok[:, :], PS[:, 0, 0:9 * HEADS]))
            own.mark(v.tensor_copy(da_tok[:, :], PS[:, 1, 0:9 * HEADS]))
            own.wait()
            v.sem_inc(step("conv_new"), 2)
            v.wait_ge(S("cf_summed"), 10)
            own.wait()
            v.sem_inc(step("ssd_region"), 1)
            v.wait_ge(S("v_store"), 16 * 10)
            own.do(v.memset(h_t[:, :], 0.0))
            v.sem_inc(S("blk_done"), 1)

            def by_head(x, n=HEADS):
                return x.rearrange("p (h n) -> p h n", h=n)

            def ssd_block_head(c):
                v.tensor_copy(da_cur[:, :], da_tok[:, ds(c * HEADS, HEADS)]).then_inc(S("da_cur_done"), 1)
                v.wait_ge(S("acs_ps"), c + 1)
                v.tensor_copy(acs_col[:, :], PS[:, 4, 0:HEADS]).then_inc(S("acs_done"), 1)
                v.wait_ge(S("x_ps"), c + 1)
                v.tensor_tensor(by_head(xdt[:, :]), by_head(flat(0, 4)),
                                dt_tok[:, ds(c * HEADS, HEADS)].unsqueeze(2).to_broadcast([P, HEADS, HD]), ALU.mult)\
                    .then_inc(S("xdt_done"), 1)
                v.wait_ge(S("acs_done"), c + 1)

            def exponents(sample, g, par, b0):
                for r in range(HG):
                    h = g * HG + r
                    ins = v.scalar_tensor_tensor(out=lm[par][:, r * P:(r + 1) * P],
                                                 in0=PS[:, b0 + r // 4, (r % 4) * P:(r % 4 + 1) * P],
                                                 scalar=acs_col[:, h:h + 1], in1=bar[sample][:, :],
                                                 op0=ALU.subtract, op1=ALU.min)
                ins.then_inc(S("diff_done"), 1)

            def scores(k, g, par):
                v.wait_ge(S("l_done"), k + 1)
                m = by_head(lm[par][:, :], HG)
                v.tensor_tensor(m, m, PS[:, 6, g * P:(g + 1) * P].unsqueeze(1).to_broadcast([P, HG, P]), ALU.mult)\
                    .then_inc(S("lm_done"), 1)

            def y_tokens(g, blk, bank):
                for pr in range(4):
                    j = 4 * g + pr
                    ins = v.scalar_tensor_tensor(out=y_out[g % 2][:, pr * P:(pr + 1) * P], in0=blk[:, j * P:(j + 1) * P],
                                                 scalar=d_col[:, j:j + 1], in1=PS[:, bank, pr * P:(pr + 1) * P],
                                                 op0=ALU.mult, op1=ALU.add)
                ins.then_inc(S("y_done"), 1)

            v.wait_ge(step("ssd_consts"), past("ssd_consts") + 7)
            v.wait_ge(step("vs_store"), past("vs_store") + 16)
            v.wait_ge(step("small_in"), past("small_in") + 80)
            with own.loop(4, 8) as i:
                for b in range(2):
                    c = 2 * i + b

                    def front(g):
                        k = c * 4 + g
                        v.wait_ge(S("cum_ps"), k + 1)
                        v.wait_ge(S("y_ps"), k + 1)
                        v.wait_ge(S("e_done"), k + 1)
                        exponents(0, g, g % 2, 2 * (g % 2))
                        v.tensor_copy(ea_last[:, g * HG:(g + 1) * HG].unsqueeze(2), by_head(ec[g % 2][:, :], HG)[:, :, P - 1:P])\
                            .then_inc(S("ea_last_done"), 1)

                    def new_state(g):
                        k = c * 4 + g
                        v.wait_ge(S("ea_last_done"), k + 1)
                        if g == 0:
                            v.wait_ge(S("h_done"), 4 * c + 1)
                        st = h_t[:, g * 512:(g + 1) * 512]
                        own.do(v.tensor_tensor(by_head(st, HG), by_head(st, HG),
                                               ea_last[:, g * HG:(g + 1) * HG].unsqueeze(2).to_broadcast([P, HG, HD]), ALU.mult))
                        v.wait_ge(S("h_ps"), k + 1)
                        v.tensor_tensor(st, st, PS[:, 7, :], ALU.add).then_inc(S("h_done"), 1)

                    ssd_block_head(c)
                    front(0)
                    front(1)
                    v.wait_ge(S("b_ps"), c + 1)
                    scores(c * 4, 0, 0)
                    scores(c * 4 + 1, 1, 1)
                    for g in range(GROUPS):
                        if g == 2:
                            scores(c * 4 + 3, 3, 1)
                        v.wait_ge(S("y_ps"), c * 4 + g + 3)
                        v.wait_ge(S(f"y_store{g % 2}"), 32 * c + 16 * (g // 2 + 1))
                        y_tokens(g, xbc_blk[b], 4)
                        if g == 1:
                            scores(c * 4 + 2, 2, 0)
                        new_state(g)
                        if g + 2 < GROUPS:
                            front(g + 2)
                    v.wait_ge(S("h_done"), 4 * c + 5)
                    v.sem_inc(S("blk_done"), 1)
            v.sem_inc(S("ea_last_done"), 4)
            ssd_block_head(8)
            for g in range(GROUPS):
                v.wait_ge(S("cum_ps"), 33 + g)
                if g:
                    v.wait_ge(S("ys_ps"), 4 * g)
                v.wait_ge(S("e_done"), 33 + g)
                exponents(1, g, 0, 0)
                v.wait_ge(S("b_ps"), 9)
                scores(32 + g, g, 0)
                for pr in range(4):
                    j = 4 * g + pr
                    v.wait_ge(S("sb_ps"), j + 1)
                    v.wait_ge(S(f"s_in_sem{j % 2}"), 16 * (j // 2 + 1))
                    v.wait_ge(step("ea_done"), past("ea_done") + 1)
                    if j >= 2:
                        v.wait_ge(S(f"out_ssm_s{j % 2}"), 16 * (j // 2))
                    for s_ in range(NS):
                        ins = v.scalar_tensor_tensor(out=s_out[j % 2][:, s_ * P:(s_ + 1) * P],
                                                     in0=s_in[j % 2][:, s_ * P:(s_ + 1) * P],
                                                     scalar=ea_seq[:, j * NS + s_:j * NS + s_ + 1],
                                                     in1=PS[:, s_ // 4, (s_ % 4) * P:(s_ % 4 + 1) * P],
                                                     op0=ALU.mult, op1=ALU.add)
                    ins.then_inc(S("sout_done"), 1)
                v.wait_ge(S("ys_ps"), 4 * g + 4)
                v.wait_ge(S(f"y_store{g % 2}"), 16 * (17 + g // 2))
                y_tokens(g, xbc_blk[0], 7)

            def wrow(m):
                return wide[:, wcol(m):wcol(m) + T]

            def inverse(row, n):
                for b in range(NB):
                    v.wait_ge(S("stat_out"), 3 * n + b + 3)
                    o = row[:, b * BW:(b + 1) * BW]
                    ins = v.reciprocal(o, o)
                return ins

            with v.Fori(0, 4) as i:
                for t in range(4):
                    j = i * 4 + t
                    v.wait_ge(S("y_in"), j * 16 + 16)
                    wait_freed(v, "z", t, i)
                    v.tensor_tensor(row0[:, :], row0[:, :], row1[:, :], ALU.mult).then_inc(S("ys_done"), 1)
                    if t == 0:
                        inverse(wrow(1), i).then_inc(step("rstd_done"), 1)
            inverse(wrow(1), 5).then_inc(step("rstd_done"), 1)

            with v.Fori(0, 4) as i:
                for h in range(2):
                    k = i * 2 + h
                    v.wait_ge(S("v_in_sem"), k * 16 + 16)
                    v.tensor_tensor(wrow(2), wrow(2), wrow(3), ALU.subtract).then_inc(S("v_cent"), 1)
                    v.wait_ge(step("ya_hi"), past("ya_hi") + k + 1)
                    low(cols(m_lo, k * T, T), wrow(0), cols(m_hi, k * T, T)).then_inc(step("ya_op"), 1)
            own.do(inverse(wrow(1), 6))

            done = 0
            for name, nxt in (("ya", "yc"), ("yc", "yb1"), ("yb1", "yb2"), ("yb2", "wo")):
                n, _, body, _ = phases[name]
                ln = len(body)
                with own.loop(n, ln if name == "ya" else 0) as i:
                    for t in range(ln):
                        k = i * ln + t
                        if name == "ya":
                            v.wait_ge(step("yc_in"), past("yc_in") + k * 16 + 16)
                            own.do(v.tensor_tensor(wrow(2), wrow(2), wrow(3), ALU.subtract))
                            v.tensor_tensor(wrow(2), wrow(2), wrow(1), ALU.mult).then_inc(step("yc_norm"), 1)
                        elif name != "yb2":
                            half = 0 if name == "yc" else 1
                            v.wait_ge(step(f"{nxt}_in"), past(f"{nxt}_in") + k * 16 + 16)
                            v.wait_ge(step(f"{nxt}_rg"), past(f"{nxt}_rg") + i * 16 + 16)
                            v.scalar_tensor_tensor(out=wrow(2), in0=wrow(2), scalar=t_sc[:, ds(k * 32 + TB_NORM + half, 1)],
                                                   in1=wrow(1), op0=ALU.mult, op1=ALU.mult).then_inc(step(f"{nxt}_norm"), 1)
                        if name != "yb2":
                            hi, lo = (m_hi, m_lo) if name == "yc" else (n_hi, n_lo)
                            v.wait_ge(step(f"{nxt}_hi"), past(f"{nxt}_hi") + k + 1)
                            low(cols(lo, k * T, T), wrow(2), cols(hi, k * T, T)).then_inc(step(f"{nxt}_op"), 1)
                        if name == "ya":
                            gate_row = rows[t % 2][:, :]
                        else:
                            gate_row, acc = (row0[:, :], row1[:, :]) if t % 2 == 0 else (wrow(3), wrow(0))
                        wait_tile(v, k + first(name))
                        v.wait_ge(S("gate_sig"), k + done + 1)
                        v.tensor_tensor(tile3(gate_row), tile3(gate_row), pset(slot(name, t)), ALU.mult)\
                            .then_inc(free(name, t), 1)
                        wait_freed(v, name, t, i)
                        if name == "ya":
                            v.sem_inc(S("acc_done"), 1)
                        else:
                            v.wait_ge(S(f"acc_in{t % 2}"), i * (8 * ln) + 16 * (t // 2 + done // 2 - 3))
                            v.tensor_tensor(acc, gate_row, acc, ALU.add).then_inc(S("acc_done"), 1)
                        if name == "yb2":
                            v.wait_ge(step("wo_hi"), past("wo_hi") + k + 1)
                            low(cols(m_lo, k * T, T), acc, cols(m_hi, k * T, T)).then_inc(step("wo_op"), 1)
                done += 8

            n_res = [0]

            def residual(name):
                with v.Fori(0, 4) as i:
                    for t in range(2):
                        wait_tile(v, i * 2 + t + first(name))
                        v.wait_ge(S(f"res_in{t}"), i * 16 + 16 * (n_res[0] // 2 + 1))
                        v.tensor_tensor(tile3(rows[t][:, :]), tile3(rows[t][:, :]), pset(slot(name, t)), ALU.add)\
                            .then_inc(free(name, t), 1)
                        wait_freed(v, name, t, i)
                        v.sem_inc(S("res_done"), 1)
                n_res[0] += 8

            def norm(before, n_stat, gain):
                own.do(inverse(wrow(0), n_stat))

                def norm_lo(k):
                    v.wait_ge(S("np_hi"), before + k + 1)
                    low(n_lo[:, k * T:(k + 1) * T], wrow(2 + k % 2), n_hi[:, k * T:(k + 1) * T]).then_inc(S("norm_op0"), 1)

                for k in range(KD):
                    if k >= 2:
                        v.wait_ge(S(f"norm_op{k % 2}"), before // 2 + k // 2)
                    v.wait_ge(S(f"np_in{k // 4}"), 16 * (before // KD + 1))
                    v.scalar_tensor_tensor(out=wrow(2 + k % 2), in0=h_fin[:, k * T:(k + 1) * T],
                                           scalar=t_sc[:, k * 32 + gain:k * 32 + gain + 1], in1=wrow(0),
                                           op0=ALU.mult, op1=ALU.mult).then_inc(S("np_scaled"), 1)
                    if k % 2:
                        norm_lo(k - 1)

            residual("wo")
            norm(0, 7, TB_GFFN)

            v.wait_ge(step("pads2"), past("pads2") + 2)
            f0 = 0
            for p, n in enumerate(FF_PARTS):
                with own.loop(n, 6) as i:
                    for t in range(2):
                        m = i * 2 + 2 * f0 + t
                        c0 = (f0 + t * FK) * 32
                        wait_freed(v, f"up{p}", t, i)
                        v.wait_ge(S("ff_pads"), m + 1)
                        taps = [(TF_TAPS + 2 - s_, s_) for s_ in range(1, 3)]
                        add_taps(older_taps(wide, wcol(t), PAD, acc_row(2 + t), taps,
                                            lambda w: t_ff[:, ds(i * 32 + c0 + w, 1)]), "ff_conv")
                    v.wait_ge(S("ff_silu"), i + f0 + 1)
                    v.wait_ge(S("ff_conv"), i * 2 + 2 * f0 + 4)
                    v.tensor_tensor(wrow(2), wrow(2), wrow(3), ALU.mult).then_inc(S("ff_prod"), 1)
                    v.wait_ge(S("ff_hi"), i + f0 + 1)
                    low(cols(m_lo, i * T, T), wrow(2), cols(m_hi, i * T, T)).then_inc(S("ff_op"), 1)
                f0 += n
                if p == 2:
                    v.wait_ge(S("ff_state"), 2 + 2 * FK)
                    v.wait_ge(S("ff_op"), FK + 1)
                    v.transpose(ff_new[:, :], t_ff[:, :]).then_inc(step("ff_new"), 1)
                residual(f"dn{p}")

            for c in range(9):
                v.wait_ge(S("p_hi_done"), c + 1)
                hi, lo = (x[:, :].rearrange("p (k n) -> p k n", k=2)[:, :, c * P:(c + 1) * P] for x in (p_hi, p_lo))
                low(lo, PS[:, 6 + c % 2, 0:2 * P].rearrange("p (k n) -> p k n", k=2), hi).then_inc(S("p_op"), 1)
            v.wait_ge(step("ff_new_out"), past("ff_new_out") + 16 * 8)
            norm(8, 8, TB_GPLE)
            with v.Fori(0, 8) as i:
                wait_tile(v, i * 2 + 1 + first("ple"))
                wait_freed(v, "ple", 0, i)
                v.tensor_tensor(tile3(row1[:, :]), tile3(row1[:, :]), pset(slot("ple", 1)), ALU.mult)\
                    .then_inc(free("ple", 1), 1)
                wait_freed(v, "ple", 1, i)
                v.tensor_tensor(cols(h_fin, i * T, T), cols(h_fin, i * T, T), row1[:, :], ALU.add).then_inc(S("fin_done"), 1)

            v.wait_ge(step("gf_in"), past("gf_in") + 16)
            for c in range(9):
                v.wait_ge(S("y_rms"), c + 1)
                own.do(v.reciprocal(y_ms[:, 18 + c:19 + c], y_ms[:, 9 + c:10 + c]))
                if c >= 4:
                    v.wait_ge(S(f"out_y{c % 4}"), 16 * (c // 4))
                v.scalar_tensor_tensor(out=y_tok[c % 4][:, :], in0=flat(2 * (c % 4), 2), scalar=y_ms[:, 18 + c:19 + c],
                                       in1=gf_row[:, :], op0=ALU.mult, op1=ALU.mult).then_inc(S("y_scaled"), 1)


OUTPUTS = {"y_prompt": (1, TP, D), "y_sample": (NS, TS, D),
           "sc_p": (1, 1, 2, D), "xbc_p": (1, 1, 3, XBC), "ssm_p": (1, 1, HEADS, HD, NST), "cf_p": (1, 1, CPAD, D),
           "ff_p": (1, 1, 2, 2 * FF),
           "sc_s": (1, NS, 2, D), "xbc_s": (1, NS, 3, XBC), "ssm_s": (1, NS, HEADS, HD, NST), "cf_s": (1, NS, CPAD, D),
           "ff_s": (1, NS, 2, 2 * FF)}


def kernel(**inputs):
    import numpy as np
    import concourse.bacc as bacc
    from concourse.bass_utils import run_bass_kernel_spmd

    nc = bacc.Bacc("TRN2", target_bir_lowering=False, num_devices=1)
    arrays, A, O = {}, {}, {}
    for name, x in inputs.items():
        arrays[f"in_{name}"] = np.ascontiguousarray(x)
        A[name] = nc.dram_tensor(f"in_{name}", x.shape, F32, kind="ExternalInput").ap()
    for name, shape in OUTPUTS.items():
        O[name] = nc.dram_tensor(f"out_{name}", shape, F32, kind="ExternalOutput").ap()
    build(nc, A, O)
    r = run_bass_kernel_spmd(nc, [arrays], core_ids=[0])
    return tuple(r.results[0][f"out_{name}"] for name in OUTPUTS)
```
